# Optimizing a Trainium2 kernel written in Bass

```python
import jax
import jax.numpy as jnp
from jax import lax
import numpy as np

D_MODEL = 1024
BATCH = 1
SEQ = 512
DEPTH = 2
DEC_BATCH = 8
DEC_SEQ = 8
PAST_LEN = 1024
PAGE_SIZE = 128

MIX_WIDTH = D_MODEL
HEAD_DIM = 64
NSA_HEADS = 8
NSA_KV_HEADS = 2
NSA_GROUP = NSA_HEADS // NSA_KV_HEADS
NSA_WIDTH = NSA_HEADS * HEAD_DIM
KV_WIDTH = NSA_KV_HEADS * HEAD_DIM
CMP_STRIDE = 16
CMP_BLOCK = 2 * CMP_STRIDE
CMP_HIDDEN = 4 * HEAD_DIM
SLC_BLOCK = 64
SLC_TOP_N = 16
WINDOW = 512
SLC_QBLK = 64
WIN_QBLK = 128
FORCED_SCORE = 1.0e4
N_KV_SLOTS = 4
HG_WIDTH = MIX_WIDTH - NSA_WIDTH
HG_HEADS = 4
HG_DK = HG_WIDTH // HG_HEADS
HG_DV = HG_DK
HG_CHUNK = 32
D_FF = 4 * D_MODEL
ROPE_THETA = 10000.0
EPS = 1e-6
PROJ_SIZES = [NSA_WIDTH] + [KV_WIDTH] * 6 + [3 * NSA_HEADS] + [HG_WIDTH] * 4
IN_WIDTH = sum(PROJ_SIZES)

kernel_name = 'nsa_hgrn2_parallel_hybrid_step'

def rms_norm(x, g):
    xf = x.astype(jnp.float32)
    y = xf * lax.rsqrt(jnp.mean(xf * xf, axis=-1, keepdims=True) + EPS)
    return (y * g.astype(jnp.float32)).astype(x.dtype)

def rope(x, pos):
    half = HEAD_DIM // 2
    inv_freq = ROPE_THETA ** (-jnp.arange(half, dtype=jnp.float32) / half)
    ang = pos.astype(jnp.float32)[:, None] * inv_freq[None, :]
    cos = jnp.cos(ang)[None, :, None, :]
    sin = jnp.sin(ang)[None, :, None, :]
    xf = x.astype(jnp.float32)
    x1, x2 = xf[..., :half], xf[..., half:]
    return jnp.concatenate([x1 * cos - x2 * sin, x2 * cos + x1 * sin], axis=-1).astype(x.dtype)

def masked_softmax(s, mask):
    s = jnp.where(mask, s.astype(jnp.float32), -jnp.inf)
    m = jnp.max(s, axis=-1, keepdims=True)
    m = jnp.where(jnp.isfinite(m), m, 0.0)
    e = jnp.exp(s - m)
    return e / jnp.maximum(jnp.sum(e, axis=-1, keepdims=True), 1e-30)

def split_proj(p):
    cuts = [int(c) for c in np.cumsum(PROJ_SIZES)[:-1]]
    return jnp.split(p, cuts, axis=-1)

def compress(rows, pos_emb, w1, b1, w2):
    B, L, hk, d = rows.shape
    ch = rows.reshape(B, L // CMP_STRIDE, CMP_STRIDE, hk, d)
    blk = jnp.concatenate([ch[:, :-1], ch[:, 1:]], axis=2) + pos_emb[None, None, :, None, :]
    flat = jnp.moveaxis(blk, 2, 3).reshape(B, -1, hk, CMP_BLOCK * d)
    return jax.nn.gelu(flat @ w1 + b1) @ w2

def window_band(qg, k, v):
    B, T = qg.shape[:2]
    nb = T // WIN_QBLK
    nsh = WINDOW // WIN_QBLK
    def band(a):
        ap = jnp.pad(a, ((0, 0), (WINDOW, 0), (0, 0), (0, 0)))
        ap = ap.reshape(B, nb + nsh, WIN_QBLK, NSA_KV_HEADS, HEAD_DIM)
        return jnp.concatenate([ap[:, j:j + nb] for j in range(nsh + 1)], axis=2)
    kb, vb = band(k), band(v)
    qb = qg.reshape(B, nb, WIN_QBLK, NSA_KV_HEADS, NSA_GROUP, HEAD_DIM)
    q_pos = jnp.arange(T).reshape(nb, WIN_QBLK)
    k_pos = (jnp.arange(nb) * WIN_QBLK - WINDOW)[:, None] + jnp.arange((nsh + 1) * WIN_QBLK)[None, :]
    diff = q_pos[:, :, None] - k_pos[:, None, :]
    mask = (diff >= 0) & (diff < WINDOW) & (k_pos[:, None, :] >= 0)
    s = jnp.einsum('bcqgnd,bcsgd->bcqgns', qb, kb) * (HEAD_DIM ** -0.5)
    p = masked_softmax(s, mask[None, :, :, None, None, :])
    o = jnp.einsum('bcqgns,bcsgd->bcqgnd', p.astype(vb.dtype), vb)
    return o.reshape(B, T, NSA_KV_HEADS, NSA_GROUP, HEAD_DIM)

def window_dense(qg, q_pos, k, v, k_pos):
    s = jnp.einsum('btgnd,bsgd->btgns', qg, k) * (HEAD_DIM ** -0.5)
    diff = q_pos[:, None] - k_pos[None, :]
    mask = (diff >= 0) & (diff < WINDOW)
    p = masked_softmax(s, mask[None, :, None, None, :])
    return jnp.einsum('btgns,bsgd->btgnd', p.astype(v.dtype), v)

def nsa_attention(q, q_rot, q_pos, gates, kv_all, win_k, win_v, win_pos,
                  kn_cmp, cmp_pos, cmp_w1, cmp_b1, cmp_w2):
    B, Tq = q.shape[:2]
    L = kv_all.shape[1]
    Lp = -(-L // SLC_BLOCK) * SLC_BLOCK
    kv_all = jnp.pad(kv_all, ((0, 0), (0, Lp - L), (0, 0), (0, 0), (0, 0)))
    k_cmp, v_cmp, k_slc, v_slc = kv_all[:, :, 0], kv_all[:, :, 1], kv_all[:, :, 2], kv_all[:, :, 3]
    scale = HEAD_DIM ** -0.5
    qg = q.reshape(B, Tq, NSA_KV_HEADS, NSA_GROUP, HEAD_DIM)
    qrg = q_rot.reshape(B, Tq, NSA_KV_HEADS, NSA_GROUP, HEAD_DIM)

    kc = rms_norm(compress(k_cmp, cmp_pos[0], cmp_w1[0], cmp_b1[0], cmp_w2[0]), kn_cmp)
    vc = compress(v_cmp, cmp_pos[1], cmp_w1[1], cmp_b1[1], cmp_w2[1])
    n_cmp = kc.shape[1]
    c_end = jnp.arange(n_cmp) * CMP_STRIDE + CMP_BLOCK - 1
    c_mask = c_end[None, :] <= q_pos[:, None]
    s = jnp.einsum('btgnd,bcgd->btgnc', qg, kc) * scale
    p_cmp = masked_softmax(s, c_mask[None, :, None, None, :])
    o_cmp = jnp.einsum('btgnc,bcgd->btgnd', p_cmp.astype(vc.dtype), vc)

    n_sel = Lp // SLC_BLOCK
    imp = jnp.pad(jnp.sum(p_cmp, axis=3), ((0, 0), (0, 0), (0, 0), (0, 1)))
    imp = jnp.sum(imp.reshape(B, Tq, NSA_KV_HEADS, n_sel, SLC_BLOCK // CMP_STRIDE), axis=-1)
    blk = jnp.arange(n_sel)[None, :]
    cur = (q_pos // SLC_BLOCK)[:, None]
    forced = (blk == 0) | (blk == cur) | (blk == cur - 1)
    visible = blk * SLC_BLOCK <= q_pos[:, None]
    imp = jnp.where(forced[None, :, None, :], FORCED_SCORE, imp)
    imp = jnp.where(visible[None, :, None, :], imp, -jnp.inf)
    n_top = min(SLC_TOP_N, n_sel)
    _, sel = lax.top_k(imp, n_top)

    kb = k_slc.reshape(B, n_sel, SLC_BLOCK, NSA_KV_HEADS, HEAD_DIM).transpose(0, 3, 1, 2, 4)
    vb = v_slc.reshape(B, n_sel, SLC_BLOCK, NSA_KV_HEADS, HEAD_DIM).transpose(0, 3, 1, 2, 4)
    qbs = SLC_QBLK if Tq % SLC_QBLK == 0 else Tq
    nqb = Tq // qbs
    gather = jax.vmap(jax.vmap(lambda a, i: a[i]))

    def slc_block(args):
        qb, ib, pb = args
        ii = ib.transpose(0, 2, 1, 3).reshape(B, NSA_KV_HEADS, qbs * n_top)
        kg = gather(kb, ii).reshape(B, NSA_KV_HEADS, qbs, n_top * SLC_BLOCK, HEAD_DIM)
        vg = gather(vb, ii).reshape(B, NSA_KV_HEADS, qbs, n_top * SLC_BLOCK, HEAD_DIM)
        kpos = (ii[..., None] * SLC_BLOCK + jnp.arange(SLC_BLOCK)).reshape(B, NSA_KV_HEADS, qbs, -1)
        mask = (kpos <= pb[None, None, :, None]).transpose(0, 2, 1, 3)[:, :, :, None, :]
        sc = jnp.einsum('bqgnd,bgqsd->bqgns', qb, kg) * scale
        pr = masked_softmax(sc, mask)
        return jnp.einsum('bqgns,bgqsd->bqgnd', pr.astype(vg.dtype), vg)

    def to_blocks(a):
        return jnp.moveaxis(a.reshape(B, nqb, qbs, *a.shape[2:]), 1, 0)

    o_slc = lax.map(slc_block, (to_blocks(qrg), to_blocks(sel), q_pos.reshape(nqb, qbs)))
    o_slc = jnp.moveaxis(o_slc, 0, 1).reshape(B, Tq, NSA_KV_HEADS, NSA_GROUP, HEAD_DIM)

    if win_pos is None:
        o_win = window_band(qrg, win_k, win_v)
    else:
        o_win = window_dense(qrg, q_pos, win_k, win_v, win_pos)

    shp = (B, Tq, NSA_HEADS, HEAD_DIM)
    o = (o_cmp.reshape(shp) * gates[..., 0:1] + o_slc.reshape(shp) * gates[..., 1:2]
         + o_win.reshape(shp) * gates[..., 2:3])
    return o.reshape(B, Tq, NSA_WIDTH)

def hgrn2(q, f_pre, i, g, lb, s0, out_gain):
    B, T, _ = q.shape
    C = HG_CHUNK if T % HG_CHUNK == 0 else T
    nc = T // C
    def heads(a):
        return a.reshape(B, nc, C, HG_HEADS, HG_DK).transpose(0, 1, 3, 2, 4)
    z = f_pre.astype(jnp.float32)
    lbf = lb.astype(jnp.float32)
    log_f = jnp.logaddexp(jnp.log(lbf), jnp.log1p(-lbf) + jax.nn.log_sigmoid(z))
    key = (1.0 - lbf) * jax.nn.sigmoid(-z)
    qh = heads(jax.nn.silu(q.astype(jnp.float32)))
    kh = heads(key)
    vh = heads(i.astype(jnp.float32))
    b = jnp.cumsum(heads(log_f), axis=3)
    qe = qh * jnp.exp(b)
    ke = kh * jnp.exp(-b)
    causal = jnp.tril(jnp.ones((C, C), dtype=bool))
    a = jnp.where(causal, jnp.einsum('bnhcd,bnhsd->bnhcs', qe, ke), 0.0)
    o_intra = jnp.einsum('bnhcs,bnhse->bnhce', a, vh)
    b_last = b[:, :, :, -1:, :]
    kd = kh * jnp.exp(b_last - b)
    decay = jnp.exp(b_last[:, :, :, 0, :])

    def step(S, inp):
        qe_n, kd_n, v_n, dec_n = inp
        o_n = jnp.einsum('bhcd,bhde->bhce', qe_n, S)
        S = dec_n[..., None] * S + jnp.einsum('bhcd,bhce->bhde', kd_n, v_n)
        return S, o_n

    s_fin, o_inter = lax.scan(step, s0.astype(jnp.float32),
                              (jnp.moveaxis(qe, 1, 0), jnp.moveaxis(kd, 1, 0),
                               jnp.moveaxis(vh, 1, 0), jnp.moveaxis(decay, 1, 0)))
    o = o_intra + jnp.moveaxis(o_inter, 0, 1)
    o = o.transpose(0, 1, 3, 2, 4).reshape(B, T, HG_HEADS, HG_DV)
    o = rms_norm(o, out_gain) * jax.nn.sigmoid(g.astype(jnp.float32)).reshape(B, T, HG_HEADS, HG_DV)
    return o.reshape(B, T, HG_WIDTH).astype(q.dtype), s_fin

def run_trunk(x, pos, nsa_cache, page_table, win_cache, hg_state,
              attn_norm_g, w_in, q_norm_g, k_norm_g, cmp_pos, cmp_w1, cmp_b1, cmp_w2,
              hg_lb_param, hg_norm_g, w_out, mlp_norm_g, w_up, w_down):
    prompt = nsa_cache is None
    B, T, _ = x.shape
    lb_all = jnp.cumsum(jax.nn.softmax(hg_lb_param.astype(jnp.float32), axis=0), axis=0)
    lb_all = lb_all - lb_all[0]

    def kv_heads(a):
        return a.reshape(B, T, NSA_KV_HEADS, HEAD_DIM)

    out_nsa, out_win, out_hg = [], [], []
    for l in range(DEPTH):
        h = rms_norm(x, attn_norm_g[l])
        (q, k_cmp, v_cmp, k_slc, v_slc, k_win, v_win, gate_pre,
         hq, hf, hi, hg) = split_proj(h @ w_in[l])
        q = rms_norm(q.reshape(B, T, NSA_HEADS, HEAD_DIM), q_norm_g[l])
        q_rot = rope(q, pos)
        k_slc = rope(rms_norm(kv_heads(k_slc), k_norm_g[l, 1]), pos)
        k_win = rope(rms_norm(kv_heads(k_win), k_norm_g[l, 2]), pos)
        v_win = kv_heads(v_win)
        nsa_rows = jnp.stack([kv_heads(k_cmp), kv_heads(v_cmp), k_slc, kv_heads(v_slc)], axis=2)
        win_rows = jnp.stack([k_win, v_win], axis=2)
        gates = jax.nn.sigmoid(gate_pre).reshape(B, T, NSA_HEADS, 3)
        if prompt:
            kv_all = nsa_rows
            wk, wv, wpos = k_win, v_win, None
            s0 = jnp.zeros((B, HG_HEADS, HG_DK, HG_DV), jnp.float32)
        else:
            past = nsa_cache[l, page_table].reshape(B, -1, N_KV_SLOTS, NSA_KV_HEADS, HEAD_DIM)
            kv_all = jnp.concatenate([past, nsa_rows], axis=1)
            buf = win_cache[l]
            n_buf = buf.shape[1]
            wk = jnp.concatenate([buf[:, :, 0], k_win], axis=1)
            wv = jnp.concatenate([buf[:, :, 1], v_win], axis=1)
            wpos = jnp.concatenate([pos[0] - n_buf + jnp.arange(n_buf, dtype=pos.dtype), pos])
            s0 = hg_state[l]
        o_nsa = nsa_attention(q, q_rot, pos, gates, kv_all, wk, wv, wpos, k_norm_g[l, 0],
                              cmp_pos[l], cmp_w1[l], cmp_b1[l], cmp_w2[l])
        o_hg, s_fin = hgrn2(hq, hf, hi, hg, lb_all[l], s0, hg_norm_g[l])
        x = x + jnp.concatenate([o_nsa, o_hg], axis=-1) @ w_out[l]
        h2 = rms_norm(x, mlp_norm_g[l])
        x = x + jnp.square(jax.nn.relu(h2 @ w_up[l])) @ w_down[l]
        out_nsa.append(nsa_rows)
        out_win.append(win_rows[:, T - min(WINDOW, T):] if prompt else win_rows)
        out_hg.append(s_fin)
    return x, jnp.stack(out_nsa), jnp.stack(out_win), jnp.stack(out_hg)

def setup_inputs(seed: int = 0) -> dict:
    key = jax.random.key(seed)
    ks = jax.random.split(key, 24)
    n_pages = PAST_LEN // PAGE_SIZE
    n_used = DEC_BATCH * n_pages
    n_pool = n_used + n_used // 4
    win_buf = min(WINDOW, PAST_LEN)

    def nrm(k, shape, scale):
        return scale * jax.random.normal(k, shape, jnp.float32)

    def gain(k, shape):
        return 1.0 + nrm(k, shape, 0.02)

    page_table = jax.random.permutation(ks[5], n_pool)[:n_used].reshape(DEC_BATCH, n_pages).astype(jnp.int32)
    return {
        'x_prompt': nrm(ks[0], (BATCH, SEQ, D_MODEL), 1.0),
        'x_sample': nrm(ks[1], (DEC_BATCH, DEC_SEQ, D_MODEL), 1.0),
        'cache_nsa_kv': nrm(ks[2], (DEPTH, n_pool, PAGE_SIZE, N_KV_SLOTS, NSA_KV_HEADS, HEAD_DIM), 1.0),
        'cache_win_kv': nrm(ks[3], (DEPTH, DEC_BATCH, win_buf, 2, NSA_KV_HEADS, HEAD_DIM), 1.0),
        'state_hgrn': nrm(ks[4], (DEPTH, DEC_BATCH, HG_HEADS, HG_DK, HG_DV), 0.5),
        'page_table': page_table,
        'attn_norm_g': gain(ks[6], (DEPTH, D_MODEL)),
        'w_in': nrm(ks[7], (DEPTH, D_MODEL, IN_WIDTH), D_MODEL ** -0.5),
        'q_norm_g': gain(ks[8], (DEPTH, HEAD_DIM)),
        'k_norm_g': gain(ks[9], (DEPTH, 3, HEAD_DIM)),
        'cmp_pos': nrm(ks[10], (DEPTH, 2, CMP_BLOCK, HEAD_DIM), 0.1),
        'cmp_w1': nrm(ks[11], (DEPTH, 2, CMP_BLOCK * HEAD_DIM, CMP_HIDDEN), (CMP_BLOCK * HEAD_DIM) ** -0.5),
        'cmp_b1': nrm(ks[12], (DEPTH, 2, CMP_HIDDEN), 0.01),
        'cmp_w2': nrm(ks[13], (DEPTH, 2, CMP_HIDDEN, HEAD_DIM), CMP_HIDDEN ** -0.5),
        'hg_lb_param': nrm(ks[14], (DEPTH, HG_WIDTH), 0.1),
        'hg_norm_g': gain(ks[15], (DEPTH, HG_DV)),
        'w_out': nrm(ks[16], (DEPTH, MIX_WIDTH, D_MODEL), MIX_WIDTH ** -0.5),
        'mlp_norm_g': gain(ks[17], (DEPTH, D_MODEL)),
        'w_up': nrm(ks[18], (DEPTH, D_MODEL, D_FF), D_MODEL ** -0.5),
        'w_down': nrm(ks[19], (DEPTH, D_FF, D_MODEL), D_FF ** -0.5),
    }

def reference(x_prompt, x_sample, cache_nsa_kv, cache_win_kv, state_hgrn, page_table,
              attn_norm_g, w_in, q_norm_g, k_norm_g, cmp_pos, cmp_w1, cmp_b1, cmp_w2,
              hg_lb_param, hg_norm_g, w_out, mlp_norm_g, w_up, w_down):
    past_len = page_table.shape[1] * cache_nsa_kv.shape[2]
    pos_prompt = jnp.arange(x_prompt.shape[1], dtype=jnp.int32)
    pos_sample = past_len + jnp.arange(x_sample.shape[1], dtype=jnp.int32)
    y_prompt, p_nsa, p_win, p_hg = run_trunk(
        x_prompt, pos_prompt, None, None, None, None,
        attn_norm_g, w_in, q_norm_g, k_norm_g, cmp_pos, cmp_w1, cmp_b1, cmp_w2,
        hg_lb_param, hg_norm_g, w_out, mlp_norm_g, w_up, w_down)
    y_sample, s_nsa, s_win, s_hg = run_trunk(
        x_sample, pos_sample, cache_nsa_kv, page_table, cache_win_kv, state_hgrn,
        attn_norm_g, w_in, q_norm_g, k_norm_g, cmp_pos, cmp_w1, cmp_b1, cmp_w2,
        hg_lb_param, hg_norm_g, w_out, mlp_norm_g, w_up, w_down)
    return (y_prompt, y_sample, p_nsa, p_win, p_hg, s_nsa, s_win, s_hg)


_drawn_inputs = setup_inputs


def setup_inputs(seed=0):
    import zlib

    import numpy as np

    out = dict(_drawn_inputs(seed))
    spreads = {}
    factors = {'q_norm_g': 8.0, 'k_norm_g': 3.837, 'cmp_b1': 8.0, 'hg_norm_g': 6.23, 'mlp_norm_g': 3.662}
    for name, (base, spread) in spreads.items():
        noise = np.random.default_rng([zlib.crc32(name.encode()), seed]).standard_normal(out[name].shape)
        drawn = base * np.exp(spread * noise) if base else spread * noise
        out[name] = jnp.asarray(drawn.astype(out[name].dtype))
    for name, factor in factors.items():
        out[name] = (out[name] * factor).astype(out[name].dtype)
    return out
```

```python
from contextlib import ExitStack

import numpy as np

import concourse.bass as bass
from concourse import mybir

F32 = mybir.dt.float32
I32 = mybir.dt.int32
U32 = mybir.dt.uint32
ALU = mybir.AluOpType
ACT = mybir.ActivationFunctionType
AX = mybir.AxisListType.X

P = 128
DM = 1024
KC = DM // P
SEQ = 512
NB = 8
DT = 8
NS = NB * DT
N = SEQ + NS
HALF = N // 2
NT = SEQ // P
TT = NT + 1
DEPTH = 2
HD = 64
NH = 8
NKV = 2
NG = NH // NKV
PAST = 1024
PAGE = 128
NPG = PAST // PAGE
HH = 4
CH = 32
NCK = P // CH
WINB = 512
DFF = 4096
FFC = DFF // P
CST = 16
CHID = 256
NCP = SEQ // CST
NCS = PAST // CST
NCC = NB * NCS
NCALL = NCC + NCP
SLOT = 4096
EPS = 1e-6
NEG = -1e30
C_Q, C_KV, C_WIN, C_HQ, C_HF, C_HI, C_HG, C_END = 0, 512, 1024, 1304, 1816, 2328, 2840, 3352
WINW = C_HQ - C_WIN

CONST_W = {}


def _constants():
    cols = []

    def put(name, a):
        a = np.asarray(a, np.float32).reshape(a.shape[0], -1)
        full = np.zeros((P, a.shape[1]), np.float32)
        full[:a.shape[0]] = a
        CONST_W[name] = (sum(c.shape[1] for c in cols), a.shape[1])
        cols.append(full)

    i = np.arange(P)
    put("ident", np.eye(P))
    put("ones", np.ones((P, P)))
    put("ones64", (i[:, None] // HD == i[None] // HD))
    put("causal", np.where(i[None] > i[:, None], NEG, 0.0))
    put("hgmask", (i[:, None] // CH == i[None] // CH) & (i[:, None] <= i[None]))
    j = np.arange(NS)
    put("hgmask8", (j[:, None] // DT == j[None] // DT) & (j[:, None] <= j[None]))
    pos = np.concatenate([np.arange(SEQ), PAST + np.tile(np.arange(DT), NB), np.zeros(P - NS)]).astype(np.float32)
    inv = (np.float32(10000.0) ** (-np.arange(HD // 2, dtype=np.float32) / np.float32(HD // 2))).astype(np.float32)
    ang = (pos[:, None] * inv[None]).astype(np.float32).reshape(TT, P, HD // 2).transpose(1, 0, 2)
    put("cos", np.cos(ang.astype(np.float64)))
    put("sin", np.sin(ang.astype(np.float64)))
    c = np.arange(NCP)
    q = np.arange(SEQ).reshape(NT, P).T
    seen = (c[None, None] * CST + 2 * CST - 1 <= q[:, :, None]) & (c < NCP - 1)
    put("cmpneg", np.where(seen, 0.0, NEG))
    put("cmp01", seen)
    rows = np.arange(NH * DT)
    t = rows % DT
    same = (np.arange(NB)[None, :, None, None] == np.arange(NB)[None, None, :, None])
    new = same & (np.arange(DT)[None, None, None] <= t[:, None, None, None])
    put("newneg", np.where(new, 0.0, NEG))
    put("winneg", np.where(np.arange(DT)[None] > t[:, None], 0.0, NEG))
    put("groupsum", (rows[:, None] // (NG * DT) == rows[None] // (NG * DT)) & (t[:, None] == t[None]))
    put("blkidx", np.tile(np.arange(16), (P, 1)))
    put("chunk", (i[:, None] // CH == np.arange(NCK)[None]))
    put("batch", (j[:, None] // DT == np.arange(NB)[None]))
    n = np.arange(N)
    put("scan", np.tile(np.where(n < SEQ, n % CH != 0, (n - SEQ) % DT != 0), (P, 1)))
    return np.concatenate(cols, axis=1)


CONSTANTS = _constants()


def rows_of(t):
    return P if t < NT else NS


def build(nc, x_prompt, x_sample, cache_nsa_kv, cache_win_kv, state_hgrn, page_table,
          attn_norm_g, w_in, q_norm_g, k_norm_g, cmp_pos, cmp_w1, cmp_b1, cmp_w2,
          hg_lb_param, hg_norm_g, w_out, mlp_norm_g, w_up, w_down, constants,
          y_prompt, y_sample, p_nsa, p_win, p_hg, s_nsa, s_win, s_hg):
    NPOOL = cache_nsa_kv.shape[1]
    with ExitStack() as ctx:
        def sb(name, cols, dt=F32):
            return ctx.enter_context(nc.sbuf_tensor(name, [P, cols], dt))

        scratch = nc.dram_tensor("branches", [NB, DT, NH, 3 * HD], F32, kind="Internal").ap()
        sems = {}

        def sem(name):
            if name not in sems:
                sems[name] = ctx.enter_context(nc.semaphore(name))
            return sems[name]

        made = {}

        def step(eng, ins, name):
            made[name] = made.get(name, 0) + 1
            ins.then_inc(sem(name), 1)
            eng.wait_ge(sem(name), made[name])

        cst = sb("cst", CONSTANTS.shape[1])
        pages = ctx.enter_context(nc.sbuf_tensor("pages", [1, NB * NPG], I32))
        XT = sb("XT", KC * N)[:, :].rearrange("p (c n) -> p c n", c=KC)
        HT_ = sb("HT", KC * N)
        HT = HT_[:, :].rearrange("p (c n) -> p c n", c=KC)
        OT_ = sb("OT", KC * N)
        OT = OT_[:, :].rearrange("p (c n) -> p c n", c=KC)
        W = [sb(f"W{i}", SLOT) for i in range(2)]
        rstd = sb("rstd", N)
        par_all = sb("par_all", DEPTH * 40)[:, :].rearrange("p (l c) -> p l c", l=DEPTH)
        par = sb("par", 40)
        qkr = sb("qkr", 60)
        lbt = sb("lbt", 40)
        eps = sb("epsc", 1)[:, 0:1]
        one = sb("onec", 1)[:, 0:1]
        gain = sb("gain", 3 * HD)
        R_ = sb("R", 27640)
        bank = [ctx.enter_context(nc.psum_tensor(f"bank{i}", [P, 512], F32)) for i in range(8)]

        def region(start):
            at = [start]

            def cut(n, upto=None):
                at[0] += n
                assert at[0] <= 27640, at
                return R_[:, at[0] - n:at[0]]
            return cut

        def const(name, rows=P):
            o, w = CONST_W[name]
            return cst[0:rows, o:o + w]

        ident, ones, ones64 = const("ident"), const("ones"), const("ones64")
        G_ATTN, G_MLP, G_HG, G_KC, P_B1, P_LBA, P_OM, P_LNOM, P_HB = 0, 8, 16, 17, 18, 22, 26, 30, 34

        def col(i):
            return par[:, i:i + 1]

        def bc(ap, n):
            return ap.unsqueeze(2).to_broadcast([ap.shape[0], ap.shape[1], n])

        cut = region(0)
        kv_tok = cut(TT * 512).rearrange("p (t c) -> p t c", t=TT)
        win_tok = cut(TT * WINW).rearrange("p (t c) -> p t c", t=TT)
        R_HI = TT * 512 + TT * WINW
        hi_tok = cut(TT * 512).rearrange("p (t c) -> p t c", t=TT)
        q_tok = cut(TT * 512).rearrange("p (t c) -> p t c", t=TT)
        R_HG = R_HI + 2 * TT * 512
        hq = cut(HH * N).rearrange("p (h n) -> p h n", h=HH)
        hf = cut(HH * N).rearrange("p (h n) -> p h n", h=HH)
        hg = cut(HH * N).rearrange("p (h n) -> p h n", h=HH)
        kd = cut(HH * N).rearrange("p (h n) -> p h n", h=HH)
        dec = cut(HH * 24).rearrange("p (h n) -> p h n", h=HH)
        R_TMP = R_HG + 4 * HH * N + HH * 24
        tmp = [cut(N) for _ in range(7)]

        P_LB, NROW = P_LBA, P_LBA + HH
        rows = HT_[0:DEPTH * NROW, 0:P]

        with nc.Block() as block:
            @block.sync
            def _(sp):
                sp.dma_start(W[0][:, :].rearrange("p (t c) -> p t c", t=NT),
                             x_prompt[0].rearrange("(t p) c -> p t c", p=P)).then_inc(sem("x_loaded"), 16)
                sp.dma_start(W[1][0:NS, 0:DM], x_sample.rearrange("b t c -> (b t) c")).then_inc(sem("x_loaded"), 16)
                sp.dma_start(cst[:, :], constants).then_inc(sem("const_loaded"), 16)
                sp.dma_start(pages[:, :], page_table.rearrange("(o a) b -> o (a b)", o=1)).then_inc(sem("pages_loaded"), 16)
                sp.wait_ge(sem("pages_loaded"), 16)

            @block.scalar
            def _(act):
                for l in range(DEPTH):
                    r = l * NROW
                    for src, w, c0 in ((attn_norm_g[l].rearrange("(c p) -> c p", p=P), KC, G_ATTN),
                                       (mlp_norm_g[l].rearrange("(c p) -> c p", p=P), KC, G_MLP),
                                       (hg_norm_g[l].rearrange("(c p) -> c p", p=P), 1, G_HG),
                                       (cmp_b1[l].rearrange("k (c p) -> (k c) p", p=P), 4, P_B1),
                                       (hg_lb_param[l].rearrange("(c p) -> c p", p=P), HH, P_LB)):
                        act.dma_start(rows[r + c0:r + c0 + w, :], src).then_inc(sem("rows_loaded"), 16)
                    for kv in range(NKV):
                        act.dma_start(rows[r + G_KC:r + G_KC + 1, kv * HD:(kv + 1) * HD], k_norm_g[l, 0:1, :]
                                      ).then_inc(sem("rows_loaded"), 16)
                act.wait_ge(sem("lb_centred"), 1)
                act.activation(lbt[:, 16:24], lbt[:, 16:24], ACT.Exp).then_inc(sem("lb_exp"), 1)
                act.wait_ge(sem("lb_ready"), 1)
                act.activation(lbt[:, 32:40], lbt[:, 32:40], ACT.Ln).then_inc(sem("lb_ln"), 1)

            @block.tensor
            def _(pe):
                pe.wait_ge(sem("const_loaded"), 16)
                pe.wait_ge(sem("x_loaded"), 32)
                for c in range(KC):
                    for t in range(NT):
                        ins = pe.transpose(bank[c % 4][:, t * P:(t + 1) * P], W[0][:, t * DM + c * P:t * DM + (c + 1) * P],
                                           ident)
                    ins.then_inc(sem("x_turned"), 1)
                    if c >= 3 and c < KC - 1:
                        pe.wait_ge(sem("x_kept"), c - 2)
                for c in range(KC):
                    ins = pe.transpose(bank[4][:, c * NS:(c + 1) * NS], W[1][0:NS, c * P:(c + 1) * P], ident[0:NS, 0:NS])
                ins.then_inc(sem("x_turned"), 1)
                pe.wait_ge(sem("rows_loaded"), 16 * 7 * DEPTH)
                pe.transpose(bank[5][:, 0:DEPTH * NROW], rows, ident[0:DEPTH * NROW, 0:DEPTH * NROW]
                             ).then_inc(sem("rows_turned"), 1)

            @block.vector
            def _(dve):
                dve.memset(eps, EPS)
                dve.memset(one, 1.0)
                dve.memset(R_[:, 0:R_HG], 0.0).then_inc(sem("cleared"), 1)
                dve.memset(par_all[:, :, P_HB:40], 0.0).then_inc(sem("cleared"), 1)
                for c in range(KC):
                    dve.wait_ge(sem("x_turned"), c + 1)
                    dve.tensor_copy(XT[:, c, 0:SEQ], bank[c % 4][:, :]).then_inc(sem("x_kept"), 1)
                dve.wait_ge(sem("x_turned"), KC + 1)
                dve.tensor_copy(XT[:, :, SEQ:N], bank[4][:, :].rearrange("p (c n) -> p c n", c=KC)
                                ).then_inc(sem("x_kept"), 1)
                dve.wait_ge(sem("rows_turned"), 1)
                turned = bank[5][:, 0:DEPTH * NROW].rearrange("p (l c) -> p l c", l=DEPTH)
                dve.tensor_copy(par_all[:, :, 0:P_LB], turned[:, :, 0:P_LB])
                step(dve, dve.tensor_copy(lbt[:, 0:8].rearrange("p (l c) -> p l c", l=DEPTH), turned[:, :, P_LB:NROW]),
                     "dve_done")
                step(dve, dve.tensor_tensor(lbt[:, 8:12], lbt[:, 0:4], lbt[:, 4:8], ALU.max), "dve_done")
                step(dve, dve.tensor_tensor(lbt[:, 16:20], lbt[:, 0:4], lbt[:, 8:12], ALU.subtract), "dve_done")
                step(dve, dve.tensor_tensor(lbt[:, 20:24], lbt[:, 4:8], lbt[:, 8:12], ALU.subtract), "lb_centred")
                dve.wait_ge(sem("lb_exp"), 1)
                step(dve, dve.tensor_tensor(lbt[:, 8:12], lbt[:, 16:20], lbt[:, 20:24], ALU.add), "dve_done")
                step(dve, dve.reciprocal(lbt[:, 12:16], lbt[:, 8:12]), "dve_done")
                step(dve, dve.tensor_tensor(lbt[:, 16:20], lbt[:, 16:20], lbt[:, 12:16], ALU.mult), "dve_done")
                step(dve, dve.tensor_tensor(lbt[:, 20:24], lbt[:, 20:24], lbt[:, 12:16], ALU.mult), "dve_done")
                step(dve, dve.tensor_tensor(lbt[:, 24:28], lbt[:, 16:20], lbt[:, 20:24], ALU.add), "dve_done")
                step(dve, dve.tensor_tensor(lbt[:, 24:28], lbt[:, 24:28], lbt[:, 16:20], ALU.subtract), "dve_done")
                step(dve, dve.tensor_scalar(lbt[:, 28:32], lbt[:, 24:28], -1.0, 1.0, ALU.mult, ALU.add), "dve_done")
                step(dve, dve.tensor_scalar(lbt[:, 32:36], lbt[:, 24:28], 1e-15, None, ALU.max), "dve_done")
                step(dve, dve.tensor_scalar(lbt[:, 36:40], lbt[:, 28:32], 1e-15, None, ALU.max), "lb_ready")
                dve.wait_ge(sem("lb_ln"), 1)
                for src, ln in ((24, 32), (28, 36)):
                    step(dve, dve.tensor_scalar(lbt[:, 8:12], lbt[:, src:src + 4], 1e-15, NEG, ALU.is_lt, ALU.mult),
                         "dve_done")
                    step(dve, dve.tensor_tensor(lbt[:, ln:ln + 4], lbt[:, ln:ln + 4], lbt[:, 8:12], ALU.add), "dve_done")
                dve.tensor_copy(par_all[:, 1, P_LBA:P_LBA + 4], lbt[:, 32:36])
                dve.tensor_copy(par_all[:, 1, P_OM:P_OM + 4], lbt[:, 28:32])
                dve.tensor_copy(par_all[:, 1, P_LNOM:P_LNOM + 4], lbt[:, 36:40])
                dve.memset(par_all[:, 0, P_LBA:P_LBA + 4], NEG)
                dve.memset(par_all[:, 0, P_OM:P_OM + 4], 1.0)
                dve.memset(par_all[:, 0, P_LNOM:P_LNOM + 4], 0.0)

        loads = []

        def weight_source(l, i):
            wi = w_in[bass.ds(l, 1)].rearrange("o (c p) n -> p (o c) n", p=P)
            if i < 7:
                a, b = [(C_HF, C_HI), (C_HQ, C_HF), (C_HG, C_END), (C_HI, C_HG), (C_Q, C_KV), (C_KV, C_WIN),
                        (C_WIN, C_HQ)][i]
                return wi[:, :, a:b]
            i -= 7
            if i < 2:
                return cmp_w1[bass.ds(l, 1), i].rearrange("o (c p) n -> p (o c) n", p=P)
            i -= 2
            if i < 2:
                return w_out[bass.ds(l, 1)].rearrange("o (c p) n -> p (o c) n", p=P)[:, :, i * 512:(i + 1) * 512]
            i -= 2
            if i < 8:
                return w_up[bass.ds(l, 1)].rearrange("o (c p) n -> p (o c) n", p=P)[:, :, i * 512:(i + 1) * 512]
            i -= 8
            return w_down[bass.ds(l, 1)].rearrange("o (c p) n -> p (o c) n", p=P)[:, :, i * P:(i + 1) * P]

        def slot(i, c):
            w = {6: WINW, 7: CHID, 8: CHID}.get(i, P if i >= 19 else 512)
            return W[i % 2][:, 0:c * w].rearrange("p (c n) -> p c n", c=c)

        SLOT_C = [8] * 7 + [16] * 2 + [8] * 2 + [8] * 8 + [32] * 8

        def load_weight(sp, l, i):
            if i >= 2:
                sp.wait_ge(sem("slot_used"), i - 1)
            sp.dma_start(slot(i, SLOT_C[i]), weight_source(l, i)).then_inc(sem(f"slot{i % 2}_loaded"), 16)

        def slot_ready(pe, i):
            pe.wait_ge(sem(f"slot{i % 2}_loaded"), 16 * (i // 2 + 1))
            return slot(i, SLOT_C[i])

        def exp_ln_tables(act):
            act.preload_act_table_set("natural_log_exp_and_others")

        def norm_products(pe, name):
            for c in range(KC):
                pe.wait_ge(sem(name + "_squared"), c + 1)
                for s in range(2):
                    ins = pe.matmul(bank[s][:, 0:HALF], ones, HT[:, c, s * HALF:(s + 1) * HALF],
                                    start=(c == 0), stop=(c == KC - 1))
            ins.then_inc(sem(name + "_summed"), 1)

        def norm_scalar(act, name, after=None):
            for c in range(KC):
                if after:
                    act.wait_ge(sem(after), 2 * c + 2)
                act.activation(HT[:, c, :], XT[:, c, :], ACT.Square).then_inc(sem(name + "_squared"), 1)
            act.wait_ge(sem(name + "_summed"), 1)
            for s in range(2):
                r = rstd[:, s * HALF:(s + 1) * HALF]
                act.activation(r, bank[s][:, 0:HALF], ACT.Ln, bias=eps, scale=1.0 / DM).then_inc(sem(name + "_ln"), 1)
            for s in range(2):
                r = rstd[:, s * HALF:(s + 1) * HALF]
                act.wait_ge(sem(name + "_ln"), s + 1)
                act.activation(r, r, ACT.Exp, scale=-0.5).then_inc(sem(name + "_rstd"), 1)

        def norm_vector(dve, name, g):
            dve.wait_ge(sem(name + "_rstd"), 2)
            for c in range(KC):
                dve.scalar_tensor_tensor(HT[:, c, :], XT[:, c, :], col(g + c), rstd[:, :], ALU.mult, ALU.mult
                                         ).then_inc(sem(name + "_out"), 1)

        def clear_semaphores():
            with nc.Block() as block:
                @block.gpsimd
                def _(pool):
                    for s in sems.values():
                        pool.sem_clear(s)
            made.clear()

        clear_semaphores()
        layers = ctx.enter_context(ExitStack())
        l = layers.enter_context(nc.Fori(0, DEPTH))

        FT = [hf, hq, hg]
        TOK = [(hi_tok, 512), (q_tok, 512), (kv_tok, 512), (win_tok, WINW)]
        NF = 3 * HH * 2
        HACT = 16
        PB = 6

        with nc.Block() as block:
            @block.sync
            def _(sp):
                for i, g in enumerate((q_norm_g[bass.ds(l, 1)], k_norm_g[bass.ds(l, 1), 1], k_norm_g[bass.ds(l, 1), 2])):
                    sp.dma_start(gain[:, i * HD:(i + 1) * HD], g.to_broadcast([P, HD])).then_inc(sem("gain_loaded"), 16)
                for i in range(9):
                    load_weight(sp, l, i)

            @block.tensor
            def _(pe):
                norm_products(pe, "n1")
                u = 0
                for i in range(3):
                    w = slot_ready(pe, i)
                    for h in range(HH):
                        for s in range(2):
                            if u >= PB:
                                pe.wait_ge(sem("proj_kept"), u - PB + 1)
                            for c in range(KC):
                                if i == 0 and h == 0 and s == 0:
                                    pe.wait_ge(sem("n1_out"), c + 1)
                                ins = pe.matmul(bank[2 + u % PB][:, 0:HALF], w[:, c, h * P:(h + 1) * P],
                                                HT[:, c, s * HALF:(s + 1) * HALF], start=(c == 0), stop=(c == KC - 1))
                            ins.then_inc(sem("proj_done"), 1)
                            u += 1
                    pe.wait_ge(sem("proj_done"), u)
                    pe.sem_inc(sem("slot_used"), 1)
                for i, (dst, w_) in enumerate(TOK):
                    w = slot_ready(pe, 3 + i)
                    for t in range(TT):
                        r = rows_of(t)
                        pe.wait_ge(sem("proj_kept"), u - PB + 1)
                        for c in range(KC):
                            ins = pe.matmul(bank[2 + u % PB][0:r, 0:w_], HT[:, c, t * P:t * P + r], w[:, c, :],
                                            start=(c == 0), stop=(c == KC - 1))
                        ins.then_inc(sem("proj_done"), 1)
                        u += 1
                    pe.wait_ge(sem("proj_done"), u)
                    pe.sem_inc(sem("slot_used"), 1)

            @block.scalar
            def _(act):
                exp_ln_tables(act)
                norm_scalar(act, "n1")

                def keep_features(u):
                    act.wait_ge(sem("proj_done"), u + 1)
                    i, h, s = u // (2 * HH), u // 2 % HH, u % 2
                    act.activation(FT[i][:, h, s * HALF:(s + 1) * HALF], bank[2 + u % PB][:, 0:HALF], ACT.Copy
                                   ).then_inc(sem("proj_kept"), 1)

                def keep_tokens(n):
                    i, t = n // TT, n % TT
                    u = NF + n
                    dst, w_ = TOK[i]
                    act.wait_ge(sem("proj_done"), u + 1)
                    r = rows_of(t)
                    out, src = dst[0:r, t, :], bank[2 + u % PB][0:r, 0:w_]
                    if i == 1:
                        out = out.rearrange("p (g v d) -> p v g d", g=NG, v=NKV)
                        src = src.rearrange("p (v g d) -> p v g d", g=NG, v=NKV)
                    act.activation(out, src, ACT.Copy).then_inc(sem("proj_kept"), 1)

                for u in range(NF):
                    keep_features(u)
                act.wait_ge(sem("proj_kept"), NF)
                for h in range(HH):
                    keep_tokens(5 * h)
                    act.wait_ge(sem("hg_vec"), 4 * h + 1)
                    n = HACT * h
                    for t in (0, 3, 6):
                        act.activation(tmp[t], tmp[t], ACT.Exp, scale=-1.0).then_inc(sem("hg_act"), 1)
                    act.activation(tmp[1], tmp[1], ACT.Exp, scale=-1.0).then_inc(sem("hg_act"), 1)
                    for k, t in enumerate((0, 3, 6)):
                        act.wait_ge(sem("hg_act"), n + k + 1)
                        act.activation(tmp[t], tmp[t], ACT.Ln, bias=one).then_inc(sem("hg_act"), 1)
                    act.wait_ge(sem("hg_act"), n + 5)
                    act.activation(tmp[2], tmp[0], ACT.Exp, scale=-1.0).then_inc(sem("hg_act"), 1)
                    keep_tokens(5 * h + 1)
                    act.wait_ge(sem("hg_vec"), 4 * h + 2)
                    act.activation(tmp[0], tmp[0], ACT.Exp).then_inc(sem("hg_act"), 1)
                    act.wait_ge(sem("hg_act"), n + 9)
                    act.activation(tmp[0], tmp[0], ACT.Ln, bias=one).then_inc(sem("hg_act"), 1)
                    act.activation(tmp[3], tmp[3], ACT.Exp).then_inc(sem("hg_act"), 1)
                    act.activation(hg[:, h, :], tmp[6], ACT.Exp).then_inc(sem("hg_act"), 1)
                    keep_tokens(5 * h + 2)
                    keep_tokens(5 * h + 3)
                    act.wait_ge(sem("hg_vec"), 4 * h + 3)
                    act.activation(tmp[0], tmp[5], ACT.Exp).then_inc(sem("hg_act"), 1)
                    act.activation(tmp[2], tmp[5], ACT.Exp, scale=-1.0).then_inc(sem("hg_act"), 1)
                    act.activation(tmp[4], tmp[4], ACT.Exp).then_inc(sem("hg_act"), 1)
                    act.activation(dec[:, h, :], dec[:, h, :], ACT.Exp).then_inc(sem("hg_act"), 1)
                    keep_tokens(5 * h + 4)

            @block.vector
            def _(dve):
                step(dve, dve.tensor_copy(par[:, :], par_all[:, bass.ds(l, 1), :].rearrange("p o c -> p (o c)")), "par_set")
                norm_vector(dve, "n1", G_ATTN)
                dve.wait_ge(sem("proj_kept"), NF)
                for h in range(HH):
                    z = hf[:, h, :]
                    n = HACT * h
                    t0, t1, t2, t3, t4, t5, t6 = tmp
                    for t, x in ((t0, z), (t3, hq[:, h, :]), (t6, hg[:, h, :])):
                        dve.scalar_tensor_tensor(t, x, -1.0, x, ALU.mult, ALU.max)
                    dve.tensor_scalar(t4, z, 0.0, col(P_LNOM + h), ALU.min, ALU.add)
                    dve.tensor_scalar(t1, z, 0.0, None, ALU.max).then_inc(sem("hg_vec"), 1)
                    dve.wait_ge(sem("hg_act"), n + 8)
                    step(dve, dve.tensor_tensor(t4, t4, t0, ALU.subtract), "dve_done")
                    step(dve, dve.tensor_scalar(t0, t4, col(P_LBA + h), None, ALU.subtract), "dve_done")
                    step(dve, dve.scalar_tensor_tensor(t0, t0, -1.0, t0, ALU.mult, ALU.min), "dve_done")
                    dve.scalar_tensor_tensor(t3, hq[:, h, :], 0.0, t3, ALU.min, ALU.subtract)
                    dve.scalar_tensor_tensor(t6, hg[:, h, :], 0.0, t6, ALU.min, ALU.subtract).then_inc(sem("hg_vec"), 1)
                    dve.scalar_tensor_tensor(t1, t1, col(P_OM + h), t2, ALU.mult, ALU.mult).then_inc(sem("hg_key"), 1)
                    dve.wait_ge(sem("hg_act"), n + 12)
                    step(dve, dve.tensor_tensor(t3, hq[:, h, :], t3, ALU.mult), "dve_done")
                    step(dve, dve.scalar_tensor_tensor(t4, t4, col(P_LBA + h), t0, ALU.max, ALU.add), "dve_done")
                    step(dve, dve.tensor_tensor_scan(t5, const("scan"), t4, 0.0, ALU.mult, ALU.add), "dve_done")
                    bp = t5[:, 0:SEQ].rearrange("p (c n) -> p c n", n=CH)
                    bs = t5[:, SEQ:N].rearrange("p (c n) -> p c n", n=DT)
                    dve.tensor_copy(dec[:, h, 0:16], bp[:, :, CH - 1]).then_inc(sem("hg_last"), 1)
                    dve.tensor_copy(dec[:, h, 16:24], bs[:, :, DT - 1]).then_inc(sem("hg_last"), 1)
                    dve.wait_ge(sem("hg_last"), 2 * h + 2)
                    dve.tensor_tensor(t4[:, 0:SEQ].rearrange("p (c n) -> p c n", n=CH), bc(dec[:, h, 0:16], CH), bp,
                                      ALU.subtract)
                    dve.tensor_tensor(t4[:, SEQ:N].rearrange("p (c n) -> p c n", n=DT), bc(dec[:, h, 16:24], DT), bs,
                                      ALU.subtract).then_inc(sem("hg_vec"), 1)
                    dve.wait_ge(sem("hg_key"), h + 1)
                    dve.wait_ge(sem("hg_act"), n + HACT)
                    dve.tensor_tensor(hq[:, h, :], t3, t0, ALU.mult)
                    dve.tensor_tensor(hf[:, h, :], t1, t2, ALU.mult)
                    dve.tensor_tensor(kd[:, h, :], t1, t4, ALU.mult).then_inc(sem("hg_vec"), 1)
                    dve.wait_ge(sem("hg_vec"), 4 * h + 4)


        cut = region(R_TMP)
        ST = [cut(17 * P).rearrange("p (n e) -> p n e", n=17) for _ in range(2)]
        S0 = [cut(NB * P).rearrange("p (b e) -> p b e", b=NB) for _ in range(2)]
        Snew = cut(NB * P).rearrange("p (b e) -> p b e", b=NB)
        Vm = cut(NB * P).rearrange("p (b e) -> p b e", b=NB)
        aTm = [cut(P) for _ in range(3)]
        aTs = [cut(NS)[0:NS] for _ in range(2)]
        kdt = [cut(P) for _ in range(2)]
        QR = HT_[:, 0:TT * 512].rearrange("p (t c) -> p t c", t=TT)
        KN = HT_[:, TT * 512:TT * 768].rearrange("p (b t c) -> p b t c", b=2, t=TT)
        ROT = OT_[:, 0:4 * N].rearrange("p (b c) -> p b c", b=3)
        ktok = [kv_tok[:, :, 256:384], win_tok[:, :, 0:128]]
        UNITS = 5 * HH

        def span(u):
            h, t = u // 5, u % 5
            r = rows_of(t)
            return h, t, r, slice(t * P, t * P + r)

        def apart(u):
            return Vm[:, 4 * (u % 5 % 2):4 * (u % 5 % 2) + 4] if u % 5 < NT else Vm[0:NS]

        def store_states(sp, h):
            sp.wait_ge(sem("hg_state"), 5 * h + 4)
            sp.dma_start(p_hg[bass.ds(l, 1), 0, h].rearrange("o d e -> (o d) e"), ST[h % 2][:, 16, :]
                         ).then_inc(sem("p_hg_stored"), 16)
            sp.wait_ge(sem("hg_state"), 5 * h + 5)
            sp.dma_start(s_hg[bass.ds(l, 1), :, h].rearrange("o b d e -> d (o b) e"), Snew
                         ).then_inc(sem("s_hg_stored"), 16)

        with nc.Block() as block:
            @block.sync
            def _(sp):
                for h in range(HH):
                    if h >= 2:
                        sp.wait_ge(sem("hg_o_done"), 5 * (h - 1))
                        sp.wait_ge(sem("hg_state"), 5 * (h - 1))
                    sp.dma_start(S0[h % 2], state_hgrn[bass.ds(l, 1), :, h].rearrange("o b d e -> d (o b) e")
                                 ).then_inc(sem(f"s0_loaded{h % 2}"), 16)
                    if h >= 1:
                        store_states(sp, h - 1)
                store_states(sp, HH - 1)
                sp.wait_ge(sem("p_hg_stored"), 16 * HH)
                sp.wait_ge(sem("s_hg_stored"), 16 * HH)

            @block.tensor
            def _(pe):
                def scores(u):
                    h, t, r, c = span(u)
                    if u >= 2:
                        pe.wait_ge(sem("hg_masked"), u - 1)
                        pe.wait_ge(sem("hg_kd_kept"), u - 1)
                    pe.matmul(bank[u % 2][0:r, 0:r], hf[:, h, c], hq[:, h, c], start=True, stop=True
                              ).then_inc(sem("hg_scores"), 1)
                    pe.transpose(bank[2 + u % 2][0:r, 0:P], kd[:, h, c], ident).then_inc(sem("hg_turned"), 1)

                def updates(u):
                    h, t, r, c = span(u)
                    pe.wait_ge(sem("hg_kd_kept"), u + 1)
                    if u >= 1:
                        pe.wait_ge(sem("hg_state"), u)
                    pe.wait_ge(sem("hg_apart"), u + 1)
                    if t < NT:
                        ins = pe.matmul(bank[4][:, :], kdt[u % 2], apart(u), start=True, stop=True)
                    else:
                        for s in range(2):
                            ins = pe.matmul(bank[4 + s][:, :], kdt[u % 2][0:NS, :], apart(u)[:, 4 * s:4 * s + 4, :],
                                            start=True, stop=True)
                    ins.then_inc(sem("hg_updates"), 1)

                def outputs(u):
                    h, t, r, c = span(u)
                    pe.wait_ge(sem("hg_masked"), u + 1)
                    if u >= 2:
                        pe.wait_ge(sem("hg_out_kept"), u - 1)
                    o = bank[6 + u % 2]
                    a = aTm[(4 * h + t) % 3] if t < NT else aTs[h % 2]
                    pe.matmul(o[:, 0:r], hi_tok[0:r, t, h * P:(h + 1) * P], a[:, :], start=True, stop=False)
                    if t < NT:
                        pe.wait_ge(sem("hg_state"), u + 1)
                        n, w, s = NCK, CH, ST[h % 2][:, 4 * t:4 * t + 4, :]
                    else:
                        pe.wait_ge(sem(f"s0_loaded{h % 2}"), 16 * (h // 2 + 1))
                        n, w, s = NB, DT, S0[h % 2]
                    for j in range(n):
                        ins = pe.matmul(o[:, j * w:(j + 1) * w], s[:, j, :], hq[:, h, t * P + j * w:t * P + (j + 1) * w],
                                        start=False, stop=(j == n - 1))
                    ins.then_inc(sem("hg_o_done"), 1)

                for u in range(UNITS + 2):
                    if u < UNITS:
                        scores(u)
                    if 1 <= u <= UNITS:
                        updates(u - 1)
                    if u >= 2:
                        outputs(u - 2)
                for h in range(HH):
                    pe.wait_ge(sem("hgn_squared"), h + 1)
                    if h >= 2:
                        pe.wait_ge(sem("hgn_ln"), h - 1)
                    for s in range(2):
                        ins = pe.matmul(bank[2 * (h % 2) + s][:, 0:HALF], ones, kd[:, h, s * HALF:(s + 1) * HALF],
                                        start=True, stop=True)
                    ins.then_inc(sem("hgn_summed"), 1)

            @block.scalar
            def _(act):
                act.activation(HT_[:, 0:TT * 512].rearrange("p (t c) -> p t c", t=TT), q_tok, ACT.Square
                               ).then_inc(sem("qk_squared"), 1)
                for b in range(2):
                    act.activation(KN[:, b], ktok[b], ACT.Square).then_inc(sem("qk_squared"), 1)
                act.wait_ge(sem("qk_summed"), 3)
                act.activation(qkr[:, 0:60], qkr[:, 0:60], ACT.Ln, bias=eps, scale=1.0 / HD).then_inc(sem("qk_ln"), 1)
                act.wait_ge(sem("qk_ln"), 1)
                act.activation(qkr[:, 0:60], qkr[:, 0:60], ACT.Exp, scale=-0.5).then_inc(sem("qk_rstd"), 1)
                for u in range(UNITS + 3):
                    if u < UNITS:
                        h, t, r, c = span(u)
                        act.wait_ge(sem("hg_turned"), u + 1)
                        if u >= 2:
                            act.wait_ge(sem("hg_updates"), u - 1)
                        act.activation(kdt[u % 2][0:r, :], bank[2 + u % 2][0:r, 0:P], ACT.Copy
                                       ).then_inc(sem("hg_kd_kept"), 1)
                    if u >= 3:
                        h, t, r, c = span(u - 3)
                        act.wait_ge(sem("hg_o_done"), u - 2)
                        act.activation(OT[:, 4 + h, c], bank[6 + (u - 3) % 2][:, 0:r], ACT.Copy
                                       ).then_inc(sem("hg_out_kept"), 1)
                act.wait_ge(sem("hg_out_kept"), UNITS)
                for h in range(HH):
                    act.activation(kd[:, h, :], OT[:, 4 + h, :], ACT.Square).then_inc(sem("hgn_squared"), 1)
                for h in range(HH):
                    act.wait_ge(sem("hgn_summed"), h + 1)
                    for s in range(2):
                        ins = act.activation(hq[:, h, s * HALF:(s + 1) * HALF], bank[2 * (h % 2) + s][:, 0:HALF], ACT.Ln,
                                             bias=eps, scale=1.0 / P)
                    ins.then_inc(sem("hgn_ln"), 1)
                    act.wait_ge(sem("hgn_ln"), h + 1)
                    act.activation(hq[:, h, :], hq[:, h, :], ACT.Exp, scale=-0.5).then_inc(sem("hgn_rstd"), 1)

            @block.vector
            def _(dve):
                for i in range(3):
                    dve.memset(aTm[i], 0.0)
                for i in range(2):
                    dve.memset(aTs[i], 0.0)
                    dve.memset(ST[i][:, 0, :], 0.0)
                dve.wait_ge(sem("qk_squared"), 3)
                dve.tensor_reduce(qkr[:, 0:40], QR.rearrange("p t (h d) -> p (t h) d", d=HD), AX, ALU.add
                                  ).then_inc(sem("qk_summed"), 1)
                for b in range(2):
                    dve.tensor_reduce(qkr[:, 40 + 10 * b:50 + 10 * b], KN[:, b].rearrange("p t (h d) -> p (t h) d", d=HD),
                                      AX, ALU.add).then_inc(sem("qk_summed"), 1)
                dve.wait_ge(sem("qk_summed"), 3)

                def masked(u):
                    h, t, r, c = span(u)
                    dve.wait_ge(sem("hg_scores"), u + 1)
                    if u >= 3:
                        dve.wait_ge(sem("hg_o_done"), u - 2)
                    a = aTm[(4 * h + t) % 3] if t < NT else aTs[h % 2]
                    m = const("hgmask") if t < NT else const("hgmask8", NS)
                    dve.copy_predicated(a, m.bitcast(U32), bank[u % 2][0:r, 0:r]).then_inc(sem("hg_masked"), 1)
                    if u >= 2:
                        dve.wait_ge(sem("hg_updates"), u if t in (0, NT) else u - 1)
                    n, m = (NCK, const("chunk")) if t < NT else (NB, const("batch", NS))
                    dve.tensor_tensor(apart(u), hi_tok[0:r, t, h * P:(h + 1) * P].unsqueeze(1).to_broadcast([r, n, P]),
                                      bc(m, P), ALU.mult).then_inc(sem("hg_apart"), 1)

                def states(u):
                    h, t, r, c = span(u)
                    dve.wait_ge(sem("hg_updates"), u + 1)
                    if t < NT:
                        if h >= 2 and t == 0:
                            dve.wait_ge(sem("p_hg_stored"), 16 * (h - 1))
                            dve.wait_ge(sem("hg_o_done"), 5 * (h - 1))
                        s = ST[h % 2]
                        for j in range(NCK):
                            n = 4 * t + j
                            ins = dve.scalar_tensor_tensor(s[:, n + 1, :], s[:, n, :], dec[:, h, n:n + 1],
                                                           bank[4][:, j * P:(j + 1) * P], ALU.mult, ALU.add)
                            if j < NCK - 1:
                                step(dve, ins, "dve_done")
                        ins.then_inc(sem("hg_state"), 1)
                        dve.wait_ge(sem("hg_state"), u + 1)
                    else:
                        dve.wait_ge(sem(f"s0_loaded{h % 2}"), 16 * (h // 2 + 1))
                        if h >= 1:
                            dve.wait_ge(sem("s_hg_stored"), 16 * h)
                        for b in range(NB):
                            ins = dve.scalar_tensor_tensor(Snew[:, b, :], S0[h % 2][:, b, :], dec[:, h, 16 + b:17 + b],
                                                           bank[4 + b // 4][:, (b % 4) * P:(b % 4 + 1) * P],
                                                           ALU.mult, ALU.add)
                        ins.then_inc(sem("hg_state"), 1)

                for u in range(UNITS + 1):
                    if u < UNITS:
                        masked(u)
                    if u >= 1:
                        states(u - 1)
                for h in range(HH):
                    dve.wait_ge(sem("hgn_rstd"), h + 1)
                    step(dve, dve.scalar_tensor_tensor(OT[:, 4 + h, :], OT[:, 4 + h, :], col(G_HG), hq[:, h, :],
                                                       ALU.mult, ALU.mult), "dve_done")
                    dve.tensor_tensor(OT[:, 4 + h, :], OT[:, 4 + h, :], hg[:, h, :], ALU.mult)

            @block.gpsimd
            def _(pool):
                pool.wait_ge(sem("qk_rstd"), 1)
                pool.wait_ge(sem("gain_loaded"), 48)

                def norm(dst, src, r0, nh, g):
                    d = dst.rearrange("p t (h d) -> p t h d", d=HD)
                    s = src.rearrange("p t (h d) -> p t h d", d=HD)
                    r = qkr[:, r0:r0 + TT * nh].rearrange("p (t h) -> p t h", t=TT)
                    g_ = gain[:, g * HD:(g + 1) * HD].unsqueeze(1).to_broadcast([P, nh, HD])
                    for t in range(TT):
                        step(pool, pool.tensor_tensor(d[:, t], s[:, t], bc(r[:, t], HD), ALU.mult), "pool_done")
                        step(pool, pool.tensor_tensor(d[:, t], d[:, t], g_, ALU.mult), "pool_done")

                def rotate(dst, src, nh):
                    d = dst.rearrange("p t (h d) -> p t h d", d=HD)
                    s = src.rearrange("p t (h d) -> p t h d", d=HD)
                    F = HD // 2
                    cos = const("cos").rearrange("p (t f) -> p t f", f=F)
                    sin = const("sin").rearrange("p (t f) -> p t f", f=F)
                    a, b = (ROT[:, i, 0:nh * F].rearrange("p (h f) -> p h f", f=F) for i in range(2))
                    for t in range(TT):
                        c_ = cos[:, t].unsqueeze(1).to_broadcast([P, nh, F])
                        s_ = sin[:, t].unsqueeze(1).to_broadcast([P, nh, F])
                        for lo, x, y, op in ((0, 0, F, ALU.subtract), (F, F, 0, ALU.add)):
                            pool.tensor_tensor(a, s[:, t, :, x:x + F], c_, ALU.mult)
                            step(pool, pool.tensor_tensor(b, s[:, t, :, y:y + F], s_, ALU.mult), "pool_done")
                            step(pool, pool.tensor_tensor(d[:, t, :, lo:lo + F], a, b, op), "pool_done")

                norm(q_tok, q_tok, 0, NH, 0)
                for b in range(2):
                    norm(KN[:, b], ktok[b], 40 + 10 * b, NKV, 1 + b)
                    rotate(ktok[b], KN[:, b], NKV)
                rotate(QR, q_tok, NH)


        o_tok = hi_tok
        cut = region(R_HG)
        QN = cut(NG * N).rearrange("p (g n) -> p g n", g=NG)
        QT = cut(NG * N).rearrange("p (g n) -> p g n", g=NG)
        KT = cut(2 * N).rearrange("p (b n) -> p b n", b=2)
        gate = cut(TT * 24).rearrange("p (t c) -> p t c", t=TT)
        R_ATT = R_HG + (2 * NG + 2) * N + TT * 24
        probs = [cut(512) for _ in range(3)]
        probsT = [cut(512) for _ in range(2)]
        nmax, rsum, coef, otmp = cut(64), cut(64), cut(64), cut(512)
        SCALE = HD ** -0.5
        vtok = [kv_tok[:, :, 384:512], win_tok[:, :, 128:256]]

        TURNS = [(k, t) for t in range(TT) for k in range(3)]
        AU = [(t, b, v, g) for t in range(NT) for b in range(2) for v in range(NKV) for g in range(NG)]
        AG = len(AU) // NH

        def turn_views(k, t):
            r = rows_of(t)
            n = NG if k < 2 else 2
            dst = (QN, QT, KT)[k][:, :, t * P:t * P + r]
            return r, n, dst

        def kept_before(n, parity):
            return (n + 1 - parity) // 2

        with nc.Block() as block:
            @block.sync
            def _(sp):
                sp.dma_start(p_nsa[bass.ds(l, 1)].rearrange("o b (t p) k h d -> p (o b t) (k h d)", p=P),
                             kv_tok[:, 0:NT, :]).then_inc(sem("nsa_stored"), 16)
                sp.dma_start(s_nsa[bass.ds(l, 1)].rearrange("o b t k h d -> (o b t) (k h d)"),
                             kv_tok[0:NS, NT, :]).then_inc(sem("rows_stored"), 16)
                sp.dma_start(p_win[bass.ds(l, 1)].rearrange("o b (t p) k h d -> p (o b t) (k h d)", p=P),
                             win_tok[:, 0:NT, 0:256]).then_inc(sem("rows_stored"), 16)
                sp.dma_start(s_win[bass.ds(l, 1)].rearrange("o b t k h d -> (o b t) (k h d)"),
                             win_tok[0:NS, NT, 0:256]).then_inc(sem("rows_stored"), 16)
                sp.wait_ge(sem("nsa_stored"), 16)
                sp.wait_ge(sem("rows_stored"), 48)

            @block.tensor
            def _(pe):
                for u, (k, t) in enumerate(TURNS):
                    r, n, dst = turn_views(k, t)
                    if u >= 4:
                        pe.wait_ge(sem(f"turn_kept{u % 2}"), (u - 4) // 2 + 1)
                    for g in range(n):
                        src = (q_tok, QR)[k][0:r, t, g * P:(g + 1) * P] if k < 2 else ktok[g][0:r, t, :]
                        ins = pe.transpose(bank[u % 4][:, g * r:(g + 1) * r], src, ident[0:r, 0:r])
                    ins.then_inc(sem("turned"), 1)
                for i in range(2):
                    pe.wait_ge(sem(f"turn_kept{i}"), kept_before(len(TURNS), i))

                def scores(n):
                    t, b, v, g = AU[n]
                    if n >= 3:
                        pe.wait_ge(sem("probs_made"), n - 2)
                    k = slice(v * HD, (v + 1) * HD)
                    pe.matmul(bank[n % 3][:, 0:(t + 1) * P], QT[k, g, t * P:(t + 1) * P], KT[k, b, 0:(t + 1) * P],
                              start=True, stop=True).then_inc(sem("scored"), 1)

                def turn_probs(n):
                    t, b, v, g = AU[n]
                    pe.wait_ge(sem("probs_made"), n + 1)
                    if n >= 2:
                        pe.wait_ge(sem(f"probsT_kept{n % 2}"), n // 2)
                    for j in range(t + 1):
                        ins = pe.transpose(bank[3 + n % 2][:, j * P:(j + 1) * P], probs[n % 3][:, j * P:(j + 1) * P], ident)
                    ins.then_inc(sem("probs_turned"), 1)

                def values(n):
                    t, b, v, g = AU[n]
                    grp, h = n // NH, n % NH
                    if h == 0 and grp >= 2:
                        pe.wait_ge(sem("o_kept"), grp - 1)
                    pe.wait_ge(sem(f"probsT_kept{n % 2}"), n // 2 + 1)
                    for j in range(t + 1):
                        ins = pe.matmul(bank[5 + grp % 2][:, h * HD:(h + 1) * HD], probsT[n % 2][:, j * P:(j + 1) * P],
                                        vtok[b][:, j, v * HD:(v + 1) * HD], start=(j == 0), stop=(j == t))
                    ins.then_inc(sem("valued"), 1)

                for n in range(len(AU) + 3):
                    if n < len(AU):
                        scores(n)
                    if 2 <= n < len(AU) + 2:
                        turn_probs(n - 2)
                    if n >= 3:
                        values(n - 3)

            def keep_turn(eng, u):
                k, t = TURNS[u]
                r, n, dst = turn_views(k, t)
                eng.wait_ge(sem("turned"), u + 1)
                src = bank[u % 4][:, 0:n * r].rearrange("p (g n) -> p g n", g=n)
                if eng is nc.scalar:
                    ins = eng.activation(dst, src, ACT.Copy, scale=SCALE if k < 2 else 1.0)
                else:
                    ins = eng.tensor_scalar(dst, src, SCALE if k < 2 else 1.0, None, ALU.mult)
                ins.then_inc(sem(f"turn_kept{u % 2}"), 1)

            def keep_probsT(eng, n):
                t = AU[n][0]
                eng.wait_ge(sem("probs_turned"), n + 1)
                if n >= 2:
                    eng.wait_ge(sem("valued"), n - 1)
                src, dst = bank[3 + n % 2][:, 0:(t + 1) * P], probsT[n % 2][:, 0:(t + 1) * P]
                ins = eng.activation(dst, src, ACT.Copy) if eng is nc.scalar else eng.tensor_copy(dst, src)
                ins.then_inc(sem(f"probsT_kept{n % 2}"), 1)

            @block.scalar
            def _(act):
                act.activation(gate, win_tok[:, :, 256:WINW], ACT.Exp, scale=-1.0).then_inc(sem("gate_exp"), 1)
                for u in range(0, len(TURNS), 2):
                    keep_turn(nc.scalar, u)
                for n in range(len(AU) + 3):
                    if n < len(AU):
                        t = AU[n][0]
                        act.wait_ge(sem("maxed"), n + 1)
                        if n >= 3:
                            act.wait_ge(sem("probs_turned"), n - 2)
                        act.activation(probs[n % 3][:, 0:(t + 1) * P], bank[n % 3][:, 0:(t + 1) * P], ACT.Exp,
                                       bias=nmax[:, n:n + 1], accum_out=rsum[:, n:n + 1]).then_inc(sem("probs_made"), 1)
                    if n >= 3 and (n - 3) % 2 == 0:
                        keep_probsT(nc.scalar, n - 3)

            @block.vector
            def _(dve):
                dve.wait_ge(sem("gate_exp"), 1)
                step(dve, dve.tensor_scalar(gate, gate, 1.0, None, ALU.add), "dve_done")
                step(dve, dve.reciprocal(gate, gate), "dve_done")
                for u in range(1, len(TURNS), 2):
                    keep_turn(nc.vector, u)

                def keep_group(grp):
                    t, b = AU[grp * NH][0:2]
                    c = coef[:, grp * NH:(grp + 1) * NH]
                    step(dve, dve.reciprocal(c, rsum[:, grp * NH:(grp + 1) * NH]), "dve_done")
                    step(dve, dve.tensor_tensor(c, c, gate[:, t, :].rearrange("p (h b) -> p h b", b=3)[:, :, 1 + b],
                                                ALU.mult), "dve_done")
                    dve.wait_ge(sem("valued"), NH * (grp + 1))
                    o = bank[5 + grp % 2][:, :].rearrange("p (h d) -> p h d", d=HD)
                    dst = (o_tok[:, t, :] if b == 0 else otmp).rearrange("p (h d) -> p h d", d=HD)
                    dve.tensor_tensor(dst, o, bc(c, HD), ALU.mult).then_inc(sem("o_kept"), 1)
                    if b == 1:
                        dve.wait_ge(sem("o_kept"), grp + 1)
                        step(dve, dve.tensor_tensor(o_tok[:, t, :], o_tok[:, t, :], otmp, ALU.add), "dve_done")

                for n in range(len(AU) + 6):
                    if n < len(AU):
                        t = AU[n][0]
                        dve.wait_ge(sem("scored"), n + 1)
                        d = bank[n % 3][:, t * P:(t + 1) * P]
                        step(dve, dve.tensor_tensor(d, d, const("causal"), ALU.add), "dve_done")
                        dve.tensor_reduce(nmax[:, n:n + 1], bank[n % 3][:, 0:(t + 1) * P], AX, ALU.max, negate=True
                                          ).then_inc(sem("maxed"), 1)
                    if n >= 3 and n - 3 < len(AU) and (n - 3) % 2 == 1:
                        keep_probsT(nc.vector, n - 3)
                    if n >= 5 and (n - 5) % NH == NH - 1:
                        keep_group((n - 5) // NH)


        raw = [HT_[:, i * 2048:(i + 1) * 2048].rearrange("p (v r d) -> p v r d", v=NKV, r=CST) for i in range(2)]
        cut = region(R_HI + TT * 512)
        KCT, VCT = cut(NCALL), cut(NCALL)
        VC = cut(4 * P).rearrange("p (a c) -> p a c", a=4)
        VB = cut(NKV * 256).rearrange("p (v c) -> p v c", v=NKV)
        cut = region(R_ATT)
        FTC = cut(NKV * 8 * NCALL).rearrange("p (v r n) -> p v r n", v=NKV, r=8)
        GH = cut(NKV * 2 * NCALL).rearrange("p (v h n) -> p v h n", v=NKV, h=2)
        cx, cu = cut(NCALL), cut(NCALL)
        W2 = OT_[:, 0:1024].rearrange("p (k v h c) -> p k v h c", k=2, v=NKV, h=2)
        posr = OT_[0:32, 1024:1152]
        posT = OT_[:, 1152:1184]
        G_A, G_B = (2 / np.pi) ** 0.5, 0.044715 * (2 / np.pi) ** 0.5
        CT = [(k, p, v, q) for k in range(2) for p in range(5) for v in range(NKV if p < 4 else 1)
              for q in range(2 if p < 4 else 1)]
        CU = [(k, i) for k in range(2) for i in range(6)]

        with nc.Block() as block:
            @block.sync
            def _(sp):
                for k in range(2):
                    sp.dma_start(posr[16 * k:16 * k + 16, :],
                                 cmp_pos[bass.ds(l, 1), k].rearrange("o (a b) d -> (o a) (b d)", b=2)
                                 ).then_inc(sem("pos_loaded"), 16)
                sp.wait_ge(sem("w2_cleared"), 1)
                for k in range(2):
                    for v in range(NKV):
                        sp.dma_start(W2[:, k, v, :, v * HD:(v + 1) * HD],
                                     cmp_w2[bass.ds(l, 1), k].rearrange("o (h p) d -> p (o h) d", p=P)
                                     ).then_inc(sem("w2_loaded"), 16)
                for k in range(2):
                    for p in range(5):
                        n = 5 * k + p
                        if n >= 2:
                            sp.wait_ge(sem("raw_used"), n - 1)
                        if p == 4:
                            for v in range(NKV):
                                sp.dma_start(raw[n % 2][0:NCP, v],
                                             p_nsa[bass.ds(l, 1), 0, :, k, v].rearrange("o (c r) d -> (o c) r d", r=CST)
                                             ).then_inc(sem(f"raw_loaded{n % 2}"), 16)
                            continue
                        for j in range(16):
                            pg = sp.value_load(pages[0:1, 16 * p + j:16 * p + j + 1], min_val=0, max_val=NPOOL - 1)
                            for v in range(NKV):
                                sp.dma_start(raw[n % 2][8 * j:8 * j + 8, v],
                                             cache_nsa_kv[bass.ds(l, 1), bass.ds(pg, 1), :, k, v].rearrange(
                                                 "o q (c r) d -> (o q c) r d", r=CST)
                                             ).then_inc(sem(f"raw_loaded{n % 2}"), 16)
                for i in (9, 10):
                    load_weight(sp, l, i)

            def raw_count(n):
                return sum(32 if m % 5 == 4 else 512 for m in range(n % 2, n + 1, 2))

            @block.tensor
            def _(pe):
                w1 = [slot_ready(pe, 7), slot_ready(pe, 8)]
                pe.wait_ge(sem("pos_loaded"), 32)
                pe.transpose(bank[6][:, 0:32], posr, ident[0:32, 0:32]).then_inc(sem("pos_turned"), 1)
                pe.wait_ge(sem("pos_kept"), 1)
                for k in range(2):
                    for h in range(2):
                        for r in range(16):
                            ins = pe.matmul(bank[7][:, 2 * k + h:2 * k + h + 1], w1[k][:, r, h * P:(h + 1) * P],
                                            posT[:, 16 * k + r:16 * k + r + 1], start=(r == 0), stop=(r == 15))
                ins.then_inc(sem("bias_done"), 1)
                u = 0
                j = 0
                for k in range(2):
                    for u in range(17 * k, 17 * k + 17):
                        _, p, v, q = CT[u]
                        n = 5 * k + p
                        if u >= 4:
                            pe.wait_ge(sem(f"ct_kept{u % 2}"), (u - 4) // 2 + 1)
                        if v == 0 and q == 0:
                            pe.wait_ge(sem(f"raw_loaded{n % 2}"), raw_count(n))
                        if p < 4:
                            for r in range(4):
                                ins = pe.transpose(bank[u % 4][:, r * P:(r + 1) * P],
                                                   raw[n % 2][:, v, 8 * q + 2 * r:8 * q + 2 * r + 2, :], ident)
                        else:
                            for r in range(16):
                                ins = pe.transpose(bank[u % 4][:, r * NCP:(r + 1) * NCP],
                                                   raw[n % 2][0:NCP, r // 8, 2 * (r % 8):2 * (r % 8) + 2, :],
                                                   ident[0:NCP, 0:NCP])
                        ins.then_inc(sem("ct_done"), 1)
                        if p == 4 or (v == 1 and q == 1):
                            pe.wait_ge(sem("ct_done"), u + 1)
                            pe.sem_inc(sem("raw_used"), 1)
                    for i in range(2):
                        pe.wait_ge(sem(f"ct_kept{i}"), kept_before(17 * k + 17, i))
                    for i in range(6):
                        j = 6 * k + i
                        B, C = bank[4 + j % 2], bank[6 + j % 2]
                        if j >= 2:
                            pe.wait_ge(sem("cu_kept"), j - 1)
                        elif j == 1:
                            pe.wait_ge(sem("bias_kept"), 1)
                        if i < 4:
                            v, h = i // 2, i % 2
                            for r in range(16):
                                s = r // 8
                                w = w1[k][:, r, h * P:(h + 1) * P]
                                pe.matmul(B[:, 0:NCC - s], w, FTC[:, v, r % 8, s:NCC], start=(r == 0), stop=(r == 15))
                                ins = pe.matmul(C[:, 0:NCP - s], w, FTC[:, v, r % 8, NCC + s:NCALL],
                                                start=(r == 0), stop=(r == 15))
                            if i == 3:
                                ins.then_inc(sem("cu_done"), 1)
                                pe.wait_ge(sem("cu_done"), j + 1)
                                pe.sem_inc(sem("slot_used"), 1)
                                continue
                        elif i == 4:
                            pe.wait_ge(sem("w2_loaded"), 64)
                            pe.wait_ge(sem("gelu_done"), 4 * k + 4)
                            for m in range(4):
                                v, h = m // 2, m % 2
                                w = W2[:, k, v, h, :]
                                pe.matmul(B[:, :], w, GH[:, v, h, 0:NCC], start=(m == 0), stop=(m == 3))
                                ins = pe.matmul(C[:, 0:NCP], w, GH[:, v, h, NCC:NCALL], start=(m == 0), stop=(m == 3))
                        elif k == 0:
                            pe.wait_ge(sem("kc_squared"), 1)
                            pe.matmul(B[:, :], ones64, cu[:, 0:NCC], start=True, stop=True)
                            ins = pe.matmul(C[:, 0:NCP], ones64, cu[:, NCC:NCALL], start=True, stop=True)
                        else:
                            pe.wait_ge(sem("vct_kept"), 1)
                            for a in range(4):
                                pe.transpose(B[:, a * P:(a + 1) * P], VCT[:, a * P:(a + 1) * P], ident)
                            ins = pe.transpose(C[:, 0:P], cx[:, 0:P], ident)
                        ins.then_inc(sem("cu_done"), 1)

            def keep_ct(eng, u):
                k, p, v, q = CT[u]
                eng.wait_ge(sem("ct_done"), u + 1)
                if k == 1:
                    eng.wait_ge(sem("cu_done"), 4)
                if p < 4:
                    dst = FTC[:, v, 4 * q:4 * q + 4, p * P:(p + 1) * P]
                    src = bank[u % 4][:, :].rearrange("p (r n) -> p r n", r=4)
                else:
                    dst = FTC[:, :, :, NCC:NCALL].rearrange("p v r n -> p (v r) n")
                    src = bank[u % 4][:, :].rearrange("p (r n) -> p r n", n=NCP)
                ins = eng.activation(dst, src, ACT.Copy) if eng is nc.scalar else eng.tensor_copy(dst, src)
                ins.then_inc(sem(f"ct_kept{u % 2}"), 1)

            @block.scalar
            def _(act):
                act.wait_ge(sem("pos_turned"), 1)
                act.activation(posT, bank[6][:, 0:32], ACT.Copy).then_inc(sem("pos_kept"), 1)
                for k in range(2):
                    for u in range(17 * k, 17 * k + 17):
                        if u % 2 == 0:
                            keep_ct(nc.scalar, u)
                    for i in range(4):
                        j = 6 * k + i
                        m = 4 * k + i
                        v, h = i // 2, i % 2
                        b = par[:, P_HB + 2 * k + h:P_HB + 2 * k + h + 1]
                        act.wait_ge(sem("bias_kept"), 1)
                        act.wait_ge(sem("cu_done"), j + 1)
                        if m >= 1:
                            act.wait_ge(sem("gelu_done"), m)
                        act.activation(cx[:, 0:NCC], bank[4 + j % 2][:, :], ACT.Identity, bias=b)
                        act.activation(cx[:, NCC:NCALL], bank[6 + j % 2][:, 0:NCP], ACT.Identity, bias=b
                                       ).then_inc(sem("cu_kept"), 1)
                        act.wait_ge(sem("gelu_arg"), m + 1)
                        for f, kw in ((ACT.Exp, dict(scale=-2.0)), (ACT.Ln, dict(bias=one)), (ACT.Exp, dict(scale=-1.0))):
                            step(act, act.activation(cu, cu, f, **kw), "gelu_act")
                    j = 6 * k + 4
                    act.wait_ge(sem("cu_done"), j + 1)
                    B, C = bank[4 + j % 2], bank[6 + j % 2]
                    dst = (KCT, VCT)[k]
                    if k == 0:
                        act.wait_ge(sem("gelu_done"), 4)
                        act.activation(cu[:, 0:NCC], B[:, :], ACT.Square)
                        act.activation(cu[:, NCC:NCALL], C[:, 0:NCP], ACT.Square).then_inc(sem("kc_squared"), 1)
                    act.activation(dst[:, 0:NCC], B[:, :], ACT.Copy)
                    act.activation(dst[:, NCC:NCALL], C[:, 0:NCP], ACT.Copy).then_inc(sem("cu_kept"), 1)
                    j += 1
                    B, C = bank[4 + j % 2], bank[6 + j % 2]
                    if k == 0:
                        act.wait_ge(sem("cu_done"), j + 1)
                        act.activation(cx[:, 0:NCC], B[:, :], ACT.Ln, bias=eps, scale=1.0 / HD)
                        act.activation(cx[:, NCC:NCALL], C[:, 0:NCP], ACT.Ln, bias=eps, scale=1.0 / HD
                                       ).then_inc(sem("cu_kept"), 1)
                        act.wait_ge(sem("cu_kept"), j + 1)
                        act.activation(cx, cx, ACT.Exp, scale=-0.5).then_inc(sem("kc_rstd"), 1)
                    else:
                        act.wait_ge(sem("cu_kept"), j)
                        act.activation(cx[:, 0:P].rearrange("p (g n) -> p g n", g=NG),
                                       VCT[:, NCC:NCALL].unsqueeze(1).to_broadcast([P, NG, NCP]), ACT.Copy
                                       ).then_inc(sem("vct_kept"), 1)

            @block.vector
            def _(dve):
                dve.memset(W2, 0.0).then_inc(sem("w2_cleared"), 1)
                dve.memset(VB, 0.0)
                dve.wait_ge(sem("bias_done"), 1)
                dve.tensor_tensor(par[:, P_HB:P_HB + 4], bank[7][:, 0:4], par[:, P_B1:P_B1 + 4], ALU.add
                                  ).then_inc(sem("bias_kept"), 1)
                for k in range(2):
                    for u in range(17 * k, 17 * k + 17):
                        if u % 2 == 1:
                            keep_ct(nc.vector, u)
                    for i in range(4):
                        j = 6 * k + i
                        m = 4 * k + i
                        v, h = i // 2, i % 2
                        dve.wait_ge(sem("cu_kept"), j + 1)
                        step(dve, dve.tensor_tensor(cu, cx, cx, ALU.mult), "dve_done")
                        step(dve, dve.tensor_scalar(cu, cu, float(G_B), float(G_A), ALU.mult, ALU.add), "dve_done")
                        step(dve, dve.tensor_tensor(cu, cu, cx, ALU.mult), "dve_done")
                        dve.tensor_scalar(cu, cu, -20.0, None, ALU.max).then_inc(sem("gelu_arg"), 1)
                        dve.wait_ge(sem("gelu_act"), 3 * (m + 1))
                        if k == 1 and i == 0:
                            dve.wait_ge(sem("cu_done"), 5)
                        dve.tensor_tensor(GH[:, v, h, :], cx, cu, ALU.mult).then_inc(sem("gelu_done"), 1)
                    if k == 0:
                        dve.wait_ge(sem("kc_rstd"), 1)
                        dve.scalar_tensor_tensor(KCT, KCT, col(G_KC), cx, ALU.mult, ALU.mult).then_inc(sem("kc_done"), 1)
                        dve.wait_ge(sem("kc_done"), 1)
                    else:
                        j = 6 * k + 5
                        dve.wait_ge(sem("cu_done"), j + 1)
                        dve.tensor_copy(VC.rearrange("p a c -> p (a c)"), bank[4 + j % 2][:, :])
                        for v in range(NKV):
                            for g in range(NG):
                                rr = slice(g * NCP, (g + 1) * NCP)
                                dve.tensor_copy(VB[rr, v, g * HD:(g + 1) * HD], bank[6 + j % 2][rr, v * HD:(v + 1) * HD])


        QD = HT_[:, 0:1024].rearrange("p (k b r) -> p k b r", k=2, b=NB)
        oS = HT_[0:NS, 1024:2560].rearrange("p (b c d) -> p b c d", b=NB, c=3)
        o3 = HT_[0:NS, 2560:4096]
        DMk = HT_[0:NS, 4096:4224].rearrange("p (b j) -> p b j", b=NB)
        cut = region(R_ATT)
        cs = [cut(256) for _ in range(2)]
        csT = [cut(256) for _ in range(2)]
        cst_ = cut(64)
        cm = [cut(256) for _ in range(2)]
        otm = cut(512)
        ss = cut(512)[0:NS].rearrange("p (b c) -> p b c", b=NB)
        ssT = cut(256).rearrange("p (a r) -> p a r", a=4)
        sm = cut(128)[0:NS]
        imp = cut(128)[0:NS].rearrange("p (b j) -> p b j", b=NB)
        val = cut(128)[0:NS].rearrange("p (b j) -> p b j", b=NB)
        NC = NCS - 1

        with nc.Block() as block:
            @block.tensor
            def _(pe):
                pe.wait_ge(sem("qd_made"), 2)
                for b in range(NB):
                    ins = pe.matmul(bank[4][0:NS, b * NCS:(b + 1) * NCS], QD[:, 0, b, :], KCT[:, b * NCS:(b + 1) * NCS],
                                    start=True, stop=True)
                ins.then_inc(sem("s_scored"), 1)

                def prompt_scores(t):
                    if t >= 2:
                        pe.wait_ge(sem("c_read"), 2 * (t - 1))
                    for v in range(NKV):
                        k = slice(v * HD, (v + 1) * HD)
                        for g in range(NG):
                            ins = pe.matmul(bank[2 * (t % 2) + v][:, g * NCP:(g + 1) * NCP],
                                            QN[k, g, t * P:(t + 1) * P], KCT[k, NCC:NCALL], start=True, stop=True)
                    ins.then_inc(sem("c_scored"), 1)

                prompt_scores(0)
                prompt_scores(1)
                pe.wait_ge(sem("s_probs"), 1)
                pe.matmul(bank[5][0:NS, :], const("groupsum", NS), ss, start=True, stop=True).then_inc(sem("s_imp"), 1)
                for a in range(4):
                    ins = pe.transpose(bank[4][:, a * NS:(a + 1) * NS], ss[:, 2 * a:2 * a + 2, :], ident[0:NS, 0:NS])
                ins.then_inc(sem("s_turned"), 1)
                pe.wait_ge(sem("s_turn_kept"), 1)
                for a in range(4):
                    for q in range(2):
                        k = slice(q * HD, (q + 1) * HD)
                        ins = pe.matmul(bank[6 + q][0:NS, a * P:(a + 1) * P], ssT[k, a, :], VC[k, a, :],
                                        start=True, stop=True)
                ins.then_inc(sem("s_valued"), 1)
                for t in range(NT):
                    if 2 <= t + 1 < NT:
                        prompt_scores(t + 1)
                    pe.wait_ge(sem("c_probs"), t + 1)
                    if t == 0:
                        pe.wait_ge(sem("s_imp_kept"), 1)
                    for v in range(NKV):
                        ins = pe.transpose(bank[4][:, v * P:(v + 1) * P], cs[t % 2][:, v * P:(v + 1) * P], ident)
                    ins.then_inc(sem("c_turned"), 1)
                    pe.wait_ge(sem("c_turn_kept"), t + 1)
                    if t >= 1:
                        pe.wait_ge(sem("c_kept"), t)
                    for v in range(NKV):
                        ins = pe.matmul(bank[5][:, v * 256:(v + 1) * 256], csT[t % 2][:, v * P:(v + 1) * P], VB[:, v, :],
                                        start=True, stop=True)
                    ins.then_inc(sem("c_valued"), 1)

            @block.scalar
            def _(act):
                act.wait_ge(sem("s_shifted"), 1)
                act.activation(ss[:, :, 0:NC], ss[:, :, 0:NC], ACT.Exp).then_inc(sem("s_exp"), 1)
                act.wait_ge(sem("s_turned"), 1)
                act.activation(ssT, bank[4][:, 0:256].rearrange("p (a r) -> p a r", a=4), ACT.Copy
                               ).then_inc(sem("s_turn_kept"), 1)
                for t in range(NT):
                    act.wait_ge(sem("c_shifted"), t + 1)
                    act.activation(cs[t % 2], cs[t % 2], ACT.Exp).then_inc(sem("c_exp"), 1)
                    act.wait_ge(sem("c_turned"), t + 1)
                    act.activation(csT[t % 2], bank[4][:, 0:256], ACT.Copy).then_inc(sem("c_turn_kept"), 1)

            @block.vector
            def _(dve):
                step(dve, dve.memset(QD, 0.0), "dve_done")
                step(dve, dve.memset(DMk, 0.0), "dve_done")
                dve.memset(ss[:, :, NC:NCS], 0.0)
                for k, q in enumerate((QN, QT)):
                    for v in range(NKV):
                        rr = slice(v * HD, (v + 1) * HD)
                        ins = dve.tensor_copy(
                            QD[rr, k, :, v * NG * DT:(v + 1) * NG * DT].rearrange("p b (g t) -> p b g t", g=NG),
                            q[rr, :, SEQ:N].rearrange("p g (b t) -> p b g t", b=NB))
                    ins.then_inc(sem("qd_made"), 1)
                dve.wait_ge(sem("s_scored"), 1)
                sc = bank[4][0:NS, :].rearrange("p (b c) -> p b c", b=NB)
                step(dve, dve.tensor_reduce(sm[:, 0:8], sc[:, :, 0:NC], AX, ALU.max, negate=True), "dve_done")
                dve.tensor_tensor(ss[:, :, 0:NC], sc[:, :, 0:NC], bc(sm[:, 0:8], NC), ALU.add).then_inc(sem("s_shifted"), 1)
                dve.wait_ge(sem("s_exp"), 1)
                step(dve, dve.tensor_reduce(sm[:, 8:16], ss[:, :, 0:NC], AX, ALU.add), "dve_done")
                step(dve, dve.reciprocal(sm[:, 16:24], sm[:, 8:16]), "dve_done")
                dve.tensor_tensor(ss[:, :, 0:NC], ss[:, :, 0:NC], bc(sm[:, 16:24], NC), ALU.mult).then_inc(sem("s_probs"), 1)
                dve.wait_ge(sem("s_imp"), 1)
                step(dve, dve.tensor_reduce(imp, bank[5][0:NS, :].rearrange("p (b j c) -> p b j c", b=NB, c=4), AX, ALU.add),
                     "dve_done")
                it, vt = imp[:, :, 1:15], val[:, :, 1:15]
                ix = const("blkidx", NS)[:, 1:15].unsqueeze(1).to_broadcast([NS, NB, 14])
                step(dve, dve.tensor_reduce(sm[:, 24:32], it, AX, ALU.min), "dve_done")
                step(dve, dve.tensor_tensor(vt, it, bc(sm[:, 24:32], 14), ALU.is_le), "dve_done")
                step(dve, dve.tensor_tensor(vt, vt, ix, ALU.mult), "dve_done")
                step(dve, dve.tensor_reduce(sm[:, 32:40], vt, AX, ALU.max), "dve_done")
                step(dve, dve.tensor_tensor(vt, ix, bc(sm[:, 32:40], 14), ALU.is_equal), "dve_done")
                dve.tensor_scalar(DMk[:, :, 1:15], vt, NEG, None, ALU.mult)
                dve.wait_ge(sem("s_turn_kept"), 1)
                dve.wait_ge(sem("s_valued"), 1)
                for q in range(2):
                    for v in range(NKV):
                        rr = slice(32 * v, 32 * v + 32)
                        ins = dve.tensor_copy(oS[rr, q::2, 0, :],
                                              bank[6 + q][rr, :].rearrange("p (a c) -> p a c", a=4)[:, :, v * HD:(v + 1) * HD])
                ins.then_inc(sem("s_imp_kept"), 1)
                for t in range(NT):
                    p = cs[t % 2]
                    p3 = p.rearrange("p (h c) -> p h c", h=NH)
                    m = cm[t % 2]
                    neg = const("cmpneg")[:, t * NCP:(t + 1) * NCP].unsqueeze(1)
                    vis = const("cmp01")[:, t * NCP:(t + 1) * NCP].unsqueeze(1)
                    dve.wait_ge(sem("c_scored"), t + 1)
                    if t >= 2:
                        dve.wait_ge(sem("c_turned"), t - 1)
                    for v in range(NKV):
                        dve.tensor_tensor(p3[:, v * NG:(v + 1) * NG, :],
                                          bank[2 * (t % 2) + v][:, 0:P].rearrange("p (g c) -> p g c", g=NG),
                                          neg.to_broadcast([P, NG, NCP]), ALU.add).then_inc(sem("c_read"), 1)
                    dve.wait_ge(sem("c_read"), 2 * t + 2)
                    step(dve, dve.tensor_reduce(m[:, 0:8], p3, AX, ALU.max, negate=True), "dve_done")
                    dve.tensor_tensor(p3, p3, bc(m[:, 0:8], NCP), ALU.add).then_inc(sem("c_shifted"), 1)
                    dve.wait_ge(sem("c_exp"), t + 1)
                    dve.tensor_tensor(p3, p3, vis.to_broadcast([P, NH, NCP]), ALU.mult).then_inc(sem("c_probs"), 1)
                    dve.wait_ge(sem("c_probs"), t + 1)
                    step(dve, dve.tensor_reduce(m[:, 8:16], p3, AX, ALU.add), "dve_done")
                    step(dve, dve.tensor_scalar(m[:, 8:16], m[:, 8:16], 1e-30, None, ALU.max), "dve_done")
                    step(dve, dve.reciprocal(m[:, 16:24], m[:, 8:16]), "dve_done")
                    step(dve, dve.tensor_tensor(m[:, 16:24], m[:, 16:24],
                                                gate[:, t, :].rearrange("p (h b) -> p h b", b=3)[:, :, 0], ALU.mult), "dve_done")
                    dve.wait_ge(sem("c_valued"), t + 1)
                    dve.tensor_tensor(otm.rearrange("p (h d) -> p h d", d=HD),
                                      bank[5][:, :].rearrange("p (h d) -> p h d", d=HD), bc(m[:, 16:24], HD), ALU.mult
                                      ).then_inc(sem("c_kept"), 1)
                    dve.wait_ge(sem("c_kept"), t + 1)
                    step(dve, dve.tensor_tensor(o_tok[:, t, :], o_tok[:, t, :], otm, ALU.add), "dve_done")

        cut = region(R_ATT)
        pastKV = [cut(NPG * 256).rearrange("p (j c) -> p j c", j=NPG) for _ in range(2)]
        winKV = [cut(4 * 256).rearrange("p (j c) -> p j c", j=4) for _ in range(2)]
        kTb = [cut(1536) for _ in range(2)]
        Sb = [cut(1664)[0:NS] for _ in range(2)]
        cut = region(R_HI + TT * 512)
        PTb = [cut(14 * NS).rearrange("p (j r) -> p j r", j=14) for _ in range(2)]
        srs = cut(64)[0:NS]
        NSLC = PAST + NS
        PARTS = [j * P for j in range(8)] + [NSLC + j * P for j in range(4)]

        with nc.Block() as block:
            @block.sync
            def _(sp):
                for b in range(NB):
                    if b >= 2:
                        sp.wait_ge(sem("b_valued"), b - 1)
                    for j in range(NPG):
                        pg = sp.value_load(pages[0:1, NPG * b + j:NPG * b + j + 1], min_val=0, max_val=NPOOL - 1)
                        sp.dma_start(pastKV[b % 2][:, j, :],
                                     cache_nsa_kv[bass.ds(l, 1), bass.ds(pg, 1), :, 2:4].rearrange(
                                         "o q r k v d -> (o q r) (k v d)")).then_inc(sem(f"past_loaded{b % 2}"), 16)
                    sp.dma_start(winKV[b % 2], cache_win_kv[bass.ds(l, 1), b].rearrange(
                        "o (j p) k v d -> p (o j) (k v d)", p=P)).then_inc(sem(f"past_loaded{b % 2}"), 16)
                sp.wait_ge(sem("oS_done"), NB)
                for h in range(NH):
                    sp.dma_start(scratch.rearrange("b t h c -> t b h c")[:, :, h, :],
                                 oS[h * DT:(h + 1) * DT].rearrange("p b c d -> p b (c d)")).then_inc(sem("oS_stored"), 16)
                sp.wait_ge(sem("oS_stored"), 16 * NH)
                sp.dma_start(o3, scratch.rearrange("b t h c -> (b t) (h c)")).then_inc(sem("o3_loaded"), 16)

            def past_count(b):
                return 16 * (NPG + 1) * (b // 2 + 1)

            @block.tensor
            def _(pe):
                def turn_keys(b):
                    pe.wait_ge(sem(f"past_loaded{b % 2}"), past_count(b))
                    for i in range(3):
                        if b >= 1:
                            pe.wait_ge(sem("k_kept_act" if i != 1 else "k_kept_dve"), [2 * b - 1, b, 2 * b][i])
                        for j in range(4):
                            n = 4 * i + j
                            src = pastKV[b % 2][:, n, 0:P] if n < 8 else winKV[b % 2][:, n - 8, 0:P]
                            ins = pe.transpose(bank[i][:, j * P:(j + 1) * P], src, ident)
                        ins.then_inc(sem("k_turned"), 1)

                def scores(b):
                    pe.wait_ge(sem("k_kept_act"), 2 * b + 2)
                    pe.wait_ge(sem("k_kept_dve"), b + 1)
                    if b >= 1:
                        pe.wait_ge(sem("oS_done"), b)
                        pe.wait_ge(sem("pT_kept"), 3 * b)
                    q = QD[:, 1, b, :]
                    for i in range(3):
                        pe.matmul(bank[3 + i][0:NS, :], q, kTb[b % 2][:, i * 512:(i + 1) * 512], start=True, stop=True)
                    for i in range(2):
                        ins = pe.matmul(bank[6][0:NS, i * NS:(i + 1) * NS], q, KT[:, i, SEQ:N], start=True, stop=True)
                    ins.then_inc(sem("b_scored"), 1)

                def turn_probs(b):
                    pe.wait_ge(sem("b_probs"), 2 * b + 2)
                    if b >= 1:
                        pe.wait_ge(sem("pT_kept"), 3 * b)
                    for j in range(8):
                        ins = pe.transpose(bank[7][:, j * NS:(j + 1) * NS], Sb[b % 2][:, PARTS[j]:PARTS[j] + P],
                                           ident[0:NS, 0:NS])
                    ins.then_inc(sem("p_turned"), 1)
                    for j in range(8, 12):
                        ins = pe.transpose(bank[6][:, (j - 8) * NS:(j - 7) * NS], Sb[b % 2][:, PARTS[j]:PARTS[j] + P],
                                           ident[0:NS, 0:NS])
                    for i, o in enumerate((PAST, NSLC + WINB)):
                        ins = pe.transpose(bank[6][0:NS, (4 + i) * NS:(5 + i) * NS], Sb[b % 2][:, o:o + NS],
                                           ident[0:NS, 0:NS])
                    ins.then_inc(sem("p_turned"), 1)

                def values(b):
                    pe.wait_ge(sem("pT_kept"), 3 * b + 3)
                    o = bank[3][0:NS, 0:256]
                    for i, (js, V, new) in enumerate(((range(8), pastKV, 12), (range(8, 12), winKV, 13))):
                        oi = o[:, i * P:(i + 1) * P]
                        for j in js:
                            pe.matmul(oi, PTb[b % 2][:, j, :], V[b % 2][:, j - js[0], P:256], start=(j == js[0]), stop=False)
                        ins = pe.matmul(oi, PTb[b % 2][0:NS, new, :], vtok[i][0:NS, NT, :], start=False, stop=True)
                    ins.then_inc(sem("b_valued"), 1)

                turn_keys(0)
                for b in range(NB):
                    scores(b)
                    if b + 1 < NB:
                        turn_keys(b + 1)
                    turn_probs(b)
                    values(b)

            @block.scalar
            def _(act):
                def keep_keys(b):
                    for i in (0, 2):
                        act.wait_ge(sem("k_turned"), 3 * b + i + 1)
                        if b >= 2:
                            act.wait_ge(sem("b_scored"), b - 1)
                        act.activation(kTb[b % 2][:, i * 512:(i + 1) * 512], bank[i][:, :], ACT.Copy
                                       ).then_inc(sem("k_kept_act"), 1)

                keep_keys(0)
                for b in range(NB):
                    if b + 1 < NB:
                        keep_keys(b + 1)
                    for i, (lo, hi) in enumerate(((0, NSLC), (NSLC, 1664))):
                        act.wait_ge(sem("b_maxed"), 2 * b + i + 1)
                        act.activation(Sb[b % 2][:, lo:hi], Sb[b % 2][:, lo:hi], ACT.Exp, bias=srs[:, 2 * b + i:2 * b + i + 1],
                                       accum_out=srs[:, 16 + 2 * b + i:17 + 2 * b + i]).then_inc(sem("b_probs"), 1)
                    act.wait_ge(sem("p_turned"), 2 * b + 1)
                    if b >= 2:
                        act.wait_ge(sem("b_valued"), b - 1)
                    act.activation(PTb[b % 2][:, 0:8, :], bank[7][:, :].rearrange("p (j r) -> p j r", j=8), ACT.Copy
                                   ).then_inc(sem("pT_kept"), 1)
                    act.wait_ge(sem("p_turned"), 2 * b + 2)
                    act.activation(PTb[b % 2][:, 8:12, :], bank[6][:, 0:256].rearrange("p (j r) -> p j r", j=4), ACT.Copy
                                   ).then_inc(sem("pT_kept"), 1)
                    act.activation(PTb[b % 2][0:NS, 12:14, :], bank[6][0:NS, 256:384].rearrange("p (j r) -> p j r", j=2),
                                   ACT.Copy).then_inc(sem("pT_kept"), 1)

            @block.vector
            def _(dve):
                def keep_keys(b):
                    dve.wait_ge(sem("k_turned"), 3 * b + 2)
                    if b >= 2:
                        dve.wait_ge(sem("b_scored"), b - 1)
                    dve.tensor_copy(kTb[b % 2][:, 512:1024], bank[1][:, :]).then_inc(sem("k_kept_dve"), 1)

                keep_keys(0)
                for b in range(NB):
                    s = Sb[b % 2]
                    new = const("newneg", NS)[:, b * NS:(b + 1) * NS]
                    dve.wait_ge(sem("b_scored"), b + 1)
                    if b >= 2:
                        dve.wait_ge(sem("p_turned"), 2 * (b - 1))
                    for i in range(2):
                        dve.tensor_tensor(s[:, i * 512:(i + 1) * 512].rearrange("p (j c) -> p j c", c=64),
                                          bank[3 + i][0:NS, :].rearrange("p (j c) -> p j c", c=64),
                                          bc(DMk[:, b, 8 * i:8 * i + 8], 64), ALU.add)
                    step(dve, dve.tensor_tensor(s[:, PAST:NSLC], bank[6][0:NS, 0:NS], new, ALU.add), "dve_done")
                    dve.tensor_reduce(srs[:, 2 * b:2 * b + 1], s[:, 0:NSLC], AX, ALU.max, negate=True
                                      ).then_inc(sem("b_maxed"), 1)
                    dve.tensor_tensor(s[:, NSLC:NSLC + DT], bank[5][0:NS, 0:DT], const("winneg", NS), ALU.add)
                    dve.tensor_copy(s[:, NSLC + DT:NSLC + WINB], bank[5][0:NS, DT:WINB])
                    step(dve, dve.tensor_tensor(s[:, NSLC + WINB:1664], bank[6][0:NS, NS:2 * NS], new, ALU.add), "dve_done")
                    dve.tensor_reduce(srs[:, 2 * b + 1:2 * b + 2], s[:, NSLC:1664], AX, ALU.max, negate=True
                                      ).then_inc(sem("b_maxed"), 1)
                    if b + 1 < NB:
                        keep_keys(b + 1)
                    dve.wait_ge(sem("b_probs"), 2 * b + 2)
                    step(dve, dve.reciprocal(srs[:, 32 + 2 * b:34 + 2 * b], srs[:, 16 + 2 * b:18 + 2 * b]), "dve_done")
                    dve.wait_ge(sem("b_valued"), b + 1)
                    for v in range(NKV):
                        rr = slice(32 * v, 32 * v + 32)
                        ins = dve.tensor_tensor(oS[rr, b, 1:3, :],
                                                bank[3][rr, 0:256].rearrange("p (i c) -> p i c", i=2)[:, :, v * HD:(v + 1) * HD],
                                                bc(srs[rr, 32 + 2 * b:34 + 2 * b], HD), ALU.mult)
                    ins.then_inc(sem("oS_done"), 1)
                dve.wait_ge(sem("o3_loaded"), 16)
                o4 = o3.rearrange("p (h b d) -> p h b d", h=NH, b=3)
                step(dve, dve.tensor_tensor(o3.rearrange("p (n d) -> p n d", d=HD), o3.rearrange("p (n d) -> p n d", d=HD),
                                            bc(gate[0:NS, NT, :], HD), ALU.mult), "dve_done")
                dst = o_tok[0:NS, NT, :].rearrange("p (h d) -> p h d", h=NH)
                step(dve, dve.tensor_tensor(dst, o4[:, :, 0, :], o4[:, :, 1, :], ALU.add), "dve_done")
                step(dve, dve.tensor_tensor(dst, dst, o4[:, :, 2, :], ALU.add), "dve_done")

        U = R_[:, 0:FFC * N].rearrange("p (f n) -> p f n", f=FFC)
        MU = ([("out", m, s) for m in range(KC) for s in range(2)] + [("up", f, s) for f in range(FFC) for s in range(2)]
              + [("down", m, s) for m in range(KC) for s in range(2)])
        NOUT = 2 * KC

        def halves(s):
            return slice(s * HALF, (s + 1) * HALF)

        with nc.Block() as block:
            @block.sync
            def _(sp):
                for i in range(11, 27):
                    load_weight(sp, l, i)

            @block.tensor
            def _(pe):
                for t in range(TT):
                    r = rows_of(t)
                    for c in range(4):
                        ins = pe.transpose(bank[2 + t][:, c * r:(c + 1) * r], o_tok[0:r, t, c * P:(c + 1) * P],
                                           ident[0:r, 0:r])
                    ins.then_inc(sem("o_turned"), 1)
                pe.wait_ge(sem("o_turn_kept"), TT)
                for u, (kind, m, s) in enumerate(MU):
                    if u == NOUT:
                        norm_products(pe, "n2")
                        pe.wait_ge(sem("n2_out"), KC)
                    if u == NOUT + 2 * FFC:
                        pe.wait_ge(sem("squared"), 2 * FFC)
                    i = {"out": 9 + m // 4, "up": 11 + m // 4, "down": 19 + m}[kind]
                    w = slot_ready(pe, i) if s == 0 else w
                    if u >= 6:
                        pe.wait_ge(sem("mu_kept"), u - 5)
                    n, src = {"out": (KC, OT), "up": (KC, HT), "down": (FFC, U)}[kind]
                    for c in range(n):
                        wc = w[:, c, :] if kind == "down" else w[:, c, (m % 4) * P:(m % 4 + 1) * P]
                        ins = pe.matmul(bank[2 + u % 6][:, 0:HALF], wc, src[:, c, halves(s)], start=(c == 0), stop=(c == n - 1))
                    ins.then_inc(sem("mu_done"), 1)
                    if s == 1 and (kind == "down" or m % 4 == 3):
                        pe.wait_ge(sem("mu_done"), u + 1)
                        pe.sem_inc(sem("slot_used"), 1)

            @block.scalar
            def _(act):
                for t in range(0, TT):
                    r = rows_of(t)
                    act.wait_ge(sem("o_turned"), t + 1)
                    act.activation(OT[:, 0:4, t * P:t * P + r], bank[2 + t][:, 0:4 * r].rearrange("p (c n) -> p c n", c=4),
                                   ACT.Copy).then_inc(sem("o_turn_kept"), 1)
                norm_scalar(act, "n2", "mu_kept")
                for u in range(NOUT, NOUT + 2 * FFC):
                    kind, f, s = MU[u]
                    act.wait_ge(sem("mu_done"), u + 1)
                    act.activation(U[:, f, halves(s)], bank[2 + u % 6][:, 0:HALF], ACT.Relu).then_inc(sem("mu_kept"), 1)

            @block.vector
            def _(dve):
                for u, (kind, m, s) in enumerate(MU):
                    if u == NOUT:
                        norm_vector(dve, "n2", G_MLP)
                    if kind == "up":
                        dve.wait_ge(sem("mu_kept"), u + 1)
                        x = U[:, m, halves(s)]
                        dve.tensor_tensor(x, x, x, ALU.mult).then_inc(sem("squared"), 1)
                    else:
                        dve.wait_ge(sem("mu_done"), u + 1)
                        x = XT[:, m, halves(s)]
                        dve.tensor_tensor(x, x, bank[2 + u % 6][:, 0:HALF], ALU.add).then_inc(sem("mu_kept"), 1)

        clear_semaphores()
        layers.close()

        YU = [(t, q) for t in range(TT) for q in range(2)]
        Y = [W[0][:, :].rearrange("p (t c) -> p t c", t=NT), W[1][:, 0:DM].rearrange("p (t c) -> p t c", t=1)]
        with nc.Block() as block:
            @block.tensor
            def _(pe):
                for u, (t, q) in enumerate(YU):
                    r = rows_of(t)
                    if u >= 8:
                        pe.wait_ge(sem("y_kept"), u - 7)
                    for c in range(4):
                        ins = pe.transpose(bank[u % 8][0:r, c * P:(c + 1) * P], XT[:, 4 * q + c, t * P:t * P + r], ident)
                    ins.then_inc(sem("y_turned"), 1)

            @block.vector
            def _(dve):
                for u, (t, q) in enumerate(YU):
                    r = rows_of(t)
                    dve.wait_ge(sem("y_turned"), u + 1)
                    dst = (Y[0][:, t] if t < NT else Y[1][0:NS, 0])[:, q * 512:(q + 1) * 512]
                    dve.tensor_copy(dst, bank[u % 8][0:r, :]).then_inc(sem("y_kept"), 1)

            @block.sync
            def _(sp):
                for t in range(NT):
                    sp.wait_ge(sem("y_kept"), 2 * t + 2)
                    sp.dma_start(y_prompt[0, t * P:(t + 1) * P, :], Y[0][:, t]).then_inc(sem("y_stored"), 16)
                sp.wait_ge(sem("y_kept"), 2 * TT)
                sp.dma_start(y_sample.rearrange("b t c -> (b t) c"), Y[1][0:NS, 0]).then_inc(sem("y_stored"), 16)
                sp.wait_ge(sem("y_stored"), 16 * TT)


_INS = ['x_prompt', 'x_sample', 'cache_nsa_kv', 'cache_win_kv', 'state_hgrn', 'page_table', 'attn_norm_g', 'w_in',
        'q_norm_g', 'k_norm_g', 'cmp_pos', 'cmp_w1', 'cmp_b1', 'cmp_w2', 'hg_lb_param', 'hg_norm_g', 'w_out',
        'mlp_norm_g', 'w_up', 'w_down']
_OUTS = [(1, SEQ, DM), (NB, DT, DM), (DEPTH, 1, SEQ, 4, NKV, HD), (DEPTH, 1, SEQ, 2, NKV, HD),
         (DEPTH, 1, HH, P, P), (DEPTH, NB, DT, 4, NKV, HD), (DEPTH, NB, DT, 2, NKV, HD), (DEPTH, NB, HH, P, P)]


def kernel(**inputs):
    import concourse.bacc as bacc
    from concourse.bass_utils import run_bass_kernel_spmd

    nc = bacc.Bacc("TRN2", target_bir_lowering=False, num_devices=1)
    arrays, args = {}, []
    for name in _INS + ['constants']:
        a = CONSTANTS if name == 'constants' else np.ascontiguousarray(inputs[name])
        arrays[f"in_{name}"] = a
        args.append(nc.dram_tensor(f"in_{name}", a.shape, mybir.dt.from_np(a.dtype), kind="ExternalInput").ap())
    for i, shape in enumerate(_OUTS):
        args.append(nc.dram_tensor(f"out_{i}", shape, F32, kind="ExternalOutput").ap())
    build(nc, *args)
    r = run_bass_kernel_spmd(nc, [arrays], core_ids=[0])
    return tuple(r.results[0][f"out_{i}"] for i in range(len(_OUTS)))
```

```python
from contextlib import ExitStack

import numpy as np

import concourse.bass as bass
from concourse import mybir

F32 = mybir.dt.float32
F32R = mybir.dt.float32r
I32 = mybir.dt.int32
U32 = mybir.dt.uint32
ALU = mybir.AluOpType
ACT = mybir.ActivationFunctionType
AX = mybir.AxisListType.X

P = 128
DM = 1024
KC = DM // P
SEQ = 512
NB = 8
DT = 8
NS = NB * DT
N = SEQ + NS
HALF = N // 2
NT = SEQ // P
TT = NT + 1
DEPTH = 2
HD = 64
NH = 8
NKV = 2
NG = NH // NKV
PAST = 1024
PAGE = 128
NPG = PAST // PAGE
HH = 4
CH = 32
NCK = P // CH
WINB = 512
DFF = 4096
FFC = DFF // P
CST = 16
CHID = 256
NCP = SEQ // CST
NCS = PAST // CST
NCC = NB * NCS
NCALL = NCC + NCP
SLOT = 4096
EPS = 1e-6
NEG = -1e30
C_Q, C_KV, C_WIN, C_HQ, C_HF, C_HI, C_HG, C_END = 0, 512, 1024, 1304, 1816, 2328, 2840, 3352
WINW = C_HQ - C_WIN

CONST_W = {}


def _constants():
    cols = []

    def put(name, a):
        a = np.asarray(a, np.float32).reshape(a.shape[0], -1)
        full = np.zeros((P, a.shape[1]), np.float32)
        full[:a.shape[0]] = a
        CONST_W[name] = (sum(c.shape[1] for c in cols), a.shape[1])
        cols.append(full)

    i = np.arange(P)
    put("ident", np.eye(P))
    put("ones", np.ones((P, P)))
    put("ones64", (i[:, None] // HD == i[None] // HD))
    put("causal", np.where(i[None] > i[:, None], NEG, 0.0))
    put("hgmask", (i[:, None] // CH == i[None] // CH) & (i[:, None] <= i[None]))
    j = np.arange(NS)
    put("hgmask8", (j[:, None] // DT == j[None] // DT) & (j[:, None] <= j[None]))
    pos = np.concatenate([np.arange(SEQ), PAST + np.tile(np.arange(DT), NB), np.zeros(P - NS)]).astype(np.float32)
    inv = (np.float32(10000.0) ** (-np.arange(HD // 2, dtype=np.float32) / np.float32(HD // 2))).astype(np.float32)
    ang = (pos[:, None] * inv[None]).astype(np.float32).reshape(TT, P, HD // 2).transpose(1, 0, 2)
    put("cos", np.cos(ang.astype(np.float64)))
    put("sin", np.sin(ang.astype(np.float64)))
    c = np.arange(NCP)
    q = np.arange(SEQ).reshape(NT, P).T
    seen = (c[None, None] * CST + 2 * CST - 1 <= q[:, :, None]) & (c < NCP - 1)
    put("cmpneg", np.where(seen, 0.0, NEG))
    put("cmp01", seen)
    rows = np.arange(NH * DT)
    t = rows % DT
    same = (np.arange(NB)[None, :, None, None] == np.arange(NB)[None, None, :, None])
    new = same & (np.arange(DT)[None, None, None] <= t[:, None, None, None])
    put("newneg", np.where(new, 0.0, NEG))
    put("winneg", np.where(np.arange(DT)[None] > t[:, None], 0.0, NEG))
    put("groupsum", (rows[:, None] // (NG * DT) == rows[None] // (NG * DT)) & (t[:, None] == t[None]))
    put("blkidx", np.tile(np.arange(16), (P, 1)))
    put("chunk", (i[:, None] // CH == np.arange(NCK)[None]))
    put("batch", (j[:, None] // DT == np.arange(NB)[None]))
    n = np.arange(N)
    put("scan", np.tile(np.where(n < SEQ, n % CH != 0, (n - SEQ) % DT != 0), (P, 1)))
    return np.concatenate(cols, axis=1)


CONSTANTS = _constants()


def rows_of(t):
    return P if t < NT else NS


def build(nc, x_prompt, x_sample, cache_nsa_kv, cache_win_kv, state_hgrn, page_table,
          attn_norm_g, w_in, q_norm_g, k_norm_g, cmp_pos, cmp_w1, cmp_b1, cmp_w2,
          hg_lb_param, hg_norm_g, w_out, mlp_norm_g, w_up, w_down, constants,
          y_prompt, y_sample, p_nsa, p_win, p_hg, s_nsa, s_win, s_hg):
    NPOOL = cache_nsa_kv.shape[1]
    with ExitStack() as ctx:
        def sb(name, cols, dt=F32):
            return ctx.enter_context(nc.sbuf_tensor(name, [P, cols], dt))

        scratch = nc.dram_tensor("branches", [NB, DT, NH, 3 * HD], F32, kind="Internal").ap()
        sems = {}

        def sem(name):
            if name not in sems:
                sems[name] = ctx.enter_context(nc.semaphore(name))
            return sems[name]

        made = {}

        def step(eng, ins, name):
            made[name] = made.get(name, 0) + 1
            ins.then_inc(sem(name), 1)
            eng.wait_ge(sem(name), made[name])

        cst = sb("cst", CONSTANTS.shape[1])
        pages = ctx.enter_context(nc.sbuf_tensor("pages", [1, NB * NPG], I32))
        XT = sb("XT", KC * N)[:, :].rearrange("p (c n) -> p c n", c=KC)
        OT_ = sb("OT", KC * N)
        OT = OT_[:, :].rearrange("p (c n) -> p c n", c=KC)
        rstd = sb("rstd", N)
        par_all = sb("par_all", DEPTH * 40)[:, :].rearrange("p (l c) -> p l c", l=DEPTH)
        par = sb("par", 40)
        qkr = sb("qkr", 60)
        lbt = sb("lbt", 40)
        eps = sb("epsc", 1)[:, 0:1]
        one = sb("onec", 1)[:, 0:1]
        gain = sb("gain", 3 * HD)
        bank = [ctx.enter_context(nc.psum_tensor(f"bank{i}", [P, 512], F32)) for i in range(8)]

        def cutter(tensor, start=0):
            at = [start]

            def cut(n):
                at[0] += n
                assert at[0] <= tensor.shape[1], at
                return tensor[:, at[0] - n:at[0]]
            return cut

        def const(name, rows=P):
            o, w = CONST_W[name]
            return cst[0:rows, o:o + w]

        ident, ones, ones64 = const("ident"), const("ones"), const("ones64")
        G_ATTN, G_MLP, G_HG, G_KC, P_B1, P_LBA, P_OM, P_LNOM, P_HB = 0, 8, 16, 17, 18, 22, 26, 30, 34

        def col(i):
            return par[:, i:i + 1]

        def bc(ap, n):
            return ap.unsqueeze(2).to_broadcast([ap.shape[0], ap.shape[1], n])

        P_LB, NROW = P_LBA, P_LBA + HH
        setup_scope = ExitStack()
        xin = [setup_scope.enter_context(nc.sbuf_tensor(f"xin{i}", [P, SLOT], F32)) for i in range(2)]
        rows = OT_[0:DEPTH * NROW, 0:P]

        with nc.Block() as block:
            @block.sync
            def _(sp):
                sp.dma_start(xin[0][:, :].rearrange("p (t c) -> p t c", t=NT),
                             x_prompt[0].rearrange("(t p) c -> p t c", p=P)).then_inc(sem("x_loaded"), 16)
                sp.dma_start(xin[1][0:NS, 0:DM], x_sample.rearrange("b t c -> (b t) c")).then_inc(sem("x_loaded"), 16)
                sp.dma_start(cst[:, :], constants).then_inc(sem("const_loaded"), 16)
                sp.dma_start(pages[:, :], page_table.rearrange("(o a) b -> o (a b)", o=1)).then_inc(sem("pages_loaded"), 16)
                sp.wait_ge(sem("pages_loaded"), 16)

            @block.scalar
            def _(act):
                for l in range(DEPTH):
                    r = l * NROW
                    for src, w, c0 in ((attn_norm_g[l].rearrange("(c p) -> c p", p=P), KC, G_ATTN),
                                       (mlp_norm_g[l].rearrange("(c p) -> c p", p=P), KC, G_MLP),
                                       (hg_norm_g[l].rearrange("(c p) -> c p", p=P), 1, G_HG),
                                       (cmp_b1[l].rearrange("k (c p) -> (k c) p", p=P), 4, P_B1),
                                       (hg_lb_param[l].rearrange("(c p) -> c p", p=P), HH, P_LB)):
                        act.dma_start(rows[r + c0:r + c0 + w, :], src).then_inc(sem("rows_loaded"), 16)
                    for kv in range(NKV):
                        act.dma_start(rows[r + G_KC:r + G_KC + 1, kv * HD:(kv + 1) * HD], k_norm_g[l, 0:1, :]
                                      ).then_inc(sem("rows_loaded"), 16)
                act.wait_ge(sem("lb_centred"), 1)
                act.activation(lbt[:, 16:24], lbt[:, 16:24], ACT.Exp).then_inc(sem("lb_exp"), 1)
                act.wait_ge(sem("lb_ready"), 1)
                act.activation(lbt[:, 32:40], lbt[:, 32:40], ACT.Ln).then_inc(sem("lb_ln"), 1)

            @block.tensor
            def _(pe):
                pe.wait_ge(sem("const_loaded"), 16)
                pe.wait_ge(sem("x_loaded"), 32)
                for c in range(KC):
                    for t in range(NT):
                        ins = pe.transpose(bank[c % 4][:, t * P:(t + 1) * P], xin[0][:, t * DM + c * P:t * DM + (c + 1) * P],
                                           ident)
                    ins.then_inc(sem("x_turned"), 1)
                    if c >= 3 and c < KC - 1:
                        pe.wait_ge(sem("x_kept"), c - 2)
                for c in range(KC):
                    ins = pe.transpose(bank[4][:, c * NS:(c + 1) * NS], xin[1][0:NS, c * P:(c + 1) * P], ident[0:NS, 0:NS])
                ins.then_inc(sem("x_turned"), 1)
                pe.wait_ge(sem("rows_loaded"), 16 * 7 * DEPTH)
                pe.transpose(bank[5][:, 0:DEPTH * NROW], rows, ident[0:DEPTH * NROW, 0:DEPTH * NROW]
                             ).then_inc(sem("rows_turned"), 1)

            @block.vector
            def _(dve):
                dve.memset(eps, EPS)
                dve.memset(one, 1.0)
                dve.memset(par_all[:, :, P_HB:40], 0.0).then_inc(sem("cleared"), 1)
                for c in range(KC):
                    dve.wait_ge(sem("x_turned"), c + 1)
                    dve.tensor_copy(XT[:, c, 0:SEQ], bank[c % 4][:, :]).then_inc(sem("x_kept"), 1)
                dve.wait_ge(sem("x_turned"), KC + 1)
                dve.tensor_copy(XT[:, :, SEQ:N], bank[4][:, :].rearrange("p (c n) -> p c n", c=KC)
                                ).then_inc(sem("x_kept"), 1)
                dve.wait_ge(sem("rows_turned"), 1)
                turned = bank[5][:, 0:DEPTH * NROW].rearrange("p (l c) -> p l c", l=DEPTH)
                dve.tensor_copy(par_all[:, :, 0:P_LB], turned[:, :, 0:P_LB])
                step(dve, dve.tensor_copy(lbt[:, 0:8].rearrange("p (l c) -> p l c", l=DEPTH), turned[:, :, P_LB:NROW]),
                     "dve_done")
                step(dve, dve.tensor_tensor(lbt[:, 8:12], lbt[:, 0:4], lbt[:, 4:8], ALU.max), "dve_done")
                step(dve, dve.tensor_tensor(lbt[:, 16:20], lbt[:, 0:4], lbt[:, 8:12], ALU.subtract), "dve_done")
                step(dve, dve.tensor_tensor(lbt[:, 20:24], lbt[:, 4:8], lbt[:, 8:12], ALU.subtract), "lb_centred")
                dve.wait_ge(sem("lb_exp"), 1)
                step(dve, dve.tensor_tensor(lbt[:, 8:12], lbt[:, 16:20], lbt[:, 20:24], ALU.add), "dve_done")
                step(dve, dve.reciprocal(lbt[:, 12:16], lbt[:, 8:12]), "dve_done")
                step(dve, dve.tensor_tensor(lbt[:, 16:20], lbt[:, 16:20], lbt[:, 12:16], ALU.mult), "dve_done")
                step(dve, dve.tensor_tensor(lbt[:, 20:24], lbt[:, 20:24], lbt[:, 12:16], ALU.mult), "dve_done")
                step(dve, dve.tensor_tensor(lbt[:, 24:28], lbt[:, 16:20], lbt[:, 20:24], ALU.add), "dve_done")
                step(dve, dve.tensor_tensor(lbt[:, 24:28], lbt[:, 24:28], lbt[:, 16:20], ALU.subtract), "dve_done")
                step(dve, dve.tensor_scalar(lbt[:, 28:32], lbt[:, 24:28], -1.0, 1.0, ALU.mult, ALU.add), "dve_done")
                step(dve, dve.tensor_scalar(lbt[:, 32:36], lbt[:, 24:28], 1e-15, None, ALU.max), "dve_done")
                step(dve, dve.tensor_scalar(lbt[:, 36:40], lbt[:, 28:32], 1e-15, None, ALU.max), "lb_ready")
                dve.wait_ge(sem("lb_ln"), 1)
                for src, ln in ((24, 32), (28, 36)):
                    step(dve, dve.tensor_scalar(lbt[:, 8:12], lbt[:, src:src + 4], 1e-15, NEG, ALU.is_lt, ALU.mult),
                         "dve_done")
                    step(dve, dve.tensor_tensor(lbt[:, ln:ln + 4], lbt[:, ln:ln + 4], lbt[:, 8:12], ALU.add), "dve_done")
                dve.tensor_copy(par_all[:, 1, P_LBA:P_LBA + 4], lbt[:, 32:36])
                dve.tensor_copy(par_all[:, 1, P_OM:P_OM + 4], lbt[:, 28:32])
                dve.tensor_copy(par_all[:, 1, P_LNOM:P_LNOM + 4], lbt[:, 36:40])
                dve.memset(par_all[:, 0, P_LBA:P_LBA + 4], NEG)
                dve.memset(par_all[:, 0, P_OM:P_OM + 4], 1.0)
                dve.memset(par_all[:, 0, P_LNOM:P_LNOM + 4], 0.0)

        setup_scope.close()

        GW = 256

        class Split:

            def __init__(self, scope, name):
                def tile(n, cols, dt):
                    return scope.enter_context(nc.sbuf_tensor(name + n, [P, cols], dt))
                self.name = name
                self.raw = [tile(f"raw{i}", KC * GW, F32) for i in range(2)]
                self.wh = [tile(f"wh{i}", KC * GW, F32R) for i in range(2)]
                self.wl = [tile(f"wl{i}", KC * GW, F32R) for i in range(2)]
                self.ah = tile("ah", KC * N, F32R)[:, :].rearrange("p (c n) -> p c n", c=KC)
                self.al = tile("al", KC * N, F32R)[:, :].rearrange("p (c n) -> p c n", c=KC)

            def granule(self, tiles, i, w):
                return tiles[i % 2][:, 0:KC * w].rearrange("p (c n) -> p c n", c=KC)

        def load_granule(sp, S, i, src):
            if i >= 2:
                sp.wait_ge(sem(S.name + "w_lo"), i - 1)
            sp.dma_start(S.granule(S.raw, i, src.shape[2]), src).then_inc(sem(S.name + f"w_raw{i % 2}"), 16)

        def split_hi(act, S, i, w, used):
            act.wait_ge(sem(S.name + f"w_raw{i % 2}"), 16 * (i // 2 + 1))
            if i >= 2:
                act.wait_ge(sem(S.name + "done"), used)
            act.activation(S.granule(S.wh, i, w), S.granule(S.raw, i, w), ACT.Copy).then_inc(sem(S.name + "w_hi"), 1)

        def split_lo(pool, S, i, w):
            pool.wait_ge(sem(S.name + "w_hi"), i + 1)
            pool.tensor_tensor(S.granule(S.wl, i, w), S.granule(S.raw, i, w), S.granule(S.wh, i, w).bitcast(F32),
                               ALU.subtract).then_inc(sem(S.name + "w_lo"), 1)

        def feature_product(pe, out, S, i, w, cols, ah, al, n):
            wh, wl = S.granule(S.wh, i, w), S.granule(S.wl, i, w)
            for c in range(KC):
                pe.matmul(out, wh[:, c, cols], ah[:, c, n], start=(c == 0), stop=False)
                pe.matmul(out, wh[:, c, cols], al[:, c, n], start=False, stop=False)
                ins = pe.matmul(out, wl[:, c, cols], ah[:, c, n], start=False, stop=(c == KC - 1))
            return ins

        def halves(s):
            return slice(s * HALF, (s + 1) * HALF)

        def exp_ln_tables(act):
            act.preload_act_table_set("natural_log_exp_and_others")

        def norm_products(pe, name, sq):
            for c in range(KC):
                pe.wait_ge(sem(name + "_squared"), c + 1)
                for s in range(2):
                    ins = pe.matmul(bank[s][:, 0:HALF], ones, sq[c % 2][:, halves(s)], start=(c == 0), stop=(c == KC - 1))
                ins.then_inc(sem(name + "_summed"), 1)

        def norm_scalar(act, name, sq, S, after=None):
            for c in range(KC):
                if after:
                    act.wait_ge(sem(after), 2 * c + 2)
                if c >= 2:
                    act.wait_ge(sem(name + "_summed"), c - 1)
                act.activation(sq[c % 2], XT[:, c, :], ACT.Square).then_inc(sem(name + "_squared"), 1)
            act.wait_ge(sem(name + "_summed"), KC)
            for s in range(2):
                act.activation(rstd[:, halves(s)], bank[s][:, 0:HALF], ACT.Ln, bias=eps, scale=1.0 / DM
                               ).then_inc(sem(name + "_ln"), 1)
            act.wait_ge(sem(name + "_ln"), 2)
            act.activation(rstd[:, :], rstd[:, :], ACT.Exp, scale=-0.5).then_inc(sem(name + "_rstd"), 1)
            for c in range(KC):
                act.wait_ge(sem(name + "_normed"), c + 1)
                act.activation(S.ah[:, c, :], sq[c % 2], ACT.Copy).then_inc(sem(name + "_hi"), 1)

        def norm_vector(dve, name, sq, S, g):
            dve.wait_ge(sem(name + "_rstd"), 1)
            for c in range(KC + 1):
                if c < KC:
                    if c >= 2:
                        dve.wait_ge(sem(name + "_out"), c - 1)
                    dve.scalar_tensor_tensor(sq[c % 2], XT[:, c, :], col(g + c), rstd[:, :], ALU.mult, ALU.mult
                                             ).then_inc(sem(name + "_normed"), 1)
                if c >= 1:
                    dve.wait_ge(sem(name + "_hi"), c)
                    dve.tensor_tensor(S.al[:, c - 1, :], sq[(c - 1) % 2], S.ah[:, c - 1, :].bitcast(F32), ALU.subtract
                                      ).then_inc(sem(name + "_out"), 1)
        def clear_semaphores():
            with nc.Block() as block:
                @block.gpsimd
                def _(pool):
                    for s in sems.values():
                        pool.sem_clear(s)
            made.clear()

        clear_semaphores()
        layers = ctx.enter_context(ExitStack())
        l = layers.enter_context(nc.Fori(0, DEPTH))

        R1_N, R2_N = 18400, 9216
        mix_scope = ExitStack()
        R1 = mix_scope.enter_context(nc.sbuf_tensor("R1", [P, R1_N], F32))
        cut = cutter(R1)
        kv_tok = cut(TT * 512).rearrange("p (t c) -> p t c", t=TT)
        win_tok = cut(TT * WINW).rearrange("p (t c) -> p t c", t=TT)
        R_HI = TT * 512 + TT * WINW
        hi_tok = cut(TT * 512).rearrange("p (t c) -> p t c", t=TT)
        q_tok = cut(TT * 512).rearrange("p (t c) -> p t c", t=TT)
        R_HG = R_HI + 2 * TT * 512
        hq = cut(HH * N).rearrange("p (h n) -> p h n", h=HH)
        hf = cut(HH * N).rearrange("p (h n) -> p h n", h=HH)
        hg = cut(HH * N).rearrange("p (h n) -> p h n", h=HH)
        kd = cut(HH * N).rearrange("p (h n) -> p h n", h=HH)
        dec = cut(HH * 24).rearrange("p (h n) -> p h n", h=HH)
        tmp = [OT_[:, i * N:(i + 1) * N] for i in range(7)]
        sq1 = [kd[:, i, :] for i in range(2)]

        FT = [hf, hq, hg]
        TOK = [(hi_tok, C_HI, GW), (q_tok, C_Q, GW), (kv_tok, C_KV, GW), (win_tok, C_WIN, WINW // 2)]
        G1 = ([(c + j * GW, GW) for c in (C_HF, C_HQ, C_HG) for j in range(2)]
              + [(c + j * w, w) for _, c, w in TOK for j in range(2)])
        NG1F = 6
        NF = NG1F * 4
        NTOK = 8 * TT
        HACT = 16
        PB = 6

        def units_before(i):
            return 4 * i if i <= NG1F else NF + TT * (i - NG1F)

        proj_scope = ExitStack()
        S1 = Split(proj_scope, "p_")

        with nc.Block() as block:
            @block.sync
            def _(sp):
                for i, g in enumerate((q_norm_g[bass.ds(l, 1)], k_norm_g[bass.ds(l, 1), 1], k_norm_g[bass.ds(l, 1), 2])):
                    sp.dma_start(gain[:, i * HD:(i + 1) * HD], g.to_broadcast([P, HD])).then_inc(sem("gain_loaded"), 16)
                for i, (c, w) in enumerate(G1):
                    load_granule(sp, S1, i, w_in[bass.ds(l, 1)].rearrange("o (c p) n -> p (o c) n", p=P)[:, :, c:c + w])

            @block.gpsimd
            def _(pool):
                for i, (c, w) in enumerate(G1):
                    split_lo(pool, S1, i, w)

            @block.tensor
            def _(pe):
                norm_products(pe, "n1", sq1)
                pe.wait_ge(sem("n1_out"), KC)
                for u in range(NF):
                    i, m, s = u // 4, u // 2 % 2, u % 2
                    pe.wait_ge(sem("p_w_lo"), i + 1)
                    if u >= PB:
                        pe.wait_ge(sem("proj_kept"), u - PB + 1)
                    feature_product(pe, bank[2 + u % PB][:, 0:HALF], S1, i, GW, slice(m * P, (m + 1) * P), S1.ah, S1.al,
                                    halves(s)).then_inc(sem("p_done"), 1)
                for n in range(NTOK):
                    u = NF + n
                    i, t = NG1F + n // TT, n % TT
                    w = G1[i][1]
                    pe.wait_ge(sem("p_w_lo"), i + 1)
                    pe.wait_ge(sem("proj_kept"), u - PB + 1)
                    tok = slice(t * P, (t + 1) * P) if t < NT else slice(N - P, N)
                    wh, wl = S1.granule(S1.wh, i, w), S1.granule(S1.wl, i, w)
                    out = bank[2 + u % PB][:, 0:w]
                    for c in range(KC):
                        pe.matmul(out, S1.ah[:, c, tok], wh[:, c, :], start=(c == 0), stop=False)
                        pe.matmul(out, S1.ah[:, c, tok], wl[:, c, :], start=False, stop=False)
                        ins = pe.matmul(out, S1.al[:, c, tok], wh[:, c, :], start=False, stop=(c == KC - 1))
                    ins.then_inc(sem("p_done"), 1)

            @block.scalar
            def _(act):
                exp_ln_tables(act)
                for i in range(2):
                    split_hi(act, S1, i, G1[i][1], 0)
                norm_scalar(act, "n1", sq1, S1)

                def next_hi(i):
                    if i + 2 < len(G1):
                        split_hi(act, S1, i + 2, G1[i + 2][1], units_before(i + 1))

                def keep_features(u):
                    act.wait_ge(sem("p_done"), u + 1)
                    i, m, s = u // 4, u // 2 % 2, u % 2
                    act.activation(FT[i // 2][:, 2 * (i % 2) + m, halves(s)], bank[2 + u % PB][:, 0:HALF], ACT.Copy
                                   ).then_inc(sem("proj_kept"), 1)
                    if u % 4 == 3:
                        next_hi(i)

                def keep_tokens(n):
                    i, t = n // TT, n % TT
                    u = NF + n
                    dst, _, w = TOK[i // 2]
                    j = i % 2
                    r = rows_of(t)
                    act.wait_ge(sem("p_done"), u + 1)
                    src = bank[2 + u % PB][P - r:P, 0:w]
                    if dst is q_tok:
                        out = dst[0:r, t, :].rearrange("p (g v d) -> p g v d", g=NG, v=NKV)[:, :, j]
                        src = src.rearrange("p (g d) -> p g d", g=NG)
                    else:
                        out = dst[0:r, t, j * w:(j + 1) * w]
                    act.activation(out, src, ACT.Copy).then_inc(sem("proj_kept"), 1)
                    if t == TT - 1:
                        next_hi(NG1F + i)

                for u in range(NF):
                    keep_features(u)
                act.wait_ge(sem("proj_kept"), NF)
                for h in range(HH):
                    for n_ in range(10 * h, 10 * h + 2):
                        keep_tokens(n_)
                    act.wait_ge(sem("hg_vec"), 4 * h + 1)
                    n = HACT * h
                    for t in (0, 3, 6):
                        act.activation(tmp[t], tmp[t], ACT.Exp, scale=-1.0).then_inc(sem("hg_act"), 1)
                    act.activation(tmp[1], tmp[1], ACT.Exp, scale=-1.0).then_inc(sem("hg_act"), 1)
                    for k, t in enumerate((0, 3, 6)):
                        act.wait_ge(sem("hg_act"), n + k + 1)
                        act.activation(tmp[t], tmp[t], ACT.Ln, bias=one).then_inc(sem("hg_act"), 1)
                    act.wait_ge(sem("hg_act"), n + 5)
                    act.activation(tmp[2], tmp[0], ACT.Exp, scale=-1.0).then_inc(sem("hg_act"), 1)
                    for n_ in range(10 * h + 2, 10 * h + 4):
                        keep_tokens(n_)
                    act.wait_ge(sem("hg_vec"), 4 * h + 2)
                    act.activation(tmp[0], tmp[0], ACT.Exp).then_inc(sem("hg_act"), 1)
                    act.wait_ge(sem("hg_act"), n + 9)
                    act.activation(tmp[0], tmp[0], ACT.Ln, bias=one).then_inc(sem("hg_act"), 1)
                    act.activation(tmp[3], tmp[3], ACT.Exp).then_inc(sem("hg_act"), 1)
                    act.activation(hg[:, h, :], tmp[6], ACT.Exp).then_inc(sem("hg_act"), 1)
                    for n_ in range(10 * h + 4, 10 * h + 8):
                        keep_tokens(n_)
                    act.wait_ge(sem("hg_vec"), 4 * h + 3)
                    act.activation(tmp[0], tmp[5], ACT.Exp).then_inc(sem("hg_act"), 1)
                    act.activation(tmp[2], tmp[5], ACT.Exp, scale=-1.0).then_inc(sem("hg_act"), 1)
                    act.activation(tmp[4], tmp[4], ACT.Exp).then_inc(sem("hg_act"), 1)
                    act.activation(dec[:, h, :], dec[:, h, :], ACT.Exp).then_inc(sem("hg_act"), 1)
                    for n_ in range(10 * h + 8, 10 * h + 10):
                        keep_tokens(n_)

            @block.vector
            def _(dve):
                step(dve, dve.tensor_copy(par[:, :], par_all[:, bass.ds(l, 1), :].rearrange("p o c -> p (o c)")), "par_set")
                for x in (kv_tok, win_tok, q_tok):
                    dve.memset(x[NS:P, NT, :], 0.0)
                norm_vector(dve, "n1", sq1, S1, G_ATTN)
                dve.wait_ge(sem("proj_kept"), NF)
                for h in range(HH):
                    z = hf[:, h, :]
                    n = HACT * h
                    t0, t1, t2, t3, t4, t5, t6 = tmp
                    for t, x in ((t0, z), (t3, hq[:, h, :]), (t6, hg[:, h, :])):
                        dve.scalar_tensor_tensor(t, x, -1.0, x, ALU.mult, ALU.max)
                    dve.tensor_scalar(t4, z, 0.0, col(P_LNOM + h), ALU.min, ALU.add)
                    dve.tensor_scalar(t1, z, 0.0, None, ALU.max).then_inc(sem("hg_vec"), 1)
                    dve.wait_ge(sem("hg_act"), n + 8)
                    step(dve, dve.tensor_tensor(t4, t4, t0, ALU.subtract), "dve_done")
                    step(dve, dve.tensor_scalar(t0, t4, col(P_LBA + h), None, ALU.subtract), "dve_done")
                    step(dve, dve.scalar_tensor_tensor(t0, t0, -1.0, t0, ALU.mult, ALU.min), "dve_done")
                    dve.scalar_tensor_tensor(t3, hq[:, h, :], 0.0, t3, ALU.min, ALU.subtract)
                    dve.scalar_tensor_tensor(t6, hg[:, h, :], 0.0, t6, ALU.min, ALU.subtract).then_inc(sem("hg_vec"), 1)
                    dve.scalar_tensor_tensor(t1, t1, col(P_OM + h), t2, ALU.mult, ALU.mult).then_inc(sem("hg_key"), 1)
                    dve.wait_ge(sem("hg_act"), n + 12)
                    step(dve, dve.tensor_tensor(t3, hq[:, h, :], t3, ALU.mult), "dve_done")
                    step(dve, dve.scalar_tensor_tensor(t4, t4, col(P_LBA + h), t0, ALU.max, ALU.add), "dve_done")
                    step(dve, dve.tensor_tensor_scan(t5, const("scan"), t4, 0.0, ALU.mult, ALU.add), "dve_done")
                    bp = t5[:, 0:SEQ].rearrange("p (c n) -> p c n", n=CH)
                    bs = t5[:, SEQ:N].rearrange("p (c n) -> p c n", n=DT)
                    dve.tensor_copy(dec[:, h, 0:16], bp[:, :, CH - 1]).then_inc(sem("hg_last"), 1)
                    dve.tensor_copy(dec[:, h, 16:24], bs[:, :, DT - 1]).then_inc(sem("hg_last"), 1)
                    dve.wait_ge(sem("hg_last"), 2 * h + 2)
                    dve.tensor_tensor(t4[:, 0:SEQ].rearrange("p (c n) -> p c n", n=CH), bc(dec[:, h, 0:16], CH), bp,
                                      ALU.subtract)
                    dve.tensor_tensor(t4[:, SEQ:N].rearrange("p (c n) -> p c n", n=DT), bc(dec[:, h, 16:24], DT), bs,
                                      ALU.subtract).then_inc(sem("hg_vec"), 1)
                    dve.wait_ge(sem("hg_key"), h + 1)
                    dve.wait_ge(sem("hg_act"), n + HACT)
                    dve.tensor_tensor(hq[:, h, :], t3, t0, ALU.mult)
                    dve.tensor_tensor(hf[:, h, :], t1, t2, ALU.mult)
                    dve.tensor_tensor(kd[:, h, :], t1, t4, ALU.mult).then_inc(sem("hg_vec"), 1)
                    dve.wait_ge(sem("hg_vec"), 4 * h + 4)

        proj_scope.close()
        R2 = mix_scope.enter_context(nc.sbuf_tensor("R2", [P, R2_N], F32))
        HT_ = mix_scope.enter_context(nc.sbuf_tensor("HT", [P, KC * N], F32))
        W1 = [mix_scope.enter_context(nc.sbuf_tensor(f"W1_{i}", [P, SLOT], F32)) for i in range(2)]

        cut = cutter(R2)
        ST = [cut(17 * P).rearrange("p (n e) -> p n e", n=17) for _ in range(2)]
        S0 = [cut(NB * P).rearrange("p (b e) -> p b e", b=NB) for _ in range(2)]
        Snew = cut(NB * P).rearrange("p (b e) -> p b e", b=NB)
        Vm = cut(NB * P).rearrange("p (b e) -> p b e", b=NB)
        aTm = [cut(P) for _ in range(3)]
        aTs = [cut(NS)[0:NS] for _ in range(2)]
        kdt = [cut(P) for _ in range(2)]
        QR = HT_[:, 0:TT * 512].rearrange("p (t c) -> p t c", t=TT)
        KN = HT_[:, TT * 512:TT * 768].rearrange("p (b t c) -> p b t c", b=2, t=TT)
        ROT = OT_[:, 0:4 * N].rearrange("p (b c) -> p b c", b=3)
        ktok = [kv_tok[:, :, 256:384], win_tok[:, :, 0:128]]
        UNITS = 5 * HH

        def span(u):
            h, t = u // 5, u % 5
            r = rows_of(t)
            return h, t, r, slice(t * P, t * P + r)

        def apart(u):
            return Vm[:, 4 * (u % 5 % 2):4 * (u % 5 % 2) + 4] if u % 5 < NT else Vm[0:NS]

        def store_states(sp, h):
            sp.wait_ge(sem("hg_state"), 5 * h + 4)
            sp.dma_start(p_hg[bass.ds(l, 1), 0, h].rearrange("o d e -> (o d) e"), ST[h % 2][:, 16, :]
                         ).then_inc(sem("p_hg_stored"), 16)
            sp.wait_ge(sem("hg_state"), 5 * h + 5)
            sp.dma_start(s_hg[bass.ds(l, 1), :, h].rearrange("o b d e -> d (o b) e"), Snew
                         ).then_inc(sem("s_hg_stored"), 16)

        with nc.Block() as block:
            @block.sync
            def _(sp):
                for k in range(2):
                    sp.dma_start(W1[k][:, :].rearrange("p (r n) -> p r n", r=16),
                                 cmp_w1[bass.ds(l, 1), k].rearrange("o (c p) n -> p (o c) n", p=P)
                                 ).then_inc(sem("w1_loaded"), 16)
                for h in range(HH):
                    if h >= 2:
                        sp.wait_ge(sem("hg_o_done"), 5 * (h - 1))
                        sp.wait_ge(sem("hg_state"), 5 * (h - 1))
                    sp.dma_start(S0[h % 2], state_hgrn[bass.ds(l, 1), :, h].rearrange("o b d e -> d (o b) e")
                                 ).then_inc(sem(f"s0_loaded{h % 2}"), 16)
                    if h >= 1:
                        store_states(sp, h - 1)
                store_states(sp, HH - 1)
                sp.wait_ge(sem("p_hg_stored"), 16 * HH)
                sp.wait_ge(sem("s_hg_stored"), 16 * HH)

            @block.tensor
            def _(pe):
                def scores(u):
                    h, t, r, c = span(u)
                    if u >= 2:
                        pe.wait_ge(sem("hg_masked"), u - 1)
                        pe.wait_ge(sem("hg_kd_kept"), u - 1)
                    pe.matmul(bank[u % 2][0:r, 0:r], hf[:, h, c], hq[:, h, c], start=True, stop=True
                              ).then_inc(sem("hg_scores"), 1)
                    pe.transpose(bank[2 + u % 2][0:r, 0:P], kd[:, h, c], ident).then_inc(sem("hg_turned"), 1)

                def updates(u):
                    h, t, r, c = span(u)
                    pe.wait_ge(sem("hg_kd_kept"), u + 1)
                    if u >= 1:
                        pe.wait_ge(sem("hg_state"), u)
                    pe.wait_ge(sem("hg_apart"), u + 1)
                    if t < NT:
                        ins = pe.matmul(bank[4][:, :], kdt[u % 2], apart(u), start=True, stop=True)
                    else:
                        for s in range(2):
                            ins = pe.matmul(bank[4 + s][:, :], kdt[u % 2][0:NS, :], apart(u)[:, 4 * s:4 * s + 4, :],
                                            start=True, stop=True)
                    ins.then_inc(sem("hg_updates"), 1)

                def outputs(u):
                    h, t, r, c = span(u)
                    pe.wait_ge(sem("hg_masked"), u + 1)
                    if u >= 2:
                        pe.wait_ge(sem("hg_out_kept"), u - 1)
                    o = bank[6 + u % 2]
                    a = aTm[(4 * h + t) % 3] if t < NT else aTs[h % 2]
                    pe.matmul(o[:, 0:r], hi_tok[0:r, t, h * P:(h + 1) * P], a[:, :], start=True, stop=False)
                    if t < NT:
                        pe.wait_ge(sem("hg_state"), u + 1)
                        n, w, s = NCK, CH, ST[h % 2][:, 4 * t:4 * t + 4, :]
                    else:
                        pe.wait_ge(sem(f"s0_loaded{h % 2}"), 16 * (h // 2 + 1))
                        n, w, s = NB, DT, S0[h % 2]
                    for j in range(n):
                        ins = pe.matmul(o[:, j * w:(j + 1) * w], s[:, j, :], hq[:, h, t * P + j * w:t * P + (j + 1) * w],
                                        start=False, stop=(j == n - 1))
                    ins.then_inc(sem("hg_o_done"), 1)

                for u in range(UNITS + 2):
                    if u < UNITS:
                        scores(u)
                    if 1 <= u <= UNITS:
                        updates(u - 1)
                    if u >= 2:
                        outputs(u - 2)
                for h in range(HH):
                    pe.wait_ge(sem("hgn_squared"), h + 1)
                    if h >= 2:
                        pe.wait_ge(sem("hgn_ln"), h - 1)
                    for s in range(2):
                        ins = pe.matmul(bank[2 * (h % 2) + s][:, 0:HALF], ones, kd[:, h, s * HALF:(s + 1) * HALF],
                                        start=True, stop=True)
                    ins.then_inc(sem("hgn_summed"), 1)

            @block.scalar
            def _(act):
                act.activation(HT_[:, 0:TT * 512].rearrange("p (t c) -> p t c", t=TT), q_tok, ACT.Square
                               ).then_inc(sem("qk_squared"), 1)
                for b in range(2):
                    act.activation(KN[:, b], ktok[b], ACT.Square).then_inc(sem("qk_squared"), 1)
                act.wait_ge(sem("qk_summed"), 3)
                act.activation(qkr[:, 0:60], qkr[:, 0:60], ACT.Ln, bias=eps, scale=1.0 / HD).then_inc(sem("qk_ln"), 1)
                act.wait_ge(sem("qk_ln"), 1)
                act.activation(qkr[:, 0:60], qkr[:, 0:60], ACT.Exp, scale=-0.5).then_inc(sem("qk_rstd"), 1)
                for u in range(UNITS + 3):
                    if u < UNITS:
                        h, t, r, c = span(u)
                        act.wait_ge(sem("hg_turned"), u + 1)
                        if u >= 2:
                            act.wait_ge(sem("hg_updates"), u - 1)
                        act.activation(kdt[u % 2][0:r, :], bank[2 + u % 2][0:r, 0:P], ACT.Copy
                                       ).then_inc(sem("hg_kd_kept"), 1)
                    if u >= 3:
                        h, t, r, c = span(u - 3)
                        act.wait_ge(sem("hg_o_done"), u - 2)
                        act.activation(OT[:, 4 + h, c], bank[6 + (u - 3) % 2][:, 0:r], ACT.Copy
                                       ).then_inc(sem("hg_out_kept"), 1)
                act.wait_ge(sem("hg_out_kept"), UNITS)
                for h in range(HH):
                    act.activation(kd[:, h, :], OT[:, 4 + h, :], ACT.Square).then_inc(sem("hgn_squared"), 1)
                for h in range(HH):
                    act.wait_ge(sem("hgn_summed"), h + 1)
                    for s in range(2):
                        ins = act.activation(hq[:, h, s * HALF:(s + 1) * HALF], bank[2 * (h % 2) + s][:, 0:HALF], ACT.Ln,
                                             bias=eps, scale=1.0 / P)
                    ins.then_inc(sem("hgn_ln"), 1)
                    act.wait_ge(sem("hgn_ln"), h + 1)
                    act.activation(hq[:, h, :], hq[:, h, :], ACT.Exp, scale=-0.5).then_inc(sem("hgn_rstd"), 1)

            @block.vector
            def _(dve):
                for i in range(3):
                    dve.memset(aTm[i], 0.0)
                for i in range(2):
                    dve.memset(aTs[i], 0.0)
                    dve.memset(ST[i][:, 0, :], 0.0)
                dve.wait_ge(sem("qk_squared"), 3)
                dve.tensor_reduce(qkr[:, 0:40], QR.rearrange("p t (h d) -> p (t h) d", d=HD), AX, ALU.add
                                  ).then_inc(sem("qk_summed"), 1)
                for b in range(2):
                    dve.tensor_reduce(qkr[:, 40 + 10 * b:50 + 10 * b], KN[:, b].rearrange("p t (h d) -> p (t h) d", d=HD),
                                      AX, ALU.add).then_inc(sem("qk_summed"), 1)
                dve.wait_ge(sem("qk_summed"), 3)

                def masked(u):
                    h, t, r, c = span(u)
                    dve.wait_ge(sem("hg_scores"), u + 1)
                    if u >= 3:
                        dve.wait_ge(sem("hg_o_done"), u - 2)
                    a = aTm[(4 * h + t) % 3] if t < NT else aTs[h % 2]
                    m = const("hgmask") if t < NT else const("hgmask8", NS)
                    dve.copy_predicated(a, m.bitcast(U32), bank[u % 2][0:r, 0:r]).then_inc(sem("hg_masked"), 1)
                    if u >= 2:
                        dve.wait_ge(sem("hg_updates"), u if t in (0, NT) else u - 1)
                    n, m = (NCK, const("chunk")) if t < NT else (NB, const("batch", NS))
                    dve.tensor_tensor(apart(u), hi_tok[0:r, t, h * P:(h + 1) * P].unsqueeze(1).to_broadcast([r, n, P]),
                                      bc(m, P), ALU.mult).then_inc(sem("hg_apart"), 1)

                def states(u):
                    h, t, r, c = span(u)
                    dve.wait_ge(sem("hg_updates"), u + 1)
                    if t < NT:
                        if h >= 2 and t == 0:
                            dve.wait_ge(sem("p_hg_stored"), 16 * (h - 1))
                            dve.wait_ge(sem("hg_o_done"), 5 * (h - 1))
                        s = ST[h % 2]
                        for j in range(NCK):
                            n = 4 * t + j
                            ins = dve.scalar_tensor_tensor(s[:, n + 1, :], s[:, n, :], dec[:, h, n:n + 1],
                                                           bank[4][:, j * P:(j + 1) * P], ALU.mult, ALU.add)
                            if j < NCK - 1:
                                step(dve, ins, "dve_done")
                        ins.then_inc(sem("hg_state"), 1)
                        dve.wait_ge(sem("hg_state"), u + 1)
                    else:
                        dve.wait_ge(sem(f"s0_loaded{h % 2}"), 16 * (h // 2 + 1))
                        if h >= 1:
                            dve.wait_ge(sem("s_hg_stored"), 16 * h)
                        for b in range(NB):
                            ins = dve.scalar_tensor_tensor(Snew[:, b, :], S0[h % 2][:, b, :], dec[:, h, 16 + b:17 + b],
                                                           bank[4 + b // 4][:, (b % 4) * P:(b % 4 + 1) * P],
                                                           ALU.mult, ALU.add)
                        ins.then_inc(sem("hg_state"), 1)

                for u in range(UNITS + 1):
                    if u < UNITS:
                        masked(u)
                    if u >= 1:
                        states(u - 1)
                for h in range(HH):
                    dve.wait_ge(sem("hgn_rstd"), h + 1)
                    step(dve, dve.scalar_tensor_tensor(OT[:, 4 + h, :], OT[:, 4 + h, :], col(G_HG), hq[:, h, :],
                                                       ALU.mult, ALU.mult), "dve_done")
                    dve.tensor_tensor(OT[:, 4 + h, :], OT[:, 4 + h, :], hg[:, h, :], ALU.mult)

            @block.gpsimd
            def _(pool):
                pool.wait_ge(sem("qk_rstd"), 1)
                pool.wait_ge(sem("gain_loaded"), 48)

                def norm(dst, src, r0, nh, g):
                    d = dst.rearrange("p t (h d) -> p t h d", d=HD)
                    s = src.rearrange("p t (h d) -> p t h d", d=HD)
                    r = qkr[:, r0:r0 + TT * nh].rearrange("p (t h) -> p t h", t=TT)
                    g_ = gain[:, g * HD:(g + 1) * HD].unsqueeze(1).to_broadcast([P, nh, HD])
                    for t in range(TT):
                        step(pool, pool.tensor_tensor(d[:, t], s[:, t], bc(r[:, t], HD), ALU.mult), "pool_done")
                        step(pool, pool.tensor_tensor(d[:, t], d[:, t], g_, ALU.mult), "pool_done")

                def rotate(dst, src, nh):
                    d = dst.rearrange("p t (h d) -> p t h d", d=HD)
                    s = src.rearrange("p t (h d) -> p t h d", d=HD)
                    F = HD // 2
                    cos = const("cos").rearrange("p (t f) -> p t f", f=F)
                    sin = const("sin").rearrange("p (t f) -> p t f", f=F)
                    a, b = (ROT[:, i, 0:nh * F].rearrange("p (h f) -> p h f", f=F) for i in range(2))
                    for t in range(TT):
                        c_ = cos[:, t].unsqueeze(1).to_broadcast([P, nh, F])
                        s_ = sin[:, t].unsqueeze(1).to_broadcast([P, nh, F])
                        for lo, x, y, op in ((0, 0, F, ALU.subtract), (F, F, 0, ALU.add)):
                            pool.tensor_tensor(a, s[:, t, :, x:x + F], c_, ALU.mult)
                            step(pool, pool.tensor_tensor(b, s[:, t, :, y:y + F], s_, ALU.mult), "pool_done")
                            step(pool, pool.tensor_tensor(d[:, t, :, lo:lo + F], a, b, op), "pool_done")

                norm(q_tok, q_tok, 0, NH, 0)
                for b in range(2):
                    norm(KN[:, b], ktok[b], 40 + 10 * b, NKV, 1 + b)
                    rotate(ktok[b], KN[:, b], NKV)
                rotate(QR, q_tok, NH)


        o_tok = hi_tok
        cut = cutter(R1, R_HG)
        QN = cut(NG * N).rearrange("p (g n) -> p g n", g=NG)
        QT = cut(NG * N).rearrange("p (g n) -> p g n", g=NG)
        KT = cut(2 * N).rearrange("p (b n) -> p b n", b=2)
        gate = cut(TT * 24).rearrange("p (t c) -> p t c", t=TT)
        R_ATT = R_HG + (2 * NG + 2) * N + TT * 24
        probs = [cut(512) for _ in range(3)]
        probsT = [cut(512) for _ in range(2)]
        nmax, rsum, coef, otmp = cut(64), cut(64), cut(64), cut(512)
        SCALE = HD ** -0.5
        vtok = [kv_tok[:, :, 384:512], win_tok[:, :, 128:256]]

        TURNS = [(k, t) for t in range(TT) for k in range(3)]
        AU = [(t, b, v, g) for t in range(NT) for b in range(2) for v in range(NKV) for g in range(NG)]
        AG = len(AU) // NH

        def turn_views(k, t):
            r = rows_of(t)
            n = NG if k < 2 else 2
            dst = (QN, QT, KT)[k][:, :, t * P:t * P + r]
            return r, n, dst

        def kept_before(n, parity):
            return (n + 1 - parity) // 2

        raw = [t.rearrange("p (r k c) -> p r k c", r=CST, k=2) for t in (HT_[:, 0:4096], R2[:, 0:4096])]
        cut = cutter(R2, 4096)
        FT_ = [cut(NKV * 8 * P) for _ in range(2)]
        ksq = cut(NCALL)
        cut = cutter(R1, R_HI + TT * 512)
        KCT, VCT = cut(NCALL), cut(NCALL)
        VC = cut(4 * P).rearrange("p (a c) -> p a c", a=4)
        VB = cut(NKV * 256).rearrange("p (v c) -> p v c", v=NKV)
        cut = cutter(R1, R_ATT)
        cx, cu, GH = ([cut(4 * P) for _ in range(2)] for _ in range(3))
        W2 = OT_[:, 0:1024].rearrange("p (k v h c) -> p k v h c", k=2, v=NKV, h=2)
        posr = OT_[0:32, 1024:1152]
        posT = OT_[:, 1152:1184]
        G_A, G_B = (2 / np.pi) ** 0.5, 0.044715 * (2 / np.pi) ** 0.5

        def load_chunks(sp, p):
            if p == 4:
                sp.dma_start(raw[0][0:NCP].rearrange("p r k c -> p r (k c)"),
                             p_nsa[bass.ds(l, 1), 0, :, 0:2].rearrange("o (c r) k v d -> (o c) r (k v d)", r=CST)
                             ).then_inc(sem("raw_loaded0"), 16)
                return
            for j in range(16):
                pg = sp.value_load(pages[0:1, 16 * p + j:16 * p + j + 1], min_val=0, max_val=NPOOL - 1)
                sp.dma_start(raw[p % 2][8 * j:8 * j + 8].rearrange("p r k c -> p r (k c)"),
                             cache_nsa_kv[bass.ds(l, 1), bass.ds(pg, 1), :, 0:2].rearrange(
                                 "o q (c r) k v d -> (o q c) r (k v d)", r=CST)
                             ).then_inc(sem(f"raw_loaded{p % 2}"), 16)

        with nc.Block() as block:
            @block.sync
            def _(sp):
                sp.dma_start(p_nsa[bass.ds(l, 1)].rearrange("o b (t p) k h d -> p (o b t) (k h d)", p=P),
                             kv_tok[:, 0:NT, :]).then_inc(sem("nsa_stored"), 16)
                sp.dma_start(s_nsa[bass.ds(l, 1)].rearrange("o b t k h d -> (o b t) (k h d)"),
                             kv_tok[0:NS, NT, :]).then_inc(sem("rows_stored"), 16)
                sp.dma_start(p_win[bass.ds(l, 1)].rearrange("o b (t p) k h d -> p (o b t) (k h d)", p=P),
                             win_tok[:, 0:NT, 0:256]).then_inc(sem("rows_stored"), 16)
                sp.dma_start(s_win[bass.ds(l, 1)].rearrange("o b t k h d -> (o b t) (k h d)"),
                             win_tok[0:NS, NT, 0:256]).then_inc(sem("rows_stored"), 16)
                load_chunks(sp, 1)
                for k in range(2):
                    sp.dma_start(posr[16 * k:16 * k + 16, :],
                                 cmp_pos[bass.ds(l, 1), k].rearrange("o (a b) d -> (o a) (b d)", b=2)
                                 ).then_inc(sem("pos_loaded"), 16)
                sp.wait_ge(sem("w2_cleared"), 1)
                for k in range(2):
                    for v in range(NKV):
                        sp.dma_start(W2[:, k, v, :, v * HD:(v + 1) * HD],
                                     cmp_w2[bass.ds(l, 1), k].rearrange("o (h p) d -> p (o h) d", p=P)
                                     ).then_inc(sem("w2_loaded"), 16)
                sp.wait_ge(sem("turned"), len(TURNS))
                load_chunks(sp, 0)
                sp.wait_ge(sem("nsa_stored"), 16)
                sp.wait_ge(sem("rows_stored"), 48)

            @block.gpsimd
            def _(pool):
                pool.memset(W2, 0.0).then_inc(sem("w2_cleared"), 1)

            @block.tensor
            def _(pe):
                for u, (k, t) in enumerate(TURNS):
                    r, n, dst = turn_views(k, t)
                    if u >= 4:
                        pe.wait_ge(sem(f"turn_kept{u % 2}"), (u - 4) // 2 + 1)
                    for g in range(n):
                        src = (q_tok, QR)[k][0:r, t, g * P:(g + 1) * P] if k < 2 else ktok[g][0:r, t, :]
                        ins = pe.transpose(bank[u % 4][:, g * r:(g + 1) * r], src, ident[0:r, 0:r])
                    ins.then_inc(sem("turned"), 1)
                for i in range(2):
                    pe.wait_ge(sem(f"turn_kept{i}"), kept_before(len(TURNS), i))

                def scores(n):
                    t, b, v, g = AU[n]
                    if n >= 3:
                        pe.wait_ge(sem("probs_made"), n - 2)
                    k = slice(v * HD, (v + 1) * HD)
                    pe.matmul(bank[n % 3][:, 0:(t + 1) * P], QT[k, g, t * P:(t + 1) * P], KT[k, b, 0:(t + 1) * P],
                              start=True, stop=True).then_inc(sem("scored"), 1)

                def turn_probs(n):
                    t, b, v, g = AU[n]
                    pe.wait_ge(sem("probs_made"), n + 1)
                    if n >= 2:
                        pe.wait_ge(sem(f"probsT_kept{n % 2}"), n // 2)
                    for j in range(t + 1):
                        ins = pe.transpose(bank[3 + n % 2][:, j * P:(j + 1) * P], probs[n % 3][:, j * P:(j + 1) * P], ident)
                    ins.then_inc(sem("probs_turned"), 1)

                def values(n):
                    t, b, v, g = AU[n]
                    grp, h = n // NH, n % NH
                    if h == 0 and grp >= 2:
                        pe.wait_ge(sem("o_kept"), grp - 1)
                    pe.wait_ge(sem(f"probsT_kept{n % 2}"), n // 2 + 1)
                    for j in range(t + 1):
                        ins = pe.matmul(bank[5 + grp % 2][:, h * HD:(h + 1) * HD], probsT[n % 2][:, j * P:(j + 1) * P],
                                        vtok[b][:, j, v * HD:(v + 1) * HD], start=(j == 0), stop=(j == t))
                    ins.then_inc(sem("valued"), 1)

                for n in range(len(AU) + 3):
                    if n < len(AU):
                        scores(n)
                    if 2 <= n < len(AU) + 2:
                        turn_probs(n - 2)
                    if n >= 3:
                        values(n - 3)

            def keep_turn(eng, u):
                k, t = TURNS[u]
                r, n, dst = turn_views(k, t)
                eng.wait_ge(sem("turned"), u + 1)
                src = bank[u % 4][:, 0:n * r].rearrange("p (g n) -> p g n", g=n)
                if eng is nc.scalar:
                    ins = eng.activation(dst, src, ACT.Copy, scale=SCALE if k < 2 else 1.0)
                else:
                    ins = eng.tensor_scalar(dst, src, SCALE if k < 2 else 1.0, None, ALU.mult)
                ins.then_inc(sem(f"turn_kept{u % 2}"), 1)

            def keep_probsT(eng, n):
                t = AU[n][0]
                eng.wait_ge(sem("probs_turned"), n + 1)
                if n >= 2:
                    eng.wait_ge(sem("valued"), n - 1)
                src, dst = bank[3 + n % 2][:, 0:(t + 1) * P], probsT[n % 2][:, 0:(t + 1) * P]
                ins = eng.activation(dst, src, ACT.Copy) if eng is nc.scalar else eng.tensor_copy(dst, src)
                ins.then_inc(sem(f"probsT_kept{n % 2}"), 1)

            @block.scalar
            def _(act):
                act.activation(gate, win_tok[:, :, 256:WINW], ACT.Exp, scale=-1.0).then_inc(sem("gate_exp"), 1)
                for u in range(0, len(TURNS), 2):
                    keep_turn(nc.scalar, u)
                for n in range(len(AU) + 3):
                    if n >= 3 and (n - 3) % 2 == 0:
                        keep_probsT(nc.scalar, n - 3)
                    if n < len(AU):
                        t = AU[n][0]
                        act.wait_ge(sem("maxed"), n + 1)
                        if n >= 3:
                            act.wait_ge(sem("probs_turned"), n - 2)
                        act.activation(probs[n % 3][:, 0:(t + 1) * P], bank[n % 3][:, 0:(t + 1) * P], ACT.Exp,
                                       bias=nmax[:, n:n + 1], accum_out=rsum[:, n:n + 1]).then_inc(sem("probs_made"), 1)

            @block.vector
            def _(dve):
                dve.wait_ge(sem("gate_exp"), 1)
                step(dve, dve.tensor_scalar(gate, gate, 1.0, None, ALU.add), "dve_done")
                step(dve, dve.reciprocal(gate, gate), "dve_done")
                for u in range(1, len(TURNS), 2):
                    keep_turn(nc.vector, u)

                def keep_group(grp):
                    t, b = AU[grp * NH][0:2]
                    c = coef[:, grp * NH:(grp + 1) * NH]
                    step(dve, dve.reciprocal(c, rsum[:, grp * NH:(grp + 1) * NH]), "dve_done")
                    step(dve, dve.tensor_tensor(c, c, gate[:, t, :].rearrange("p (h b) -> p h b", b=3)[:, :, 1 + b],
                                                ALU.mult), "dve_done")
                    dve.wait_ge(sem("valued"), NH * (grp + 1))
                    o = bank[5 + grp % 2][:, :].rearrange("p (h d) -> p h d", d=HD)
                    dst = (o_tok[:, t, :] if b == 0 else otmp).rearrange("p (h d) -> p h d", d=HD)
                    dve.tensor_tensor(dst, o, bc(c, HD), ALU.mult).then_inc(sem("o_kept"), 1)
                    if b == 1:
                        dve.wait_ge(sem("o_kept"), grp + 1)
                        step(dve, dve.tensor_tensor(o_tok[:, t, :], o_tok[:, t, :], otmp, ALU.add), "dve_done")

                for n in range(len(AU) + 6):
                    if n >= 3 and n - 3 < len(AU) and (n - 3) % 2 == 1:
                        keep_probsT(nc.vector, n - 3)
                    if n < len(AU):
                        t = AU[n][0]
                        dve.wait_ge(sem("scored"), n + 1)
                        d = bank[n % 3][:, t * P:(t + 1) * P]
                        step(dve, dve.tensor_tensor(d, d, const("causal"), ALU.add), "dve_done")
                        dve.tensor_reduce(nmax[:, n:n + 1], bank[n % 3][:, 0:(t + 1) * P], AX, ALU.max, negate=True
                                          ).then_inc(sem("maxed"), 1)
                    if n >= 5 and (n - 5) % NH == NH - 1:
                        keep_group((n - 5) // NH)


        FT = [FT_[i].rearrange("p (v r n) -> p v r n", v=NKV, r=8) for i in range(2)]
        CU = [(p, k) for p in range(5) for k in range(2)]

        def chunks_of(w):
            p = CU[w][0]
            n = P if p < 4 else NCP
            return n, slice(p * P, p * P + n)

        with nc.Block() as block:
            @block.sync
            def _(sp):
                for p in range(2, 5):
                    sp.wait_ge(sem("ct_done"), 8 * (p - 1))
                    load_chunks(sp, p)

            def raw_count(p):
                return sum(16 if m == 4 else 256 for m in range(p % 2, p + 1, 2))

            @block.tensor
            def _(pe):
                w1 = [W1[k][:, :].rearrange("p (r n) -> p r n", r=16) for k in range(2)]
                pe.wait_ge(sem("w1_loaded"), 32)
                pe.wait_ge(sem("pos_loaded"), 32)
                pe.transpose(bank[6][:, 0:32], posr, ident[0:32, 0:32]).then_inc(sem("pos_turned"), 1)
                pe.wait_ge(sem("pos_kept"), 1)
                for k in range(2):
                    for h in range(2):
                        for r in range(16):
                            ins = pe.matmul(bank[7][:, 2 * k + h:2 * k + h + 1], w1[k][:, r, h * P:(h + 1) * P],
                                            posT[:, 16 * k + r:16 * k + r + 1], start=(r == 0), stop=(r == 15))
                ins.then_inc(sem("bias_done"), 1)

                def turns(w):
                    p, k = CU[w]
                    n, _ = chunks_of(w)
                    if k == 0:
                        pe.wait_ge(sem(f"raw_loaded{p % 2}"), raw_count(p))
                    for j in range(4):
                        u = 4 * w + j
                        if u >= 4:
                            pe.wait_ge(sem(f"ct_kept{u % 2}"), (u - 4) // 2 + 1)
                        for r in range(4):
                            ins = pe.transpose(bank[j][:, r * n:(r + 1) * n], raw[p % 2][0:n, 4 * j + r, k, :],
                                               ident[0:n, 0:n])
                        ins.then_inc(sem("ct_done"), 1)

                def hidden(w):
                    p, k = CU[w]
                    n, _ = chunks_of(w)
                    for i in range(2):
                        pe.wait_ge(sem(f"ct_kept{i}"), 2 * (w + 1))
                    if w >= 2:
                        pe.wait_ge(sem("x_kept"), w - 1)
                    for v in range(NKV):
                        for h in range(2):
                            o = (2 * v + h) * n
                            for r in range(16):
                                s = r // 8
                                ins = pe.matmul(bank[4 + w % 2][:, o:o + n - s], w1[k][:, r, h * P:(h + 1) * P],
                                                FT[w % 2][:, v, r % 8, s:n], start=(r == 0), stop=(r == 15))
                    ins.then_inc(sem("h_done"), 1)

                def outputs(w):
                    p, k = CU[w]
                    n, _ = chunks_of(w)
                    if w == 0:
                        pe.wait_ge(sem("w2_loaded"), 64)
                        pe.wait_ge(sem("bias_kept"), 1)
                    else:
                        pe.wait_ge(sem("c_out_kept"), w - 1)
                    pe.wait_ge(sem("gelu_done"), w + 1)
                    for m in range(4):
                        ins = pe.matmul(bank[6 + w % 2][:, 0:n], W2[:, k, m // 2, m % 2, :], GH[w % 2][:, m * n:(m + 1) * n],
                                        start=(m == 0), stop=(m == 3))
                    ins.then_inc(sem("c_out_done"), 1)

                for w in range(len(CU) + 2):
                    if w < len(CU):
                        turns(w)
                    if 1 <= w <= len(CU):
                        hidden(w - 1)
                    if w >= 2:
                        outputs(w - 2)
                pe.wait_ge(sem("kc_squared"), 1)
                pe.wait_ge(sem("x_kept"), len(CU))
                pe.matmul(bank[4][:, :], ones64, ksq[:, 0:NCC], start=True, stop=True)
                pe.matmul(bank[5][:, 0:NCP], ones64, ksq[:, NCC:NCALL], start=True, stop=True).then_inc(sem("kc_summed"), 1)
                pe.wait_ge(sem("vct_kept"), 1)
                for a in range(4):
                    pe.transpose(bank[6][:, a * P:(a + 1) * P], VCT[:, a * P:(a + 1) * P], ident)
                pe.transpose(bank[7][:, 0:P], cx[0][:, 0:P], ident).then_inc(sem("vc_turned"), 1)

            def keep_ct(eng, w, odd):
                n, _ = chunks_of(w)
                for j in (odd, 2 + odd):
                    eng.wait_ge(sem("ct_done"), 4 * w + j + 1)
                    if w >= 2:
                        eng.wait_ge(sem("h_done"), w - 1)
                    src = bank[j][:, 0:4 * n].rearrange("p (a b n) -> p a b n", a=2, b=2)
                    for v in range(NKV):
                        for b in range(2):
                            d = FT[w % 2][b * HD:(b + 1) * HD, v, 2 * j:2 * j + 2, 0:n]
                            x = src[v * HD:(v + 1) * HD, :, b, :]
                            ins = eng.activation(d, x, ACT.Copy) if eng is nc.scalar else eng.tensor_copy(d, x)
                    ins.then_inc(sem(f"ct_kept{odd}"), 1)

            @block.scalar
            def _(act):
                act.wait_ge(sem("pos_turned"), 1)
                act.activation(posT, bank[6][:, 0:32], ACT.Copy).then_inc(sem("pos_kept"), 1)

                def gelu(w):
                    p, k = CU[w]
                    n, _ = chunks_of(w)
                    act.wait_ge(sem("h_done"), w + 1)
                    if w >= 2:
                        act.wait_ge(sem("gelu_done"), w - 1)
                    for h in range(2):
                        b = par[:, P_HB + 2 * k + h:P_HB + 2 * k + h + 1]
                        if w == 0 and h == 0:
                            act.wait_ge(sem("bias_kept"), 1)
                        x, y = (t[:, 0:4 * n].rearrange("p (v h n) -> p v h n", v=NKV, h=2)[:, :, h, :]
                                for t in (cx[w % 2], bank[4 + w % 2]))
                        ins = act.activation(x, y, ACT.Identity, bias=b)
                    ins.then_inc(sem("x_kept"), 1)
                    act.wait_ge(sem("gelu_arg"), w + 1)
                    c = cu[w % 2][:, 0:4 * n]
                    for f, kw in ((ACT.Exp, dict(scale=-2.0)), (ACT.Ln, dict(bias=one)), (ACT.Exp, dict(scale=-1.0))):
                        step(act, act.activation(c, c, f, **kw), "gelu_act")

                def keep_output(w):
                    n, cols = chunks_of(w)
                    act.wait_ge(sem("c_out_done"), w + 1)
                    act.activation((KCT, VCT)[CU[w][1]][:, cols], bank[6 + w % 2][:, 0:n], ACT.Copy
                                   ).then_inc(sem("c_out_kept"), 1)

                for w in range(len(CU) + 2):
                    if w < len(CU):
                        keep_ct(nc.scalar, w, 0)
                    if 1 <= w <= len(CU):
                        gelu(w - 1)
                    if w >= 2:
                        keep_output(w - 2)
                    if w == len(CU):
                        act.wait_ge(sem("c_out_kept"), len(CU) - 1)
                        act.activation(ksq, KCT, ACT.Square).then_inc(sem("kc_squared"), 1)
                act.wait_ge(sem("c_out_kept"), len(CU))
                act.activation(cx[0][:, 0:P].rearrange("p (g n) -> p g n", g=NG),
                               VCT[:, NCC:NCALL].unsqueeze(1).to_broadcast([P, NG, NCP]), ACT.Copy
                               ).then_inc(sem("vct_kept"), 1)
                act.wait_ge(sem("kc_summed"), 1)
                act.activation(ksq[:, 0:NCC], bank[4][:, :], ACT.Ln, bias=eps, scale=1.0 / HD)
                act.activation(ksq[:, NCC:NCALL], bank[5][:, 0:NCP], ACT.Ln, bias=eps, scale=1.0 / HD
                               ).then_inc(sem("kc_ln"), 1)
                act.wait_ge(sem("kc_ln"), 1)
                act.activation(ksq, ksq, ACT.Exp, scale=-0.5).then_inc(sem("kc_rstd"), 1)

            @block.vector
            def _(dve):
                dve.memset(VB, 0.0)
                dve.wait_ge(sem("bias_done"), 1)
                dve.tensor_tensor(par[:, P_HB:P_HB + 4], bank[7][:, 0:4], par[:, P_B1:P_B1 + 4], ALU.add
                                  ).then_inc(sem("bias_kept"), 1)

                def gelu(w):
                    n, _ = chunks_of(w)
                    x, c, g = (t[w % 2][:, 0:4 * n] for t in (cx, cu, GH))
                    dve.wait_ge(sem("x_kept"), w + 1)
                    if w >= 2:
                        dve.wait_ge(sem("gelu_done"), w - 1)
                    step(dve, dve.tensor_tensor(c, x, x, ALU.mult), "dve_done")
                    step(dve, dve.tensor_scalar(c, c, float(G_B), float(G_A), ALU.mult, ALU.add), "dve_done")
                    step(dve, dve.tensor_tensor(c, c, x, ALU.mult), "dve_done")
                    dve.tensor_scalar(c, c, -20.0, None, ALU.max).then_inc(sem("gelu_arg"), 1)
                    dve.wait_ge(sem("gelu_act"), 3 * (w + 1))
                    if w >= 2:
                        dve.wait_ge(sem("c_out_done"), w - 1)
                    dve.tensor_tensor(g, x, c, ALU.mult).then_inc(sem("gelu_done"), 1)

                for w in range(len(CU) + 1):
                    if w < len(CU):
                        keep_ct(nc.vector, w, 1)
                    if w >= 1:
                        gelu(w - 1)
                dve.wait_ge(sem("vc_turned"), 1)
                dve.tensor_copy(VC.rearrange("p a c -> p (a c)"), bank[6][:, :])
                for v in range(NKV):
                    for g in range(NG):
                        rr = slice(g * NCP, (g + 1) * NCP)
                        dve.tensor_copy(VB[rr, v, g * HD:(g + 1) * HD], bank[7][rr, v * HD:(v + 1) * HD])
                dve.wait_ge(sem("kc_rstd"), 1)
                dve.scalar_tensor_tensor(KCT, KCT, col(G_KC), ksq, ALU.mult, ALU.mult).then_inc(sem("kc_done"), 1)
                dve.wait_ge(sem("kc_done"), 1)



        QD = HT_[:, 0:1024].rearrange("p (k b r) -> p k b r", k=2, b=NB)
        oS = HT_[0:NS, 1024:2560].rearrange("p (b c d) -> p b c d", b=NB, c=3)
        o3 = HT_[0:NS, 2560:4096]
        DMk = HT_[0:NS, 4096:4224].rearrange("p (b j) -> p b j", b=NB)
        cut = cutter(R1, R_ATT)
        cs = [cut(256) for _ in range(2)]
        csT = [cut(256) for _ in range(2)]
        cm = [cut(256) for _ in range(2)]
        otm = cut(512)
        ss = cut(512)[0:NS].rearrange("p (b c) -> p b c", b=NB)
        ssT = cut(256).rearrange("p (a r) -> p a r", a=4)
        sm = cut(128)[0:NS]
        imp = cut(128)[0:NS].rearrange("p (b j) -> p b j", b=NB)
        val = cut(128)[0:NS].rearrange("p (b j) -> p b j", b=NB)
        NC = NCS - 1

        with nc.Block() as block:
            @block.tensor
            def _(pe):
                pe.wait_ge(sem("qd_made"), 2)
                for b in range(NB):
                    ins = pe.matmul(bank[4][0:NS, b * NCS:(b + 1) * NCS], QD[:, 0, b, :], KCT[:, b * NCS:(b + 1) * NCS],
                                    start=True, stop=True)
                ins.then_inc(sem("s_scored"), 1)

                def prompt_scores(t):
                    if t >= 2:
                        pe.wait_ge(sem("c_read"), 2 * (t - 1))
                    for v in range(NKV):
                        k = slice(v * HD, (v + 1) * HD)
                        for g in range(NG):
                            ins = pe.matmul(bank[2 * (t % 2) + v][:, g * NCP:(g + 1) * NCP],
                                            QN[k, g, t * P:(t + 1) * P], KCT[k, NCC:NCALL], start=True, stop=True)
                    ins.then_inc(sem("c_scored"), 1)

                prompt_scores(0)
                prompt_scores(1)
                pe.wait_ge(sem("s_probs"), 1)
                pe.matmul(bank[5][0:NS, :], const("groupsum", NS), ss, start=True, stop=True).then_inc(sem("s_imp"), 1)
                for a in range(4):
                    ins = pe.transpose(bank[4][:, a * NS:(a + 1) * NS], ss[:, 2 * a:2 * a + 2, :], ident[0:NS, 0:NS])
                ins.then_inc(sem("s_turned"), 1)
                pe.wait_ge(sem("s_turn_kept"), 1)
                for a in range(4):
                    for q in range(2):
                        k = slice(q * HD, (q + 1) * HD)
                        ins = pe.matmul(bank[6 + q][0:NS, a * P:(a + 1) * P], ssT[k, a, :], VC[k, a, :],
                                        start=True, stop=True)
                ins.then_inc(sem("s_valued"), 1)
                for t in range(NT):
                    if 2 <= t + 1 < NT:
                        prompt_scores(t + 1)
                    pe.wait_ge(sem("c_probs"), t + 1)
                    if t == 0:
                        pe.wait_ge(sem("s_imp_kept"), 1)
                    for v in range(NKV):
                        ins = pe.transpose(bank[4][:, v * P:(v + 1) * P], cs[t % 2][:, v * P:(v + 1) * P], ident)
                    ins.then_inc(sem("c_turned"), 1)
                    pe.wait_ge(sem("c_turn_kept"), t + 1)
                    if t >= 1:
                        pe.wait_ge(sem("c_kept"), t)
                    for v in range(NKV):
                        ins = pe.matmul(bank[5][:, v * 256:(v + 1) * 256], csT[t % 2][:, v * P:(v + 1) * P], VB[:, v, :],
                                        start=True, stop=True)
                    ins.then_inc(sem("c_valued"), 1)

            @block.scalar
            def _(act):
                act.wait_ge(sem("s_shifted"), 1)
                act.activation(ss[:, :, 0:NC], ss[:, :, 0:NC], ACT.Exp).then_inc(sem("s_exp"), 1)
                act.wait_ge(sem("s_turned"), 1)
                act.activation(ssT, bank[4][:, 0:256].rearrange("p (a r) -> p a r", a=4), ACT.Copy
                               ).then_inc(sem("s_turn_kept"), 1)
                for t in range(NT):
                    act.wait_ge(sem("c_shifted"), t + 1)
                    act.activation(cs[t % 2], cs[t % 2], ACT.Exp).then_inc(sem("c_exp"), 1)
                    act.wait_ge(sem("c_turned"), t + 1)
                    act.activation(csT[t % 2], bank[4][:, 0:256], ACT.Copy).then_inc(sem("c_turn_kept"), 1)

            @block.vector
            def _(dve):
                step(dve, dve.memset(QD, 0.0), "dve_done")
                step(dve, dve.memset(DMk, 0.0), "dve_done")
                dve.memset(ss[:, :, NC:NCS], 0.0)
                for k, q in enumerate((QN, QT)):
                    for v in range(NKV):
                        rr = slice(v * HD, (v + 1) * HD)
                        ins = dve.tensor_copy(
                            QD[rr, k, :, v * NG * DT:(v + 1) * NG * DT].rearrange("p b (g t) -> p b g t", g=NG),
                            q[rr, :, SEQ:N].rearrange("p g (b t) -> p b g t", b=NB))
                    ins.then_inc(sem("qd_made"), 1)
                dve.wait_ge(sem("s_scored"), 1)
                sc = bank[4][0:NS, :].rearrange("p (b c) -> p b c", b=NB)
                step(dve, dve.tensor_reduce(sm[:, 0:8], sc[:, :, 0:NC], AX, ALU.max, negate=True), "dve_done")
                dve.tensor_tensor(ss[:, :, 0:NC], sc[:, :, 0:NC], bc(sm[:, 0:8], NC), ALU.add).then_inc(sem("s_shifted"), 1)
                dve.wait_ge(sem("s_exp"), 1)
                step(dve, dve.tensor_reduce(sm[:, 8:16], ss[:, :, 0:NC], AX, ALU.add), "dve_done")
                step(dve, dve.reciprocal(sm[:, 16:24], sm[:, 8:16]), "dve_done")
                dve.tensor_tensor(ss[:, :, 0:NC], ss[:, :, 0:NC], bc(sm[:, 16:24], NC), ALU.mult).then_inc(sem("s_probs"), 1)
                dve.wait_ge(sem("s_imp"), 1)
                step(dve, dve.tensor_reduce(imp, bank[5][0:NS, :].rearrange("p (b j c) -> p b j c", b=NB, c=4), AX, ALU.add),
                     "dve_done")
                it, vt = imp[:, :, 1:15], val[:, :, 1:15]
                ix = const("blkidx", NS)[:, 1:15].unsqueeze(1).to_broadcast([NS, NB, 14])
                step(dve, dve.tensor_reduce(sm[:, 24:32], it, AX, ALU.min), "dve_done")
                step(dve, dve.tensor_tensor(vt, it, bc(sm[:, 24:32], 14), ALU.is_le), "dve_done")
                step(dve, dve.tensor_tensor(vt, vt, ix, ALU.mult), "dve_done")
                step(dve, dve.tensor_reduce(sm[:, 32:40], vt, AX, ALU.max), "dve_done")
                step(dve, dve.tensor_tensor(vt, ix, bc(sm[:, 32:40], 14), ALU.is_equal), "dve_done")
                dve.tensor_scalar(DMk[:, :, 1:15], vt, NEG, None, ALU.mult)
                dve.wait_ge(sem("s_turn_kept"), 1)
                dve.wait_ge(sem("s_valued"), 1)
                for q in range(2):
                    for v in range(NKV):
                        rr = slice(32 * v, 32 * v + 32)
                        ins = dve.tensor_copy(oS[rr, q::2, 0, :],
                                              bank[6 + q][rr, :].rearrange("p (a c) -> p a c", a=4)[:, :, v * HD:(v + 1) * HD])
                ins.then_inc(sem("s_imp_kept"), 1)
                for t in range(NT):
                    p = cs[t % 2]
                    p3 = p.rearrange("p (h c) -> p h c", h=NH)
                    m = cm[t % 2]
                    neg = const("cmpneg")[:, t * NCP:(t + 1) * NCP].unsqueeze(1)
                    vis = const("cmp01")[:, t * NCP:(t + 1) * NCP].unsqueeze(1)
                    dve.wait_ge(sem("c_scored"), t + 1)
                    if t >= 2:
                        dve.wait_ge(sem("c_turned"), t - 1)
                    for v in range(NKV):
                        dve.tensor_tensor(p3[:, v * NG:(v + 1) * NG, :],
                                          bank[2 * (t % 2) + v][:, 0:P].rearrange("p (g c) -> p g c", g=NG),
                                          neg.to_broadcast([P, NG, NCP]), ALU.add).then_inc(sem("c_read"), 1)
                    dve.wait_ge(sem("c_read"), 2 * t + 2)
                    step(dve, dve.tensor_reduce(m[:, 0:8], p3, AX, ALU.max, negate=True), "dve_done")
                    dve.tensor_tensor(p3, p3, bc(m[:, 0:8], NCP), ALU.add).then_inc(sem("c_shifted"), 1)
                    dve.wait_ge(sem("c_exp"), t + 1)
                    dve.tensor_tensor(p3, p3, vis.to_broadcast([P, NH, NCP]), ALU.mult).then_inc(sem("c_probs"), 1)
                    dve.wait_ge(sem("c_probs"), t + 1)
                    step(dve, dve.tensor_reduce(m[:, 8:16], p3, AX, ALU.add), "dve_done")
                    step(dve, dve.tensor_scalar(m[:, 8:16], m[:, 8:16], 1e-30, None, ALU.max), "dve_done")
                    step(dve, dve.reciprocal(m[:, 16:24], m[:, 8:16]), "dve_done")
                    step(dve, dve.tensor_tensor(m[:, 16:24], m[:, 16:24],
                                                gate[:, t, :].rearrange("p (h b) -> p h b", b=3)[:, :, 0], ALU.mult), "dve_done")
                    dve.wait_ge(sem("c_valued"), t + 1)
                    dve.tensor_tensor(otm.rearrange("p (h d) -> p h d", d=HD),
                                      bank[5][:, :].rearrange("p (h d) -> p h d", d=HD), bc(m[:, 16:24], HD), ALU.mult
                                      ).then_inc(sem("c_kept"), 1)
                    dve.wait_ge(sem("c_kept"), t + 1)
                    step(dve, dve.tensor_tensor(o_tok[:, t, :], o_tok[:, t, :], otm, ALU.add), "dve_done")

        cut = cutter(R2)
        pastKV = [cut(NPG * 256).rearrange("p (j c) -> p j c", j=NPG) for _ in range(2)]
        winKV = [cut(4 * 256).rearrange("p (j c) -> p j c", j=4) for _ in range(2)]
        kTb = [cut(1536) for _ in range(2)]
        cut = cutter(R1, R_ATT)
        Sb = [cut(1664)[0:NS] for _ in range(2)]
        cut = cutter(R1, R_HI + TT * 512)
        PTb = [cut(14 * NS).rearrange("p (j r) -> p j r", j=14) for _ in range(2)]
        srs = cut(64)[0:NS]
        NSLC = PAST + NS
        PARTS = [j * P for j in range(8)] + [NSLC + j * P for j in range(4)]

        with nc.Block() as block:
            @block.sync
            def _(sp):
                for b in range(NB):
                    if b >= 2:
                        sp.wait_ge(sem("b_valued"), b - 1)
                    for j in range(NPG):
                        pg = sp.value_load(pages[0:1, NPG * b + j:NPG * b + j + 1], min_val=0, max_val=NPOOL - 1)
                        sp.dma_start(pastKV[b % 2][:, j, :],
                                     cache_nsa_kv[bass.ds(l, 1), bass.ds(pg, 1), :, 2:4].rearrange(
                                         "o q r k v d -> (o q r) (k v d)")).then_inc(sem(f"past_loaded{b % 2}"), 16)
                    sp.dma_start(winKV[b % 2], cache_win_kv[bass.ds(l, 1), b].rearrange(
                        "o (j p) k v d -> p (o j) (k v d)", p=P)).then_inc(sem(f"past_loaded{b % 2}"), 16)
                sp.wait_ge(sem("oS_done"), NB)
                for h in range(NH):
                    sp.dma_start(scratch.rearrange("b t h c -> t b h c")[:, :, h, :],
                                 oS[h * DT:(h + 1) * DT].rearrange("p b c d -> p b (c d)")).then_inc(sem("oS_stored"), 16)
                sp.wait_ge(sem("oS_stored"), 16 * NH)
                sp.dma_start(o3, scratch.rearrange("b t h c -> (b t) (h c)")).then_inc(sem("o3_loaded"), 16)

            def past_count(b):
                return 16 * (NPG + 1) * (b // 2 + 1)

            @block.tensor
            def _(pe):
                def turn_keys(b):
                    pe.wait_ge(sem(f"past_loaded{b % 2}"), past_count(b))
                    for i in range(3):
                        if b >= 1:
                            pe.wait_ge(sem("k_kept_act" if i != 1 else "k_kept_dve"), [2 * b - 1, b, 2 * b][i])
                        for j in range(4):
                            n = 4 * i + j
                            src = pastKV[b % 2][:, n, 0:P] if n < 8 else winKV[b % 2][:, n - 8, 0:P]
                            ins = pe.transpose(bank[i][:, j * P:(j + 1) * P], src, ident)
                        ins.then_inc(sem("k_turned"), 1)

                def scores(b):
                    pe.wait_ge(sem("k_kept_act"), 2 * b + 2)
                    pe.wait_ge(sem("k_kept_dve"), b + 1)
                    if b >= 1:
                        pe.wait_ge(sem("oS_done"), b)
                        pe.wait_ge(sem("pT_kept"), 3 * b)
                    q = QD[:, 1, b, :]
                    for i in range(3):
                        pe.matmul(bank[3 + i][0:NS, :], q, kTb[b % 2][:, i * 512:(i + 1) * 512], start=True, stop=True)
                    for i in range(2):
                        ins = pe.matmul(bank[6][0:NS, i * NS:(i + 1) * NS], q, KT[:, i, SEQ:N], start=True, stop=True)
                    ins.then_inc(sem("b_scored"), 1)

                def turn_probs(b):
                    pe.wait_ge(sem("b_probs"), 2 * b + 2)
                    if b >= 1:
                        pe.wait_ge(sem("pT_kept"), 3 * b)
                    for j in range(8):
                        ins = pe.transpose(bank[7][:, j * NS:(j + 1) * NS], Sb[b % 2][:, PARTS[j]:PARTS[j] + P],
                                           ident[0:NS, 0:NS])
                    ins.then_inc(sem("p_turned"), 1)
                    for j in range(8, 12):
                        ins = pe.transpose(bank[6][:, (j - 8) * NS:(j - 7) * NS], Sb[b % 2][:, PARTS[j]:PARTS[j] + P],
                                           ident[0:NS, 0:NS])
                    for i, o in enumerate((PAST, NSLC + WINB)):
                        ins = pe.transpose(bank[6][0:NS, (4 + i) * NS:(5 + i) * NS], Sb[b % 2][:, o:o + NS],
                                           ident[0:NS, 0:NS])
                    ins.then_inc(sem("p_turned"), 1)

                def values(b):
                    pe.wait_ge(sem("pT_kept"), 3 * b + 3)
                    o = bank[3][0:NS, 0:256]
                    for i, (js, V, new) in enumerate(((range(8), pastKV, 12), (range(8, 12), winKV, 13))):
                        oi = o[:, i * P:(i + 1) * P]
                        for j in js:
                            pe.matmul(oi, PTb[b % 2][:, j, :], V[b % 2][:, j - js[0], P:256], start=(j == js[0]), stop=False)
                        ins = pe.matmul(oi, PTb[b % 2][0:NS, new, :], vtok[i][0:NS, NT, :], start=False, stop=True)
                    ins.then_inc(sem("b_valued"), 1)

                turn_keys(0)
                for b in range(NB):
                    scores(b)
                    if b + 1 < NB:
                        turn_keys(b + 1)
                    turn_probs(b)
                    values(b)

            @block.scalar
            def _(act):
                def keep_keys(b):
                    for i in (0, 2):
                        act.wait_ge(sem("k_turned"), 3 * b + i + 1)
                        if b >= 2:
                            act.wait_ge(sem("b_scored"), b - 1)
                        act.activation(kTb[b % 2][:, i * 512:(i + 1) * 512], bank[i][:, :], ACT.Copy
                                       ).then_inc(sem("k_kept_act"), 1)

                keep_keys(0)
                for b in range(NB):
                    if b + 1 < NB:
                        keep_keys(b + 1)
                    for i, (lo, hi) in enumerate(((0, NSLC), (NSLC, 1664))):
                        act.wait_ge(sem("b_maxed"), 2 * b + i + 1)
                        act.activation(Sb[b % 2][:, lo:hi], Sb[b % 2][:, lo:hi], ACT.Exp, bias=srs[:, 2 * b + i:2 * b + i + 1],
                                       accum_out=srs[:, 16 + 2 * b + i:17 + 2 * b + i]).then_inc(sem("b_probs"), 1)
                    act.wait_ge(sem("p_turned"), 2 * b + 1)
                    if b >= 2:
                        act.wait_ge(sem("b_valued"), b - 1)
                    act.activation(PTb[b % 2][:, 0:8, :], bank[7][:, :].rearrange("p (j r) -> p j r", j=8), ACT.Copy
                                   ).then_inc(sem("pT_kept"), 1)
                    act.wait_ge(sem("p_turned"), 2 * b + 2)
                    act.activation(PTb[b % 2][:, 8:12, :], bank[6][:, 0:256].rearrange("p (j r) -> p j r", j=4), ACT.Copy
                                   ).then_inc(sem("pT_kept"), 1)
                    act.activation(PTb[b % 2][0:NS, 12:14, :], bank[6][0:NS, 256:384].rearrange("p (j r) -> p j r", j=2),
                                   ACT.Copy).then_inc(sem("pT_kept"), 1)

            @block.vector
            def _(dve):
                def keep_keys(b):
                    dve.wait_ge(sem("k_turned"), 3 * b + 2)
                    if b >= 2:
                        dve.wait_ge(sem("b_scored"), b - 1)
                    dve.tensor_copy(kTb[b % 2][:, 512:1024], bank[1][:, :]).then_inc(sem("k_kept_dve"), 1)

                keep_keys(0)
                for b in range(NB):
                    s = Sb[b % 2]
                    new = const("newneg", NS)[:, b * NS:(b + 1) * NS]
                    dve.wait_ge(sem("b_scored"), b + 1)
                    if b >= 2:
                        dve.wait_ge(sem("p_turned"), 2 * (b - 1))
                    for i in range(2):
                        dve.tensor_tensor(s[:, i * 512:(i + 1) * 512].rearrange("p (j c) -> p j c", c=64),
                                          bank[3 + i][0:NS, :].rearrange("p (j c) -> p j c", c=64),
                                          bc(DMk[:, b, 8 * i:8 * i + 8], 64), ALU.add)
                    step(dve, dve.tensor_tensor(s[:, PAST:NSLC], bank[6][0:NS, 0:NS], new, ALU.add), "dve_done")
                    dve.tensor_reduce(srs[:, 2 * b:2 * b + 1], s[:, 0:NSLC], AX, ALU.max, negate=True
                                      ).then_inc(sem("b_maxed"), 1)
                    dve.tensor_tensor(s[:, NSLC:NSLC + DT], bank[5][0:NS, 0:DT], const("winneg", NS), ALU.add)
                    dve.tensor_copy(s[:, NSLC + DT:NSLC + WINB], bank[5][0:NS, DT:WINB])
                    step(dve, dve.tensor_tensor(s[:, NSLC + WINB:1664], bank[6][0:NS, NS:2 * NS], new, ALU.add), "dve_done")
                    dve.tensor_reduce(srs[:, 2 * b + 1:2 * b + 2], s[:, NSLC:1664], AX, ALU.max, negate=True
                                      ).then_inc(sem("b_maxed"), 1)
                    if b + 1 < NB:
                        keep_keys(b + 1)
                    dve.wait_ge(sem("b_probs"), 2 * b + 2)
                    step(dve, dve.reciprocal(srs[:, 32 + 2 * b:34 + 2 * b], srs[:, 16 + 2 * b:18 + 2 * b]), "dve_done")
                    dve.wait_ge(sem("b_valued"), b + 1)
                    for v in range(NKV):
                        rr = slice(32 * v, 32 * v + 32)
                        ins = dve.tensor_tensor(oS[rr, b, 1:3, :],
                                                bank[3][rr, 0:256].rearrange("p (i c) -> p i c", i=2)[:, :, v * HD:(v + 1) * HD],
                                                bc(srs[rr, 32 + 2 * b:34 + 2 * b], HD), ALU.mult)
                    ins.then_inc(sem("oS_done"), 1)
                dve.wait_ge(sem("o3_loaded"), 16)
                o4 = o3.rearrange("p (h b d) -> p h b d", h=NH, b=3)
                step(dve, dve.tensor_tensor(o3.rearrange("p (n d) -> p n d", d=HD), o3.rearrange("p (n d) -> p n d", d=HD),
                                            bc(gate[0:NS, NT, :], HD), ALU.mult), "dve_done")
                dst = o_tok[0:NS, NT, :].rearrange("p (h d) -> p h d", h=NH)
                step(dve, dve.tensor_tensor(dst, o4[:, :, 0, :], o4[:, :, 1, :], ALU.add), "dve_done")
                step(dve, dve.tensor_tensor(dst, dst, o4[:, :, 2, :], ALU.add), "dve_done")

        with nc.Block() as block:
            @block.tensor
            def _(pe):
                for t in range(TT):
                    r = rows_of(t)
                    for c in range(4):
                        ins = pe.transpose(bank[t][:, c * r:(c + 1) * r], o_tok[0:r, t, c * P:(c + 1) * P], ident[0:r, 0:r])
                    ins.then_inc(sem("o_turned"), 1)

            @block.scalar
            def _(act):
                for t in range(TT):
                    r = rows_of(t)
                    act.wait_ge(sem("o_turned"), t + 1)
                    act.activation(OT[:, 0:4, t * P:t * P + r], bank[t][:, 0:4 * r].rearrange("p (c n) -> p c n", c=4),
                                   ACT.Copy)

        mix_scope.close()

        mlp_scope = ExitStack()
        S7 = Split(mlp_scope, "m_")
        UH, UL = (mlp_scope.enter_context(nc.sbuf_tensor(n, [P, KC * N], F32R))[:, :].rearrange("p (c n) -> p c n", c=KC)
                  for n in ("UH", "UL"))
        sq2_ = mlp_scope.enter_context(nc.sbuf_tensor("sq2", [P, 4 * N], F32))
        sq2 = [sq2_[:, i * N:(i + 1) * N] for i in range(2)]
        relu = [sq2_[:, 2 * N + i * HALF:2 * N + (i + 1) * HALF] for i in range(4)]
        G7 = [("out", 0, g) for g in range(4)]
        for q in range(4):
            G7 += [(kind, q, g) for kind in ("up", "down") for g in range(4)]
        U7 = [(kind, q, 2 * g + m, s, i) for i, (kind, q, g) in enumerate(G7) for m in range(2) for s in range(2)]
        NOUT = 16
        FQ = DFF // 4
        RANK = [sum(U7[x][0] == U7[u][0] or (U7[u][0] != "up" and U7[x][0] != "up") for x in range(u + 1))
                for u in range(len(U7))]

        with nc.Block() as block:
            @block.sync
            def _(sp):
                for i, (kind, q, g) in enumerate(G7):
                    cols = slice(g * GW, (g + 1) * GW)
                    if kind == "out":
                        src = w_out[bass.ds(l, 1)].rearrange("o (c p) n -> p (o c) n", p=P)[:, :, cols]
                    elif kind == "up":
                        src = w_up[bass.ds(l, 1)].rearrange("o (c p) n -> p (o c) n", p=P)[
                            :, :, q * FQ + g * GW:q * FQ + (g + 1) * GW]
                    else:
                        src = w_down[bass.ds(l, 1)].rearrange("o (c p) n -> p (o c) n", p=P)[:, KC * q:KC * (q + 1), cols]
                    load_granule(sp, S7, i, src)

            @block.gpsimd
            def _(pool):
                for i in range(len(G7)):
                    split_lo(pool, S7, i, GW)

            @block.tensor
            def _(pe):
                for u, (kind, q, m, s, i) in enumerate(U7):
                    if u == 0:
                        pe.wait_ge(sem("mix_lo"), KC)
                    if u == NOUT:
                        norm_products(pe, "n2", sq2)
                        pe.wait_ge(sem("n2_out"), KC)
                    if kind == "down" and m == 0 and s == 0:
                        pe.wait_ge(sem("relu_lo"), 16 * (q + 1))
                    pe.wait_ge(sem("m_w_lo"), i + 1)
                    if u >= 6:
                        pe.wait_ge(sem("m_relued" if U7[u - 6][0] == "up" else "m_added"), RANK[u - 6])
                    ah, al = (UH, UL) if kind == "down" else (S7.ah, S7.al)
                    feature_product(pe, bank[2 + u % 6][:, 0:HALF], S7, i, GW, slice(m % 2 * P, (m % 2 + 1) * P), ah, al,
                                    halves(s)).then_inc(sem("m_done"), 1)

            def relu_hi(act, n):
                act.wait_ge(sem("relu_squared"), n + 1)
                q = n // 16
                if q >= 1 and n % 16 == 0:
                    act.wait_ge(sem("m_done"), NOUT + 32 * q)
                act.activation(UH[:, n % 16 // 2, halves(n % 2)], relu[n % 4], ACT.Copy).then_inc(sem("relu_hi"), 1)

            @block.scalar
            def _(act):
                for i in range(2):
                    split_hi(act, S7, i, GW, 0)
                for c in range(KC):
                    act.activation(S7.ah[:, c, :], OT[:, c, :], ACT.Copy).then_inc(sem("mix_hi"), 1)
                for u, (kind, q, m, s, i) in enumerate(U7):
                    if u == NOUT:
                        norm_scalar(act, "n2", sq2, S7, "m_added")
                    if kind == "up":
                        act.wait_ge(sem("m_done"), u + 1)
                        n = RANK[u] - 1
                        if n >= 4:
                            act.wait_ge(sem("relu_lo"), n - 3)
                        act.activation(relu[n % 4], bank[2 + u % 6][:, 0:HALF], ACT.Relu).then_inc(sem("m_relued"), 1)
                        if n % 16 >= 1:
                            relu_hi(act, n - 1)
                        if n % 16 == 15:
                            relu_hi(act, n)
                    if u % 4 == 3 and i + 2 < len(G7):
                        split_hi(act, S7, i + 2, GW, u + 1)

            @block.vector
            def _(dve):
                for c in range(KC):
                    dve.wait_ge(sem("mix_hi"), c + 1)
                    dve.tensor_tensor(S7.al[:, c, :], OT[:, c, :], S7.ah[:, c, :].bitcast(F32), ALU.subtract
                                      ).then_inc(sem("mix_lo"), 1)

                def relu_lo(n):
                    dve.wait_ge(sem("relu_hi"), n + 1)
                    x = (slice(None), n % 16 // 2, halves(n % 2))
                    dve.tensor_tensor(UL[x], relu[n % 4], UH[x].bitcast(F32), ALU.subtract).then_inc(sem("relu_lo"), 1)

                for u, (kind, q, m, s, i) in enumerate(U7):
                    if u == NOUT:
                        norm_vector(dve, "n2", sq2, S7, G_MLP)
                    if kind == "up":
                        n = RANK[u] - 1
                        dve.wait_ge(sem("m_relued"), n + 1)
                        dve.tensor_tensor(relu[n % 4], relu[n % 4], relu[n % 4], ALU.mult).then_inc(sem("relu_squared"), 1)
                        if n % 16 >= 1:
                            relu_lo(n - 1)
                        if n % 16 == 15:
                            relu_lo(n)
                    else:
                        dve.wait_ge(sem("m_done"), u + 1)
                        if kind == "down" and q >= 1:
                            dve.wait_ge(sem("m_added"), RANK[u] - 16)
                        x = XT[:, m, halves(s)]
                        dve.tensor_tensor(x, x, bank[2 + u % 6][:, 0:HALF], ALU.add).then_inc(sem("m_added"), 1)

        mlp_scope.close()
        clear_semaphores()
        layers.close()

        YU = [(t, q) for t in range(TT) for q in range(2)]
        xout = [ctx.enter_context(nc.sbuf_tensor(f"xout{i}", [P, SLOT], F32)) for i in range(2)]
        Y = [xout[0][:, :].rearrange("p (t c) -> p t c", t=NT), xout[1][:, 0:DM].rearrange("p (t c) -> p t c", t=1)]
        with nc.Block() as block:
            @block.tensor
            def _(pe):
                for u, (t, q) in enumerate(YU):
                    r = rows_of(t)
                    if u >= 8:
                        pe.wait_ge(sem("y_kept"), u - 7)
                    for c in range(4):
                        ins = pe.transpose(bank[u % 8][0:r, c * P:(c + 1) * P], XT[:, 4 * q + c, t * P:t * P + r], ident)
                    ins.then_inc(sem("y_turned"), 1)

            @block.vector
            def _(dve):
                for u, (t, q) in enumerate(YU):
                    r = rows_of(t)
                    dve.wait_ge(sem("y_turned"), u + 1)
                    dst = (Y[0][:, t] if t < NT else Y[1][0:NS, 0])[:, q * 512:(q + 1) * 512]
                    dve.tensor_copy(dst, bank[u % 8][0:r, :]).then_inc(sem("y_kept"), 1)

            @block.sync
            def _(sp):
                for t in range(NT):
                    sp.wait_ge(sem("y_kept"), 2 * t + 2)
                    sp.dma_start(y_prompt[0, t * P:(t + 1) * P, :], Y[0][:, t]).then_inc(sem("y_stored"), 16)
                sp.wait_ge(sem("y_kept"), 2 * TT)
                sp.dma_start(y_sample.rearrange("b t c -> (b t) c"), Y[1][0:NS, 0]).then_inc(sem("y_stored"), 16)
                sp.wait_ge(sem("y_stored"), 16 * TT)


_INS = ['x_prompt', 'x_sample', 'cache_nsa_kv', 'cache_win_kv', 'state_hgrn', 'page_table', 'attn_norm_g', 'w_in',
        'q_norm_g', 'k_norm_g', 'cmp_pos', 'cmp_w1', 'cmp_b1', 'cmp_w2', 'hg_lb_param', 'hg_norm_g', 'w_out',
        'mlp_norm_g', 'w_up', 'w_down']
_OUTS = [(1, SEQ, DM), (NB, DT, DM), (DEPTH, 1, SEQ, 4, NKV, HD), (DEPTH, 1, SEQ, 2, NKV, HD),
         (DEPTH, 1, HH, P, P), (DEPTH, NB, DT, 4, NKV, HD), (DEPTH, NB, DT, 2, NKV, HD), (DEPTH, NB, HH, P, P)]


def kernel(**inputs):
    import concourse.bacc as bacc
    from concourse.bass_utils import run_bass_kernel_spmd

    nc = bacc.Bacc("TRN2", target_bir_lowering=False, num_devices=1)
    arrays, args = {}, []
    for name in _INS + ['constants']:
        a = CONSTANTS if name == 'constants' else np.ascontiguousarray(inputs[name])
        arrays[f"in_{name}"] = a
        args.append(nc.dram_tensor(f"in_{name}", a.shape, mybir.dt.from_np(a.dtype), kind="ExternalInput").ap())
    for i, shape in enumerate(_OUTS):
        args.append(nc.dram_tensor(f"out_{i}", shape, F32, kind="ExternalOutput").ap())
    build(nc, *args)
    r = run_bass_kernel_spmd(nc, [arrays], core_ids=[0])
    return tuple(r.results[0][f"out_{i}"] for i in range(len(_OUTS)))
```

```python
from contextlib import ExitStack

import numpy as np

import concourse.bass as bass
from concourse import mybir

F32 = mybir.dt.float32
F32R = mybir.dt.float32r
I32 = mybir.dt.int32
U32 = mybir.dt.uint32
ALU = mybir.AluOpType
ACT = mybir.ActivationFunctionType
AX = mybir.AxisListType.X

P = 128
DM = 1024
KC = DM // P
SEQ = 512
NB = 8
DT = 8
NS = NB * DT
N = SEQ + NS
HALF = N // 2
NT = SEQ // P
TT = NT + 1
DEPTH = 2
HD = 64
NH = 8
NKV = 2
NG = NH // NKV
PAST = 1024
PAGE = 128
NPG = PAST // PAGE
HH = 4
CH = 32
NCK = P // CH
WINB = 512
DFF = 4096
FFC = DFF // P
CST = 16
CHID = 256
NCP = SEQ // CST
NCS = PAST // CST
NCC = NB * NCS
NCALL = NCC + NCP
SLOT = 4096
EPS = 1e-6
NEG = -1e30
C_Q, C_KV, C_WIN, C_HQ, C_HF, C_HI, C_HG, C_END = 0, 512, 1024, 1304, 1816, 2328, 2840, 3352
WINW = C_HQ - C_WIN

CONST_W = {}


def _constants():
    cols = []

    def put(name, a):
        a = np.asarray(a, np.float32).reshape(a.shape[0], -1)
        full = np.zeros((P, a.shape[1]), np.float32)
        full[:a.shape[0]] = a
        CONST_W[name] = (sum(c.shape[1] for c in cols), a.shape[1])
        cols.append(full)

    i = np.arange(P)
    put("ident", np.eye(P))
    put("ones", np.ones((P, P)))
    put("ones64", (i[:, None] // HD == i[None] // HD))
    put("causal", np.where(i[None] > i[:, None], NEG, 0.0))
    put("hgmask", (i[:, None] // CH == i[None] // CH) & (i[:, None] <= i[None]))
    j = np.arange(NS)
    put("hgmask8", (j[:, None] // DT == j[None] // DT) & (j[:, None] <= j[None]))
    pos = np.concatenate([np.arange(SEQ), PAST + np.tile(np.arange(DT), NB), np.zeros(P - NS)]).astype(np.float32)
    inv = (np.float32(10000.0) ** (-np.arange(HD // 2, dtype=np.float32) / np.float32(HD // 2))).astype(np.float32)
    ang = (pos[:, None] * inv[None]).astype(np.float32).reshape(TT, P, HD // 2).transpose(1, 0, 2)
    put("cos", np.cos(ang.astype(np.float64)))
    put("sin", np.sin(ang.astype(np.float64)))
    c = np.arange(NCP)
    q = np.arange(SEQ).reshape(NT, P).T
    seen = (c[None, None] * CST + 2 * CST - 1 <= q[:, :, None]) & (c < NCP - 1)
    put("cmpneg", np.where(seen, 0.0, NEG))
    put("cmp01", seen)
    rows = np.arange(P)
    par_, hd, t = rows // (NH * DT), rows // DT % NH, rows % DT
    own = np.arange(NB // 2)[None, :, None, None] * 2 + par_[:, None, None, None] == np.arange(NB)[None, None, :, None]
    new = own & (np.arange(DT)[None, None, None] <= t[:, None, None, None])
    put("newneg", np.where(new, 0.0, NEG))
    put("winneg", np.where(np.arange(DT)[None] > t[:, None], 0.0, NEG))
    put("groupsum", (rows[:, None] // (NG * DT) == rows[None] // (NG * DT)) & (t[:, None] == t[None]))
    put("rowsel", j[:, None] % (2 * DT) == (par_ * DT + t)[None])
    put("pair", j[:, None] // (2 * DT) == np.arange(NB // 2)[None])
    put("head", hd[:, None] == np.arange(NH)[None])
    put("blkidx", np.tile(np.arange(16), (P, 1)))
    put("chunk", (i[:, None] // CH == np.arange(NCK)[None]))
    put("batch", (j[:, None] // DT == np.arange(NB)[None]))
    n = np.arange(N)
    put("scan", np.tile(np.where(n < SEQ, n % CH != 0, (n - SEQ) % DT != 0), (P, 1)))
    return np.concatenate(cols, axis=1)


CONSTANTS = _constants()


def rows_of(t):
    return P if t < NT else NS


def build(nc, x_prompt, x_sample, cache_nsa_kv, cache_win_kv, state_hgrn, page_table,
          attn_norm_g, w_in, q_norm_g, k_norm_g, cmp_pos, cmp_w1, cmp_b1, cmp_w2,
          hg_lb_param, hg_norm_g, w_out, mlp_norm_g, w_up, w_down, constants,
          y_prompt, y_sample, p_nsa, p_win, p_hg, s_nsa, s_win, s_hg):
    NPOOL = cache_nsa_kv.shape[1]
    with ExitStack() as ctx:
        def sb(name, cols, dt=F32):
            return ctx.enter_context(nc.sbuf_tensor(name, [P, cols], dt))

        sems = {}
        sem_scope = ctx.enter_context(ExitStack())

        def sem(name):
            if name not in sems:
                sems[name] = sem_scope.enter_context(nc.semaphore(name))
            return sems[name]

        made = {}

        def step(eng, ins, name):
            made[name] = made.get(name, 0) + 1
            ins.then_inc(sem(name), 1)
            eng.wait_ge(sem(name), made[name])

        cst = sb("cst", CONSTANTS.shape[1])
        pages = ctx.enter_context(nc.sbuf_tensor("pages", [1, NB * NPG], I32))
        XT = sb("XT", KC * N)[:, :].rearrange("p (c n) -> p c n", c=KC)
        OT_ = sb("OT", KC * N)
        OT = OT_[:, :].rearrange("p (c n) -> p c n", c=KC)
        rstd = sb("rstd", N)
        par_all = sb("par_all", DEPTH * 40)[:, :].rearrange("p (l c) -> p l c", l=DEPTH)
        par = sb("par", 40)
        qkr = sb("qkr", 60)
        lbt = sb("lbt", 40)
        eps = sb("epsc", 1)[:, 0:1]
        one = sb("onec", 1)[:, 0:1]
        gain = sb("gain", 3 * HD)
        bank = [ctx.enter_context(nc.psum_tensor(f"bank{i}", [P, 512], F32)) for i in range(8)]

        def cutter(tensor, start=0):
            at = [start]

            def cut(n):
                at[0] += n
                assert at[0] <= tensor.shape[1], at
                return tensor[:, at[0] - n:at[0]]
            return cut

        def const(name, rows=P):
            o, w = CONST_W[name]
            return cst[0:rows, o:o + w]

        ident, ones, ones64 = const("ident"), const("ones"), const("ones64")
        G_ATTN, G_MLP, G_HG, G_KC, P_B1, P_LBA, P_OM, P_LNOM, P_HB = 0, 8, 16, 17, 18, 22, 26, 30, 34

        def col(i):
            return par[:, i:i + 1]

        def bc(ap, n):
            return ap.unsqueeze(2).to_broadcast([ap.shape[0], ap.shape[1], n])

        P_LB, NROW = P_LBA, P_LBA + HH
        setup_scope = ExitStack()
        xin = [setup_scope.enter_context(nc.sbuf_tensor(f"xin{i}", [P, SLOT], F32)) for i in range(2)]
        rows = OT_[0:DEPTH * NROW, 0:P]

        with nc.Block() as block:
            @block.sync
            def _(sp):
                sp.dma_start(xin[0][:, :].rearrange("p (t c) -> p t c", t=NT),
                             x_prompt[0].rearrange("(t p) c -> p t c", p=P)).then_inc(sem("x_loaded"), 16)
                sp.dma_start(xin[1][0:NS, 0:DM], x_sample.rearrange("b t c -> (b t) c")).then_inc(sem("x_loaded"), 16)
                sp.dma_start(cst[:, :], constants).then_inc(sem("const_loaded"), 16)
                sp.dma_start(pages[:, :], page_table.rearrange("(o a) b -> o (a b)", o=1)).then_inc(sem("pages_loaded"), 16)
                sp.wait_ge(sem("pages_loaded"), 16)

            @block.scalar
            def _(act):
                for l in range(DEPTH):
                    r = l * NROW
                    for src, w, c0 in ((attn_norm_g[l].rearrange("(c p) -> c p", p=P), KC, G_ATTN),
                                       (mlp_norm_g[l].rearrange("(c p) -> c p", p=P), KC, G_MLP),
                                       (hg_norm_g[l].rearrange("(c p) -> c p", p=P), 1, G_HG),
                                       (cmp_b1[l].rearrange("k (c p) -> (k c) p", p=P), 4, P_B1),
                                       (hg_lb_param[l].rearrange("(c p) -> c p", p=P), HH, P_LB)):
                        act.dma_start(rows[r + c0:r + c0 + w, :], src).then_inc(sem("rows_loaded"), 16)
                    for kv in range(NKV):
                        act.dma_start(rows[r + G_KC:r + G_KC + 1, kv * HD:(kv + 1) * HD], k_norm_g[l, 0:1, :]
                                      ).then_inc(sem("rows_loaded"), 16)
                act.wait_ge(sem("lb_centred"), 1)
                act.activation(lbt[:, 16:24], lbt[:, 16:24], ACT.Exp).then_inc(sem("lb_exp"), 1)
                act.wait_ge(sem("lb_ready"), 1)
                act.activation(lbt[:, 32:40], lbt[:, 32:40], ACT.Ln).then_inc(sem("lb_ln"), 1)

            @block.tensor
            def _(pe):
                pe.wait_ge(sem("const_loaded"), 16)
                pe.wait_ge(sem("x_loaded"), 32)
                for c in range(KC):
                    for t in range(NT):
                        ins = pe.transpose(bank[c % 4][:, t * P:(t + 1) * P], xin[0][:, t * DM + c * P:t * DM + (c + 1) * P],
                                           ident)
                    ins.then_inc(sem("x_turned"), 1)
                    if c >= 3 and c < KC - 1:
                        pe.wait_ge(sem("x_kept"), c - 2)
                for c in range(KC):
                    ins = pe.transpose(bank[4][:, c * NS:(c + 1) * NS], xin[1][0:NS, c * P:(c + 1) * P], ident[0:NS, 0:NS])
                ins.then_inc(sem("x_turned"), 1)
                pe.wait_ge(sem("rows_loaded"), 16 * 7 * DEPTH)
                pe.transpose(bank[5][:, 0:DEPTH * NROW], rows, ident[0:DEPTH * NROW, 0:DEPTH * NROW]
                             ).then_inc(sem("rows_turned"), 1)

            @block.vector
            def _(dve):
                dve.memset(eps, EPS)
                dve.memset(one, 1.0)
                dve.memset(par_all[:, :, P_HB:40], 0.0).then_inc(sem("cleared"), 1)
                for c in range(KC):
                    dve.wait_ge(sem("x_turned"), c + 1)
                    dve.tensor_copy(XT[:, c, 0:SEQ], bank[c % 4][:, :]).then_inc(sem("x_kept"), 1)
                dve.wait_ge(sem("x_turned"), KC + 1)
                dve.tensor_copy(XT[:, :, SEQ:N], bank[4][:, :].rearrange("p (c n) -> p c n", c=KC)
                                ).then_inc(sem("x_kept"), 1)
                dve.wait_ge(sem("rows_turned"), 1)
                turned = bank[5][:, 0:DEPTH * NROW].rearrange("p (l c) -> p l c", l=DEPTH)
                dve.tensor_copy(par_all[:, :, 0:P_LB], turned[:, :, 0:P_LB])
                step(dve, dve.tensor_copy(lbt[:, 0:8].rearrange("p (l c) -> p l c", l=DEPTH), turned[:, :, P_LB:NROW]),
                     "dve_done")
                step(dve, dve.tensor_tensor(lbt[:, 8:12], lbt[:, 0:4], lbt[:, 4:8], ALU.max), "dve_done")
                step(dve, dve.tensor_tensor(lbt[:, 16:20], lbt[:, 0:4], lbt[:, 8:12], ALU.subtract), "dve_done")
                step(dve, dve.tensor_tensor(lbt[:, 20:24], lbt[:, 4:8], lbt[:, 8:12], ALU.subtract), "lb_centred")
                dve.wait_ge(sem("lb_exp"), 1)
                step(dve, dve.tensor_tensor(lbt[:, 8:12], lbt[:, 16:20], lbt[:, 20:24], ALU.add), "dve_done")
                step(dve, dve.reciprocal(lbt[:, 12:16], lbt[:, 8:12]), "dve_done")
                step(dve, dve.tensor_tensor(lbt[:, 16:20], lbt[:, 16:20], lbt[:, 12:16], ALU.mult), "dve_done")
                step(dve, dve.tensor_tensor(lbt[:, 20:24], lbt[:, 20:24], lbt[:, 12:16], ALU.mult), "dve_done")
                step(dve, dve.tensor_tensor(lbt[:, 24:28], lbt[:, 16:20], lbt[:, 20:24], ALU.add), "dve_done")
                step(dve, dve.tensor_tensor(lbt[:, 24:28], lbt[:, 24:28], lbt[:, 16:20], ALU.subtract), "dve_done")
                step(dve, dve.tensor_scalar(lbt[:, 28:32], lbt[:, 24:28], -1.0, 1.0, ALU.mult, ALU.add), "dve_done")
                step(dve, dve.tensor_scalar(lbt[:, 32:36], lbt[:, 24:28], 1e-15, None, ALU.max), "dve_done")
                step(dve, dve.tensor_scalar(lbt[:, 36:40], lbt[:, 28:32], 1e-15, None, ALU.max), "lb_ready")
                dve.wait_ge(sem("lb_ln"), 1)
                for src, ln in ((24, 32), (28, 36)):
                    step(dve, dve.tensor_scalar(lbt[:, 8:12], lbt[:, src:src + 4], 1e-15, NEG, ALU.is_lt, ALU.mult),
                         "dve_done")
                    step(dve, dve.tensor_tensor(lbt[:, ln:ln + 4], lbt[:, ln:ln + 4], lbt[:, 8:12], ALU.add), "dve_done")
                dve.tensor_copy(par_all[:, 1, P_LBA:P_LBA + 4], lbt[:, 32:36])
                dve.tensor_copy(par_all[:, 1, P_OM:P_OM + 4], lbt[:, 28:32])
                dve.tensor_copy(par_all[:, 1, P_LNOM:P_LNOM + 4], lbt[:, 36:40])
                dve.memset(par_all[:, 0, P_LBA:P_LBA + 4], NEG)
                dve.memset(par_all[:, 0, P_OM:P_OM + 4], 1.0)
                dve.memset(par_all[:, 0, P_LNOM:P_LNOM + 4], 0.0)

        setup_scope.close()

        GW = 256
        RAW = sb("RAW", 2 * KC * GW)

        class Split:

            def __init__(self, scope, name):
                def tile(n, cols, dt):
                    return scope.enter_context(nc.sbuf_tensor(name + n, [P, cols], dt))
                self.name = name
                self.raw = [RAW[:, i * KC * GW:(i + 1) * KC * GW] for i in range(2)]
                self.wh = [tile(f"wh{i}", KC * GW, F32R) for i in range(2)]
                self.wl = [tile(f"wl{i}", KC * GW, F32R) for i in range(2)]
                self.ah = tile("ah", KC * N, F32R)[:, :].rearrange("p (c n) -> p c n", c=KC)
                self.al = tile("al", KC * N, F32R)[:, :].rearrange("p (c n) -> p c n", c=KC)

            def granule(self, tiles, i, w):
                return tiles[i % 2][:, 0:KC * w].rearrange("p (c n) -> p c n", c=KC)

        def load_granule(sp, S, i, src):
            if i >= 2:
                sp.wait_ge(sem(S.name + "w_lo"), i - 1)
            sp.dma_start(S.granule(S.raw, i, src.shape[2]), src).then_inc(sem(S.name + f"w_raw{i % 2}"), 16)

        def split_hi(act, S, i, w, used):
            act.wait_ge(sem(S.name + f"w_raw{i % 2}"), 16 * (i // 2 + 1))
            if i >= 2:
                act.wait_ge(sem(S.name + "done"), used)
            act.activation(S.granule(S.wh, i, w), S.granule(S.raw, i, w), ACT.Copy).then_inc(sem(S.name + "w_hi"), 1)

        def split_lo(pool, S, i, w):
            pool.wait_ge(sem(S.name + "w_hi"), i + 1)
            pool.tensor_tensor(S.granule(S.wl, i, w), S.granule(S.raw, i, w), S.granule(S.wh, i, w).bitcast(F32),
                               ALU.subtract).then_inc(sem(S.name + "w_lo"), 1)

        def feature_product(pe, out, S, i, w, cols, ah, al, n, operand=None):
            wh, wl = S.granule(S.wh, i, w), S.granule(S.wl, i, w)
            for c in range(KC):
                if operand:
                    pe.wait_ge(sem(operand[0]), operand[1] + 2 * c)
                pe.matmul(out, wh[:, c, cols], ah[:, c, n], start=(c == 0), stop=False)
                pe.matmul(out, wh[:, c, cols], al[:, c, n], start=False, stop=False)
                ins = pe.matmul(out, wl[:, c, cols], ah[:, c, n], start=False, stop=(c == KC - 1))
            return ins

        def keep_warm(pe, out, n):
            pe.matmul(out[:, 0:n], ident, cst[:, 0:n], start=True, stop=True)

        def first_products(pe, banks, S, i, w, done, counts):
            wh, wl = S.granule(S.wh, i, w), S.granule(S.wl, i, w)
            for c in range(KC):
                pe.wait_ge(sem(done), counts(c))
                for u in range(4):
                    out, cols, n = banks[u][:, 0:HALF], slice(u // 2 * P, (u // 2 + 1) * P), halves(u % 2)
                    pe.matmul(out, wh[:, c, cols], S.ah[:, c, n], start=(c == 0), stop=False)
                    pe.matmul(out, wh[:, c, cols], S.al[:, c, n], start=False, stop=False)
                    ins = pe.matmul(out, wl[:, c, cols], S.ah[:, c, n], start=False, stop=(c == KC - 1))
                    if c == KC - 1:
                        ins.then_inc(sem(S.name + "done"), 1)

        def halves(s):
            return slice(s * HALF, (s + 1) * HALF)

        def exp_ln_tables(act):
            act.preload_act_table_set("natural_log_exp_and_others")

        def square(act, name, sq, c):
            if c >= 2:
                act.wait_ge(sem(name + "_added"), max(c - 2, 1))
            act.activation(sq[c % 2], XT[:, c, :], ACT.Square).then_inc(sem(name + "_squared"), 1)

        def add_square(dve, name, sq, c):
            dve.wait_ge(sem(name + "_squared"), c + 1)
            dve.tensor_tensor(rstd[:, :], sq[0] if c == 1 else rstd[:, :], sq[c % 2], ALU.add
                              ).then_inc(sem(name + "_added"), 1)
            dve.wait_ge(sem(name + "_added"), c)

        def norm_products(pe, name):
            pe.wait_ge(sem(name + "_added"), KC - 1)
            for s in range(2):
                ins = pe.matmul(bank[s][:, 0:HALF], ones, rstd[:, halves(s)], start=True, stop=True)
            ins.then_inc(sem(name + "_summed"), 1)

        def norm_scalar(act, name, sq, S):
            act.wait_ge(sem(name + "_summed"), 1)
            for s in range(2):
                act.activation(rstd[:, halves(s)], bank[s][:, 0:HALF], ACT.Ln, bias=eps, scale=1.0 / DM
                               ).then_inc(sem(name + "_ln"), 1)
            act.wait_ge(sem(name + "_ln"), 2)
            act.activation(rstd[:, :], rstd[:, :], ACT.Exp, scale=-0.5).then_inc(sem(name + "_rstd"), 1)
            for c in range(KC):
                act.wait_ge(sem(name + "_normed"), c + 1)
                act.activation(S.ah[:, c, :], sq[c % 2], ACT.Copy).then_inc(sem(name + "_hi"), 1)

        def norm_vector(dve, name, sq, S, g):
            dve.wait_ge(sem(name + "_rstd"), 1)
            for c in range(KC + 1):
                if c < KC:
                    if c >= 2:
                        dve.wait_ge(sem(name + "_out"), c - 1)
                    dve.scalar_tensor_tensor(sq[c % 2], XT[:, c, :], col(g + c), rstd[:, :], ALU.mult, ALU.mult
                                             ).then_inc(sem(name + "_normed"), 1)
                if c >= 1:
                    dve.wait_ge(sem(name + "_hi"), c)
                    dve.tensor_tensor(S.al[:, c - 1, :], sq[(c - 1) % 2], S.ah[:, c - 1, :].bitcast(F32), ALU.subtract
                                      ).then_inc(sem(name + "_out"), 1)
        def clear_semaphores():
            with nc.Block() as block:
                @block.gpsimd
                def _(pool):
                    for s in sems.values():
                        pool.sem_clear(s)
            made.clear()

        clear_semaphores()
        sem_scope.close()
        sems.clear()
        layers = ctx.enter_context(ExitStack())
        l = layers.enter_context(nc.Fori(0, DEPTH))

        R1_N, R2_N = 18400, 9280
        mix_scope = ExitStack()
        R1 = mix_scope.enter_context(nc.sbuf_tensor("R1", [P, R1_N], F32))
        cut = cutter(R1)
        kv_tok = cut(TT * 512).rearrange("p (t c) -> p t c", t=TT)
        win_tok = cut(TT * WINW).rearrange("p (t c) -> p t c", t=TT)
        R_HI = TT * 512 + TT * WINW
        hi_tok = cut(TT * 512).rearrange("p (t c) -> p t c", t=TT)
        q_tok = cut(TT * 512).rearrange("p (t c) -> p t c", t=TT)
        R_HG = R_HI + 2 * TT * 512
        hq = cut(HH * N).rearrange("p (h n) -> p h n", h=HH)
        hf = cut(HH * N).rearrange("p (h n) -> p h n", h=HH)
        hg = cut(HH * N).rearrange("p (h n) -> p h n", h=HH)
        kd = cut(HH * N).rearrange("p (h n) -> p h n", h=HH)
        dec = cut(HH * 24).rearrange("p (h n) -> p h n", h=HH)
        tmp = [OT_[:, i * N:(i + 1) * N] for i in range(7)]
        sq1 = [kd[:, i, :] for i in range(2)]

        FT = [hf, hq, hg]
        TOK = [(hi_tok, C_HI, GW), (q_tok, C_Q, GW), (kv_tok, C_KV, GW), (win_tok, C_WIN, WINW // 2)]
        G1 = ([(c + j * GW, GW) for c in (C_HF, C_HQ, C_HG) for j in range(2)]
              + [(c + j * w, w) for _, c, w in TOK for j in range(2)])
        NG1F = 6
        NF = NG1F * 4
        NTOK = 8 * TT
        HACT = 16
        PB = 6

        def units_before(i):
            return 4 * i if i <= NG1F else NF + TT * (i - NG1F)

        proj_scope = ExitStack()
        S1 = Split(proj_scope, "p_")

        with nc.Block() as block:
            @block.sync
            def _(sp):
                for i, g in enumerate((q_norm_g[bass.ds(l, 1)], k_norm_g[bass.ds(l, 1), 1], k_norm_g[bass.ds(l, 1), 2])):
                    sp.dma_start(gain[:, i * HD:(i + 1) * HD], g.to_broadcast([P, HD])).then_inc(sem("gain_loaded"), 16)
                for i, (c, w) in enumerate(G1):
                    load_granule(sp, S1, i, w_in[bass.ds(l, 1)].rearrange("o (c p) n -> p (o c) n", p=P)[:, :, c:c + w])

            @block.gpsimd
            def _(pool):
                for i, (c, w) in enumerate(G1):
                    split_lo(pool, S1, i, w)

            @block.tensor
            def _(pe):
                norm_products(pe, "n1")
                pe.wait_ge(sem("p_w_lo"), 1)
                first_products(pe, bank[2:6], S1, 0, GW, "n1_out", lambda c: c + 1)
                for u in range(4, NF):
                    i, m, s = u // 4, u // 2 % 2, u % 2
                    pe.wait_ge(sem("p_w_lo"), i + 1)
                    if u >= PB:
                        pe.wait_ge(sem("proj_kept"), u - PB + 1)
                    feature_product(pe, bank[2 + u % PB][:, 0:HALF], S1, i, GW, slice(m * P, (m + 1) * P), S1.ah, S1.al,
                                    halves(s)).then_inc(sem("p_done"), 1)
                for n in range(NTOK):
                    u = NF + n
                    i, t = NG1F + n // TT, n % TT
                    w = G1[i][1]
                    pe.wait_ge(sem("p_w_lo"), i + 1)
                    pe.wait_ge(sem("proj_kept"), u - PB + 1)
                    tok = slice(t * P, (t + 1) * P) if t < NT else slice(N - P, N)
                    wh, wl = S1.granule(S1.wh, i, w), S1.granule(S1.wl, i, w)
                    out = bank[2 + u % PB][:, 0:w]
                    for c in range(KC):
                        pe.matmul(out, S1.ah[:, c, tok], wh[:, c, :], start=(c == 0), stop=False)
                        pe.matmul(out, S1.ah[:, c, tok], wl[:, c, :], start=False, stop=False)
                        ins = pe.matmul(out, S1.al[:, c, tok], wh[:, c, :], start=False, stop=(c == KC - 1))
                    ins.then_inc(sem("p_done"), 1)

            @block.scalar
            def _(act):
                exp_ln_tables(act)
                for c in range(KC):
                    square(act, "n1", sq1, c)
                split_hi(act, S1, 0, G1[0][1], 0)
                norm_scalar(act, "n1", sq1, S1)
                split_hi(act, S1, 1, G1[1][1], 0)

                def next_hi(i):
                    if i + 2 < len(G1):
                        split_hi(act, S1, i + 2, G1[i + 2][1], units_before(i + 1))

                def keep_features(u):
                    act.wait_ge(sem("p_done"), u + 1)
                    i, m, s = u // 4, u // 2 % 2, u % 2
                    act.activation(FT[i // 2][:, 2 * (i % 2) + m, halves(s)], bank[2 + u % PB][:, 0:HALF], ACT.Copy
                                   ).then_inc(sem("proj_kept"), 1)
                    if u % 4 == 3:
                        next_hi(i)

                def keep_tokens(n):
                    i, t = n // TT, n % TT
                    u = NF + n
                    dst, _, w = TOK[i // 2]
                    j = i % 2
                    r = rows_of(t)
                    act.wait_ge(sem("p_done"), u + 1)
                    src = bank[2 + u % PB][P - r:P, 0:w]
                    if dst is q_tok:
                        out = dst[0:r, t, :].rearrange("p (g v d) -> p g v d", g=NG, v=NKV)[:, :, j]
                        src = src.rearrange("p (g d) -> p g d", g=NG)
                    else:
                        out = dst[0:r, t, j * w:(j + 1) * w]
                    act.activation(out, src, ACT.Copy).then_inc(sem("proj_kept"), 1)
                    if t == TT - 1:
                        next_hi(NG1F + i)

                for u in range(NF):
                    keep_features(u)
                act.wait_ge(sem("proj_kept"), NF)
                for h in range(HH):
                    for n_ in range(10 * h, 10 * h + 2):
                        keep_tokens(n_)
                    act.wait_ge(sem("hg_vec"), 4 * h + 1)
                    n = HACT * h
                    for t in (0, 3, 6):
                        act.activation(tmp[t], tmp[t], ACT.Exp, scale=-1.0).then_inc(sem("hg_act"), 1)
                    act.activation(tmp[1], tmp[1], ACT.Exp, scale=-1.0).then_inc(sem("hg_act"), 1)
                    for k, t in enumerate((0, 3, 6)):
                        act.wait_ge(sem("hg_act"), n + k + 1)
                        act.activation(tmp[t], tmp[t], ACT.Ln, bias=one).then_inc(sem("hg_act"), 1)
                    act.wait_ge(sem("hg_act"), n + 5)
                    act.activation(tmp[2], tmp[0], ACT.Exp, scale=-1.0).then_inc(sem("hg_act"), 1)
                    for n_ in range(10 * h + 2, 10 * h + 4):
                        keep_tokens(n_)
                    act.wait_ge(sem("hg_vec"), 4 * h + 2)
                    act.activation(tmp[0], tmp[0], ACT.Exp).then_inc(sem("hg_act"), 1)
                    act.wait_ge(sem("hg_act"), n + 9)
                    act.activation(tmp[0], tmp[0], ACT.Ln, bias=one).then_inc(sem("hg_act"), 1)
                    act.activation(tmp[3], tmp[3], ACT.Exp).then_inc(sem("hg_act"), 1)
                    act.activation(hg[:, h, :], tmp[6], ACT.Exp).then_inc(sem("hg_act"), 1)
                    for n_ in range(10 * h + 4, 10 * h + 8):
                        keep_tokens(n_)
                    act.wait_ge(sem("hg_vec"), 4 * h + 3)
                    act.activation(tmp[0], tmp[5], ACT.Exp).then_inc(sem("hg_act"), 1)
                    act.activation(tmp[2], tmp[5], ACT.Exp, scale=-1.0).then_inc(sem("hg_act"), 1)
                    act.activation(tmp[4], tmp[4], ACT.Exp).then_inc(sem("hg_act"), 1)
                    act.activation(dec[:, h, :], dec[:, h, :], ACT.Exp).then_inc(sem("hg_act"), 1)
                    for n_ in range(10 * h + 8, 10 * h + 10):
                        keep_tokens(n_)

            @block.vector
            def _(dve):
                for c in range(1, KC):
                    add_square(dve, "n1", sq1, c)
                step(dve, dve.tensor_copy(par[:, :], par_all[:, bass.ds(l, 1), :].rearrange("p o c -> p (o c)")), "par_set")
                for x in (kv_tok, win_tok, q_tok):
                    dve.memset(x[NS:P, NT, :], 0.0)
                norm_vector(dve, "n1", sq1, S1, G_ATTN)
                dve.wait_ge(sem("proj_kept"), NF)
                for h in range(HH):
                    z = hf[:, h, :]
                    n = HACT * h
                    t0, t1, t2, t3, t4, t5, t6 = tmp
                    for t, x in ((t0, z), (t3, hq[:, h, :]), (t6, hg[:, h, :])):
                        dve.scalar_tensor_tensor(t, x, -1.0, x, ALU.mult, ALU.max)
                    dve.tensor_scalar(t4, z, 0.0, col(P_LNOM + h), ALU.min, ALU.add)
                    dve.tensor_scalar(t1, z, 0.0, None, ALU.max).then_inc(sem("hg_vec"), 1)
                    dve.wait_ge(sem("hg_act"), n + 8)
                    step(dve, dve.tensor_tensor(t4, t4, t0, ALU.subtract), "dve_done")
                    step(dve, dve.tensor_scalar(t0, t4, col(P_LBA + h), None, ALU.subtract), "dve_done")
                    step(dve, dve.scalar_tensor_tensor(t0, t0, -1.0, t0, ALU.mult, ALU.min), "dve_done")
                    dve.scalar_tensor_tensor(t3, hq[:, h, :], 0.0, t3, ALU.min, ALU.subtract)
                    dve.scalar_tensor_tensor(t6, hg[:, h, :], 0.0, t6, ALU.min, ALU.subtract).then_inc(sem("hg_vec"), 1)
                    dve.scalar_tensor_tensor(t1, t1, col(P_OM + h), t2, ALU.mult, ALU.mult).then_inc(sem("hg_key"), 1)
                    dve.wait_ge(sem("hg_act"), n + 12)
                    step(dve, dve.tensor_tensor(t3, hq[:, h, :], t3, ALU.mult), "dve_done")
                    step(dve, dve.scalar_tensor_tensor(t4, t4, col(P_LBA + h), t0, ALU.max, ALU.add), "dve_done")
                    step(dve, dve.tensor_tensor_scan(t5, const("scan"), t4, 0.0, ALU.mult, ALU.add), "dve_done")
                    bp = t5[:, 0:SEQ].rearrange("p (c n) -> p c n", n=CH)
                    bs = t5[:, SEQ:N].rearrange("p (c n) -> p c n", n=DT)
                    dve.tensor_copy(dec[:, h, 0:16], bp[:, :, CH - 1]).then_inc(sem("hg_last"), 1)
                    dve.tensor_copy(dec[:, h, 16:24], bs[:, :, DT - 1]).then_inc(sem("hg_last"), 1)
                    dve.wait_ge(sem("hg_last"), 2 * h + 2)
                    dve.tensor_tensor(t4[:, 0:SEQ].rearrange("p (c n) -> p c n", n=CH), bc(dec[:, h, 0:16], CH), bp,
                                      ALU.subtract)
                    dve.tensor_tensor(t4[:, SEQ:N].rearrange("p (c n) -> p c n", n=DT), bc(dec[:, h, 16:24], DT), bs,
                                      ALU.subtract).then_inc(sem("hg_vec"), 1)
                    dve.wait_ge(sem("hg_key"), h + 1)
                    dve.wait_ge(sem("hg_act"), n + HACT)
                    dve.tensor_tensor(hq[:, h, :], t3, t0, ALU.mult)
                    dve.tensor_tensor(hf[:, h, :], t1, t2, ALU.mult)
                    dve.tensor_tensor(kd[:, h, :], t1, t4, ALU.mult).then_inc(sem("hg_vec"), 1)
                    dve.wait_ge(sem("hg_vec"), 4 * h + 4)

        proj_scope.close()
        R2 = mix_scope.enter_context(nc.sbuf_tensor("R2", [P, R2_N], F32))
        HT_ = mix_scope.enter_context(nc.sbuf_tensor("HT", [P, KC * N], F32))
        W1 = [RAW, mix_scope.enter_context(nc.sbuf_tensor("W1_1", [P, SLOT], F32))]

        cut = cutter(R2)
        ST = [cut(17 * P).rearrange("p (n e) -> p n e", n=17) for _ in range(2)]
        S0 = [cut(NB * P).rearrange("p (b e) -> p b e", b=NB) for _ in range(2)]
        Snew = cut(NB * P).rearrange("p (b e) -> p b e", b=NB)
        Vm = cut(NB * P).rearrange("p (b e) -> p b e", b=NB)
        aTm = [cut(P) for _ in range(3)]
        aTs = [cut(NS)[0:NS] for _ in range(2)]
        kdt = [cut(P) for _ in range(2)]
        QR = HT_[:, 0:TT * 512].rearrange("p (t c) -> p t c", t=TT)
        KN = HT_[:, TT * 512:TT * 768].rearrange("p (b t c) -> p b t c", b=2, t=TT)
        ROT = OT_[:, 0:4 * N].rearrange("p (b c) -> p b c", b=3)
        ktok = [kv_tok[:, :, 256:384], win_tok[:, :, 0:128]]
        UNITS = 5 * HH

        def span(u):
            h, t = u // 5, u % 5
            r = rows_of(t)
            return h, t, r, slice(t * P, t * P + r)

        def apart(u):
            return Vm[:, 4 * (u % 5 % 2):4 * (u % 5 % 2) + 4] if u % 5 < NT else Vm[0:NS]

        def store_states(sp, h):
            sp.wait_ge(sem("hg_state"), 5 * h + 4)
            sp.dma_start(p_hg[bass.ds(l, 1), 0, h].rearrange("o d e -> (o d) e"), ST[h % 2][:, 16, :]
                         ).then_inc(sem("p_hg_stored"), 16)
            sp.wait_ge(sem("hg_state"), 5 * h + 5)
            sp.dma_start(s_hg[bass.ds(l, 1), :, h].rearrange("o b d e -> d (o b) e"), Snew
                         ).then_inc(sem("s_hg_stored"), 16)

        with nc.Block() as block:
            @block.sync
            def _(sp):
                for k in range(2):
                    sp.dma_start(W1[k][:, :].rearrange("p (r n) -> p r n", r=16),
                                 cmp_w1[bass.ds(l, 1), k].rearrange("o (c p) n -> p (o c) n", p=P)
                                 ).then_inc(sem("w1_loaded"), 16)
                for h in range(HH):
                    if h >= 2:
                        sp.wait_ge(sem("hg_o_done"), 5 * (h - 1))
                        sp.wait_ge(sem("hg_state"), 5 * (h - 1))
                    sp.dma_start(S0[h % 2], state_hgrn[bass.ds(l, 1), :, h].rearrange("o b d e -> d (o b) e")
                                 ).then_inc(sem(f"s0_loaded{h % 2}"), 16)
                    if h >= 1:
                        store_states(sp, h - 1)
                store_states(sp, HH - 1)
                sp.wait_ge(sem("p_hg_stored"), 16 * HH)
                sp.wait_ge(sem("s_hg_stored"), 16 * HH)

            @block.tensor
            def _(pe):
                def scores(u):
                    h, t, r, c = span(u)
                    if u >= 2:
                        pe.wait_ge(sem("hg_masked"), u - 1)
                        pe.wait_ge(sem("hg_kd_kept"), u - 1)
                    keep_warm(pe, bank[u % 2], 384)
                    pe.matmul(bank[u % 2][0:r, 0:r], hf[:, h, c], hq[:, h, c], start=True, stop=True
                              ).then_inc(sem("hg_scores"), 1)
                    pe.transpose(bank[2 + u % 2][0:r, 0:P], kd[:, h, c], ident).then_inc(sem("hg_turned"), 1)

                def updates(u):
                    h, t, r, c = span(u)
                    pe.wait_ge(sem("hg_kd_kept"), u + 1)
                    if u >= 2:
                        pe.wait_ge(sem("hg_state"), u if t in (0, NT) else u - 1)
                    pe.wait_ge(sem("hg_apart"), u + 1)
                    if t < NT:
                        ins = pe.matmul(bank[4 + u % 2][:, :], kdt[u % 2], apart(u), start=True, stop=True)
                    else:
                        for s in range(2):
                            ins = pe.matmul(bank[4 + s][:, :], kdt[u % 2][0:NS, :], apart(u)[:, 4 * s:4 * s + 4, :],
                                            start=True, stop=True)
                    ins.then_inc(sem("hg_updates"), 1)

                def outputs(u):
                    h, t, r, c = span(u)
                    pe.wait_ge(sem("hg_masked"), u + 1)
                    if u >= 2:
                        pe.wait_ge(sem("hg_out_kept"), u - 1)
                    o = bank[6 + u % 2]
                    a = aTm[(4 * h + t) % 3] if t < NT else aTs[h % 2]
                    pe.matmul(o[:, 0:r], hi_tok[0:r, t, h * P:(h + 1) * P], a[:, :], start=True, stop=False)
                    if t < NT:
                        pe.wait_ge(sem("hg_state"), u + 1)
                        n, w, s = NCK, CH, ST[h % 2][:, 4 * t:4 * t + 4, :]
                    else:
                        pe.wait_ge(sem(f"s0_loaded{h % 2}"), 16 * (h // 2 + 1))
                        n, w, s = NB, DT, S0[h % 2]
                    for j in range(n):
                        ins = pe.matmul(o[:, j * w:(j + 1) * w], s[:, j, :], hq[:, h, t * P + j * w:t * P + (j + 1) * w],
                                        start=False, stop=(j == n - 1))
                    ins.then_inc(sem("hg_o_done"), 1)

                for u in range(UNITS + 2):
                    if u < UNITS:
                        scores(u)
                    if 1 <= u <= UNITS:
                        updates(u - 1)
                    if u >= 2:
                        outputs(u - 2)
                for h in range(HH):
                    pe.wait_ge(sem("hgn_squared"), h + 1)
                    if h >= 2:
                        pe.wait_ge(sem("hgn_ln"), h - 1)
                    for s in range(2):
                        ins = pe.matmul(bank[2 * (h % 2) + s][:, 0:HALF], ones, kd[:, h, s * HALF:(s + 1) * HALF],
                                        start=True, stop=True)
                    ins.then_inc(sem("hgn_summed"), 1)

            @block.scalar
            def _(act):
                for u in range(UNITS + 3):
                    if u == 1:
                        act.activation(HT_[:, 0:TT * 512].rearrange("p (t c) -> p t c", t=TT), q_tok, ACT.Square
                                       ).then_inc(sem("qk_squared"), 1)
                        for b in range(2):
                            act.activation(KN[:, b], ktok[b], ACT.Square).then_inc(sem("qk_squared"), 1)
                    if u == 3:
                        act.wait_ge(sem("qk_summed"), 3)
                        act.activation(qkr[:, 0:60], qkr[:, 0:60], ACT.Ln, bias=eps, scale=1.0 / HD).then_inc(sem("qk_ln"), 1)
                        act.wait_ge(sem("qk_ln"), 1)
                        act.activation(qkr[:, 0:60], qkr[:, 0:60], ACT.Exp, scale=-0.5).then_inc(sem("qk_rstd"), 1)
                    if u < UNITS:
                        h, t, r, c = span(u)
                        act.wait_ge(sem("hg_turned"), u + 1)
                        if u >= 2:
                            act.wait_ge(sem("hg_updates"), u - 1)
                        act.activation(kdt[u % 2][0:r, :], bank[2 + u % 2][0:r, 0:P], ACT.Copy
                                       ).then_inc(sem("hg_kd_kept"), 1)
                        if u >= 2 and t in (0, NT):
                            act.wait_ge(sem("hg_updates"), u)
                        n, m = (NCK, const("chunk")) if t < NT else (NB, const("batch", NS))
                        for j in range(n):
                            ins = act.activation(apart(u)[:, j, :], hi_tok[0:r, t, h * P:(h + 1) * P], ACT.Copy,
                                                 scale=m[:, j:j + 1])
                        ins.then_inc(sem("hg_apart"), 1)
                    if u >= 3:
                        h, t, r, c = span(u - 3)
                        act.wait_ge(sem("hg_o_done"), u - 2)
                        act.activation(OT[:, 4 + h, c], bank[6 + (u - 3) % 2][:, 0:r], ACT.Copy
                                       ).then_inc(sem("hg_out_kept"), 1)
                act.wait_ge(sem("hg_out_kept"), UNITS)
                for h in range(HH):
                    act.activation(kd[:, h, :], OT[:, 4 + h, :], ACT.Square).then_inc(sem("hgn_squared"), 1)
                for h in range(HH):
                    act.wait_ge(sem("hgn_summed"), h + 1)
                    for s in range(2):
                        ins = act.activation(hq[:, h, s * HALF:(s + 1) * HALF], bank[2 * (h % 2) + s][:, 0:HALF], ACT.Ln,
                                             bias=eps, scale=1.0 / P)
                    ins.then_inc(sem("hgn_ln"), 1)
                    act.wait_ge(sem("hgn_ln"), h + 1)
                    act.activation(hq[:, h, :], hq[:, h, :], ACT.Exp, scale=-0.5).then_inc(sem("hgn_rstd"), 1)

            @block.vector
            def _(dve):
                for i in range(3):
                    dve.memset(aTm[i], 0.0)
                for i in range(2):
                    dve.memset(aTs[i], 0.0)
                for i in range(2):
                    dve.memset(ST[i][:, 0, :], 0.0).then_inc(sem("st_cleared"), 1)
                dve.wait_ge(sem("st_cleared"), 2)

                def masked(u):
                    h, t, r, c = span(u)
                    dve.wait_ge(sem("hg_scores"), u + 1)
                    if u >= 3:
                        dve.wait_ge(sem("hg_o_done"), u - 2)
                    a = aTm[(4 * h + t) % 3] if t < NT else aTs[h % 2]
                    m = const("hgmask") if t < NT else const("hgmask8", NS)
                    dve.copy_predicated(a, m.bitcast(U32), bank[u % 2][0:r, 0:r]).then_inc(sem("hg_masked"), 1)

                def states(u):
                    h, t, r, c = span(u)
                    dve.wait_ge(sem("hg_updates"), u + 1)
                    if t < NT:
                        if h >= 2 and t == 0:
                            dve.wait_ge(sem("p_hg_stored"), 16 * (h - 1))
                            dve.wait_ge(sem("hg_o_done"), 5 * (h - 1))
                        s = ST[h % 2]
                        for j in range(NCK):
                            n = 4 * t + j
                            ins = dve.scalar_tensor_tensor(s[:, n + 1, :], s[:, n, :], dec[:, h, n:n + 1],
                                                           bank[4 + u % 2][:, j * P:(j + 1) * P], ALU.mult, ALU.add)
                            if j < NCK - 1:
                                step(dve, ins, "dve_done")
                        ins.then_inc(sem("hg_state"), 1)
                        dve.wait_ge(sem("hg_state"), u + 1)
                    else:
                        dve.wait_ge(sem(f"s0_loaded{h % 2}"), 16 * (h // 2 + 1))
                        if h >= 1:
                            dve.wait_ge(sem("s_hg_stored"), 16 * h)
                        for b in range(NB):
                            ins = dve.scalar_tensor_tensor(Snew[:, b, :], S0[h % 2][:, b, :], dec[:, h, 16 + b:17 + b],
                                                           bank[4 + b // 4][:, (b % 4) * P:(b % 4 + 1) * P],
                                                           ALU.mult, ALU.add)
                        ins.then_inc(sem("hg_state"), 1)

                for u in range(UNITS + 1):
                    if u < UNITS:
                        masked(u)
                    if u >= 1:
                        states(u - 1)
                    if u == 1:
                        dve.wait_ge(sem("qk_squared"), 3)
                        dve.tensor_reduce(qkr[:, 0:40], QR.rearrange("p t (h d) -> p (t h) d", d=HD), AX, ALU.add
                                          ).then_inc(sem("qk_summed"), 1)
                        for b in range(2):
                            dve.tensor_reduce(qkr[:, 40 + 10 * b:50 + 10 * b],
                                              KN[:, b].rearrange("p t (h d) -> p (t h) d", d=HD), AX, ALU.add
                                              ).then_inc(sem("qk_summed"), 1)
                for h in range(HH):
                    dve.wait_ge(sem("hgn_rstd"), h + 1)
                    step(dve, dve.scalar_tensor_tensor(OT[:, 4 + h, :], OT[:, 4 + h, :], col(G_HG), hq[:, h, :],
                                                       ALU.mult, ALU.mult), "dve_done")
                    dve.tensor_tensor(OT[:, 4 + h, :], OT[:, 4 + h, :], hg[:, h, :], ALU.mult)

            @block.gpsimd
            def _(pool):
                pool.wait_ge(sem("qk_rstd"), 1)
                pool.wait_ge(sem("gain_loaded"), 48)

                def norm(dst, src, r0, nh, g):
                    d = dst.rearrange("p t (h d) -> p t h d", d=HD)
                    s = src.rearrange("p t (h d) -> p t h d", d=HD)
                    r = qkr[:, r0:r0 + TT * nh].rearrange("p (t h) -> p t h", t=TT)
                    g_ = gain[:, g * HD:(g + 1) * HD].unsqueeze(1).to_broadcast([P, nh, HD])
                    for t in range(TT):
                        step(pool, pool.tensor_tensor(d[:, t], s[:, t], bc(r[:, t], HD), ALU.mult), "pool_done")
                        step(pool, pool.tensor_tensor(d[:, t], d[:, t], g_, ALU.mult), "pool_done")

                def rotate(dst, src, nh):
                    d = dst.rearrange("p t (h d) -> p t h d", d=HD)
                    s = src.rearrange("p t (h d) -> p t h d", d=HD)
                    F = HD // 2
                    cos = const("cos").rearrange("p (t f) -> p t f", f=F)
                    sin = const("sin").rearrange("p (t f) -> p t f", f=F)
                    a, b = (ROT[:, i, 0:nh * F].rearrange("p (h f) -> p h f", f=F) for i in range(2))
                    for t in range(TT):
                        c_ = cos[:, t].unsqueeze(1).to_broadcast([P, nh, F])
                        s_ = sin[:, t].unsqueeze(1).to_broadcast([P, nh, F])
                        for lo, x, y, op in ((0, 0, F, ALU.subtract), (F, F, 0, ALU.add)):
                            pool.tensor_tensor(a, s[:, t, :, x:x + F], c_, ALU.mult)
                            step(pool, pool.tensor_tensor(b, s[:, t, :, y:y + F], s_, ALU.mult), "pool_done")
                            step(pool, pool.tensor_tensor(d[:, t, :, lo:lo + F], a, b, op), "pool_done")

                norm(q_tok, q_tok, 0, NH, 0)
                for b in range(2):
                    norm(KN[:, b], ktok[b], 40 + 10 * b, NKV, 1 + b)
                    rotate(ktok[b], KN[:, b], NKV)
                rotate(QR, q_tok, NH)


        o_tok = hi_tok
        cut = cutter(R1, R_HG)
        QN = cut(NG * N).rearrange("p (g n) -> p g n", g=NG)
        QT = cut(NG * N).rearrange("p (g n) -> p g n", g=NG)
        KT = cut(2 * N).rearrange("p (b n) -> p b n", b=2)
        gate = cut(TT * 24).rearrange("p (t c) -> p t c", t=TT)
        R_ATT = R_HG + (2 * NG + 2) * N + TT * 24
        probs = [cut(512) for _ in range(3)]
        probsT = [cut(512) for _ in range(2)]
        nmax, rsum, coef, otmp = cut(64), cut(64), cut(64), cut(512)
        SCALE = HD ** -0.5
        vtok = [kv_tok[:, :, 384:512], win_tok[:, :, 128:256]]

        TURNS = [(k, t) for t in range(TT) for k in range(3)]
        AU = [(t, b, v, g) for t in range(NT) for b in range(2) for v in range(NKV) for g in range(NG)]
        AG = len(AU) // NH

        def turn_views(k, t):
            r = rows_of(t)
            n = NG if k < 2 else 2
            dst = (QN, QT, KT)[k][:, :, t * P:t * P + r]
            return r, n, dst

        def kept_before(n, parity):
            return (n + 1 - parity) // 2

        NEXT = NCP + 2
        WIDE = P + NEXT
        raw = [t.rearrange("p (r k c) -> p r k c", r=CST, k=2) for t in (HT_[:, 0:4096], R2[:, 0:4096])]
        cut = cutter(R2, 4096)
        FT = [cut(NKV * 8 * WIDE) for _ in range(2)]
        cut = cutter(R1)
        GH = [cut(4 * WIDE) for _ in range(2)]
        ksq = cut(NCALL)
        cut = cutter(R1, R_HI + TT * 512)
        KCT, VCT = cut(NCALL), cut(NCALL)
        VC = cut(4 * P).rearrange("p (a c) -> p a c", a=4)
        VB = cut(NKV * 256).rearrange("p (v c) -> p v c", v=NKV)
        cut = cutter(R1, R_ATT)
        cx, cu = ([cut(4 * WIDE) for _ in range(2)] for _ in range(2))
        W2 = OT_[:, 0:1024].rearrange("p (k v h c) -> p k v h c", k=2, v=NKV, h=2)
        G_A, G_B = (2 / np.pi) ** 0.5, 0.044715 * (2 / np.pi) ** 0.5

        def load_chunks(sp, p):
            for j in range(16):
                pg = sp.value_load(pages[0:1, 16 * p + j:16 * p + j + 1], min_val=0, max_val=NPOOL - 1)
                sp.dma_start(raw[p % 2][8 * j:8 * j + 8].rearrange("p r k c -> p r (k c)"),
                             cache_nsa_kv[bass.ds(l, 1), bass.ds(pg, 1), :, 0:2].rearrange(
                                 "o q (c r) k v d -> (o q c) r (k v d)", r=CST)
                             ).then_inc(sem(f"raw_loaded{p % 2}"), 16)

        with nc.Block() as block:
            @block.sync
            def _(sp):
                sp.dma_start(p_nsa[bass.ds(l, 1)].rearrange("o b (t p) k h d -> p (o b t) (k h d)", p=P),
                             kv_tok[:, 0:NT, :]).then_inc(sem("nsa_stored"), 16)
                sp.dma_start(s_nsa[bass.ds(l, 1)].rearrange("o b t k h d -> (o b t) (k h d)"),
                             kv_tok[0:NS, NT, :]).then_inc(sem("rows_stored"), 16)
                sp.dma_start(p_win[bass.ds(l, 1)].rearrange("o b (t p) k h d -> p (o b t) (k h d)", p=P),
                             win_tok[:, 0:NT, 0:256]).then_inc(sem("rows_stored"), 16)
                sp.dma_start(s_win[bass.ds(l, 1)].rearrange("o b t k h d -> (o b t) (k h d)"),
                             win_tok[0:NS, NT, 0:256]).then_inc(sem("rows_stored"), 16)
                for k in range(2):
                    for v in range(NKV):
                        sp.dma_start(raw[1][NCP:NEXT, :, k, v * HD:(v + 1) * HD],
                                     cmp_pos[bass.ds(l, 1), k].rearrange("o (c r) d -> (o c) r d", r=CST)
                                     ).then_inc(sem("raw_loaded1"), 16)
                sp.wait_ge(sem("w2_cleared"), 1)
                for k in range(2):
                    for v in range(NKV):
                        sp.dma_start(W2[:, k, v, :, v * HD:(v + 1) * HD],
                                     cmp_w2[bass.ds(l, 1), k].rearrange("o (h p) d -> p (o h) d", p=P)
                                     ).then_inc(sem("w2_loaded"), 16)
                sp.wait_ge(sem("nsa_stored"), 16)
                sp.dma_start(raw[1][0:NCP].rearrange("p r k c -> p r (k c)"),
                             p_nsa[bass.ds(l, 1), 0, :, 0:2].rearrange("o (c r) k v d -> (o c) r (k v d)", r=CST)
                             ).then_inc(sem("raw_loaded1"), 16)
                sp.wait_ge(sem("turned"), len(TURNS))
                load_chunks(sp, 0)
                sp.wait_ge(sem("rows_stored"), 48)

            @block.gpsimd
            def _(pool):
                pool.memset(W2, 0.0).then_inc(sem("w2_cleared"), 1)

            @block.tensor
            def _(pe):
                for u, (k, t) in enumerate(TURNS):
                    r, n, dst = turn_views(k, t)
                    if u >= 4:
                        pe.wait_ge(sem(f"turn_kept{u % 2}"), (u - 4) // 2 + 1)
                    for g in range(n):
                        src = (q_tok, QR)[k][0:r, t, g * P:(g + 1) * P] if k < 2 else ktok[g][0:r, t, :]
                        ins = pe.transpose(bank[u % 4][:, g * r:(g + 1) * r], src, ident[0:r, 0:r])
                    ins.then_inc(sem("turned"), 1)
                for i in range(2):
                    pe.wait_ge(sem(f"turn_kept{i}"), kept_before(len(TURNS), i))

                def scores(n):
                    t, b, v, g = AU[n]
                    if n >= 3:
                        pe.wait_ge(sem("probs_made"), n - 2)
                    k = slice(v * HD, (v + 1) * HD)
                    pe.matmul(bank[n % 3][:, 0:(t + 1) * P], QT[k, g, t * P:(t + 1) * P], KT[k, b, 0:(t + 1) * P],
                              start=True, stop=False)
                    pe.matmul(bank[n % 3][:, t * P:(t + 1) * P], ident, const("causal"), start=False, stop=True
                              ).then_inc(sem("scored"), 1)

                def turn_probs(n):
                    t, b, v, g = AU[n]
                    pe.wait_ge(sem("probs_made"), n + 1)
                    if n >= 2:
                        pe.wait_ge(sem(f"probsT_kept{n % 2}"), n // 2)
                    for j in range(t + 1):
                        ins = pe.transpose(bank[3 + n % 2][:, j * P:(j + 1) * P], probs[n % 3][:, j * P:(j + 1) * P], ident)
                    ins.then_inc(sem("probs_turned"), 1)

                def values(n):
                    t, b, v, g = AU[n]
                    grp, h = n // NH, n % NH
                    if h == 0 and grp >= 2:
                        pe.wait_ge(sem("o_kept"), grp - 1)
                    pe.wait_ge(sem(f"probsT_kept{n % 2}"), n // 2 + 1)
                    for j in range(t + 1):
                        ins = pe.matmul(bank[5 + grp % 2][:, h * HD:(h + 1) * HD], probsT[n % 2][:, j * P:(j + 1) * P],
                                        vtok[b][:, j, v * HD:(v + 1) * HD], start=(j == 0), stop=(j == t))
                    ins.then_inc(sem("valued"), 1)

                for n in range(len(AU) + 3):
                    if n < len(AU):
                        scores(n)
                    if 2 <= n < len(AU) + 2:
                        turn_probs(n - 2)
                    if n >= 3:
                        values(n - 3)

            def keep_turn(eng, u):
                k, t = TURNS[u]
                r, n, dst = turn_views(k, t)
                eng.wait_ge(sem("turned"), u + 1)
                src = bank[u % 4][:, 0:n * r].rearrange("p (g n) -> p g n", g=n)
                if eng is nc.scalar:
                    ins = eng.activation(dst, src, ACT.Copy, scale=SCALE if k < 2 else 1.0)
                else:
                    ins = eng.tensor_scalar(dst, src, SCALE if k < 2 else 1.0, None, ALU.mult)
                ins.then_inc(sem(f"turn_kept{u % 2}"), 1)

            def keep_probsT(eng, n):
                t = AU[n][0]
                eng.wait_ge(sem("probs_turned"), n + 1)
                if n >= 2:
                    eng.wait_ge(sem("valued"), n - 1)
                src, dst = bank[3 + n % 2][:, 0:(t + 1) * P], probsT[n % 2][:, 0:(t + 1) * P]
                ins = eng.activation(dst, src, ACT.Copy) if eng is nc.scalar else eng.tensor_copy(dst, src)
                ins.then_inc(sem(f"probsT_kept{n % 2}"), 1)

            @block.scalar
            def _(act):
                act.activation(gate, win_tok[:, :, 256:WINW], ACT.Exp, scale=-1.0).then_inc(sem("gate_exp"), 1)
                for u in range(0, len(TURNS), 2):
                    keep_turn(nc.scalar, u)
                for n in range(len(AU) + 3):
                    if n >= 3 and (n - 3) % 2 == 0:
                        keep_probsT(nc.scalar, n - 3)
                    if n < len(AU):
                        t = AU[n][0]
                        act.wait_ge(sem("maxed"), n + 1)
                        if n >= 3:
                            act.wait_ge(sem("probs_turned"), n - 2)
                        act.activation(probs[n % 3][:, 0:(t + 1) * P], bank[n % 3][:, 0:(t + 1) * P], ACT.Exp,
                                       bias=nmax[:, n:n + 1], accum_out=rsum[:, n:n + 1]).then_inc(sem("probs_made"), 1)

            @block.vector
            def _(dve):
                dve.wait_ge(sem("gate_exp"), 1)
                step(dve, dve.tensor_scalar(gate, gate, 1.0, None, ALU.add), "dve_done")
                step(dve, dve.reciprocal(gate, gate), "dve_done")
                for u in range(1, len(TURNS), 2):
                    keep_turn(nc.vector, u)

                def keep_group(grp):
                    t, b = AU[grp * NH][0:2]
                    c = coef[:, grp * NH:(grp + 1) * NH]
                    step(dve, dve.reciprocal(c, rsum[:, grp * NH:(grp + 1) * NH]), "dve_done")
                    step(dve, dve.tensor_tensor(c, c, gate[:, t, :].rearrange("p (h b) -> p h b", b=3)[:, :, 1 + b],
                                                ALU.mult), "dve_done")
                    dve.wait_ge(sem("valued"), NH * (grp + 1))
                    o = bank[5 + grp % 2][:, :].rearrange("p (h d) -> p h d", d=HD)
                    dst = (o_tok[:, t, :] if b == 0 else otmp).rearrange("p (h d) -> p h d", d=HD)
                    dve.tensor_tensor(dst, o, bc(c, HD), ALU.mult).then_inc(sem("o_kept"), 1)
                    if b == 1:
                        dve.wait_ge(sem("o_kept"), grp + 1)
                        step(dve, dve.tensor_tensor(o_tok[:, t, :], o_tok[:, t, :], otmp, ALU.add), "dve_done")

                for n in range(len(AU) + 6):
                    if n >= 3 and n - 3 < len(AU) and (n - 3) % 2 == 1:
                        keep_probsT(nc.vector, n - 3)
                    if n < len(AU):
                        t = AU[n][0]
                        dve.wait_ge(sem("scored"), n + 1)
                        dve.tensor_reduce(nmax[:, n:n + 1], bank[n % 3][:, 0:(t + 1) * P], AX, ALU.max, negate=True
                                          ).then_inc(sem("maxed"), 1)
                    if n >= 5 and (n - 5) % NH == NH - 1:
                        keep_group((n - 5) // NH)


        CU = [(p, k) for p in range(4) for k in range(2)]

        def chunks_of(w):
            n = P if w >= 2 else WIDE
            return n, FT[w % 2][:, 0:NKV * 8 * n].rearrange("p (v r n) -> p v r n", v=NKV, r=8)

        def hidden_of(w, t, v):
            n = chunks_of(w)[0]
            return t[:, 2 * v * n:2 * (v + 1) * n].rearrange("p (h n) -> p h n", h=2)

        def hidden_bank(w, v):
            return hidden_of(w, bank[4 + w % 2], v) if w >= 2 else hidden_of(w, bank[4 + v], 0)

        with nc.Block() as block:
            @block.sync
            def _(sp):
                for p in range(1, 4):
                    sp.wait_ge(sem("pt_done" if p == 1 else "ct_done"), 4 if p == 1 else 8 * (p - 1))
                    load_chunks(sp, p)

            def raw_count(p):
                return 256 * (p // 2 + 1) + (80 if p % 2 else 0)

            @block.tensor
            def _(pe):
                w1 = [W1[k][:, :].rearrange("p (r n) -> p r n", r=16) for k in range(2)]
                pe.wait_ge(sem("w1_loaded"), 32)
                pe.wait_ge(sem("raw_loaded1"), 80)
                for u in range(4):
                    k, j = u // 2, u % 2
                    for r in range(8):
                        ins = pe.transpose(bank[u][:, r * NEXT:(r + 1) * NEXT], raw[1][0:NEXT, 8 * j + r, k, :],
                                           ident[0:NEXT, 0:NEXT])
                    ins.then_inc(sem("pt_done"), 1)

                def turns(w):
                    p, k = CU[w]
                    if k == 0:
                        pe.wait_ge(sem(f"raw_loaded{p % 2}"), raw_count(p))
                    for j in range(4):
                        u = 4 * w + j
                        if u >= 4:
                            pe.wait_ge(sem(f"ct_kept{u % 2}"), (u - 4) // 2 + 1)
                        else:
                            pe.wait_ge(sem(f"pt_kept{u % 2}"), u // 2 + 1)
                        for r in range(4):
                            ins = pe.transpose(bank[j][:, r * P:(r + 1) * P], raw[p % 2][:, 4 * j + r, k, :], ident)
                        ins.then_inc(sem("ct_done"), 1)

                def hidden(w):
                    p, k = CU[w]
                    n, ft = chunks_of(w)
                    for i in range(2):
                        pe.wait_ge(sem(f"ct_kept{i}"), 2 * (w + 1))
                    if w >= 1:
                        pe.wait_ge(sem("x_kept"), w if w <= 2 else w - 1)
                    for v in range(NKV):
                        for h in range(2):
                            for r in range(16):
                                s = r // 8
                                ins = pe.matmul(hidden_bank(w, v)[:, h, 0:n - s], w1[k][:, r, h * P:(h + 1) * P],
                                                ft[:, v, r % 8, s:n], start=(r == 0), stop=(r == 15))
                    ins.then_inc(sem("h_done"), 1)

                def outputs(w):
                    p, k = CU[w]
                    n, _ = chunks_of(w)
                    if w == 0:
                        pe.wait_ge(sem("w2_loaded"), 64)
                    elif w >= 2:
                        pe.wait_ge(sem("c_out_kept"), w - 1)
                    pe.wait_ge(sem("gelu_done"), w + 1)
                    for m in range(4):
                        ins = pe.matmul(bank[6 + w % 2][:, 0:n], W2[:, k, m // 2, m % 2, :], GH[w % 2][:, m * n:(m + 1) * n],
                                        start=(m == 0), stop=(m == 3))
                    ins.then_inc(sem("c_out_done"), 1)

                for w in range(len(CU) + 2):
                    if w < len(CU):
                        turns(w)
                    if 1 <= w <= len(CU):
                        hidden(w - 1)
                    if w >= 2:
                        outputs(w - 2)
                pe.wait_ge(sem("kc_squared"), 1)
                pe.wait_ge(sem("x_kept"), len(CU))
                pe.matmul(bank[4][:, :], ones64, ksq[:, 0:NCC], start=True, stop=True)
                pe.matmul(bank[5][:, 0:NCP], ones64, ksq[:, NCC:NCALL], start=True, stop=True).then_inc(sem("kc_summed"), 1)
                pe.wait_ge(sem("vct_kept"), 1)
                for a in range(4):
                    pe.transpose(bank[6][:, a * P:(a + 1) * P], VCT[:, a * P:(a + 1) * P], ident)
                pe.transpose(bank[7][:, 0:P], cx[0][:, 0:P], ident).then_inc(sem("vc_turned"), 1)

            def keep_rows(eng, dst, src):
                src = src.rearrange("p (a b n) -> p a b n", b=2, n=dst.shape[3])
                for v in range(NKV):
                    for b in range(2):
                        d, x = dst[b * HD:(b + 1) * HD, v], src[v * HD:(v + 1) * HD, :, b, :]
                        ins = eng.activation(d, x, ACT.Copy) if eng is nc.scalar else eng.tensor_copy(d, x)
                return ins

            def keep_ct(eng, w, odd):
                n, ft = chunks_of(w)
                for j in (odd, 2 + odd):
                    eng.wait_ge(sem("ct_done"), 4 * w + j + 1)
                    if w >= 2:
                        eng.wait_ge(sem("h_done"), w - 1)
                    keep_rows(eng, ft[:, :, 2 * j:2 * j + 2, 0:P], bank[j][:, :]).then_inc(sem(f"ct_kept{odd}"), 1)

            def keep_prompt(eng, odd):
                for u in (odd, 2 + odd):
                    eng.wait_ge(sem("pt_done"), u + 1)
                    keep_rows(eng, chunks_of(u // 2)[1][:, :, 4 * odd:4 * odd + 4, P:WIDE], bank[u][:, 0:8 * NEXT]
                              ).then_inc(sem(f"pt_kept{odd}"), 1)

            @block.scalar
            def _(act):
                def gelu(w):
                    p, k = CU[w]
                    n, _ = chunks_of(w)
                    act.wait_ge(sem("h_done"), w + 1)
                    if w >= 2:
                        act.wait_ge(sem("gelu_done"), w - 1)
                    if w < 2:
                        act.wait_ge(sem("bias_kept"), w + 1)
                    for h in range(2):
                        for v in range(NKV):
                            ins = act.activation(hidden_of(w, cx[w % 2], v)[:, h], hidden_bank(w, v)[:, h], ACT.Identity,
                                                 bias=par[:, P_HB + 2 * k + h:P_HB + 2 * k + h + 1])
                    ins.then_inc(sem("x_kept"), 1)
                    act.wait_ge(sem("gelu_arg"), w + 1)
                    c = cu[w % 2][:, 0:4 * n]
                    for f, kw in ((ACT.Exp, dict(scale=-2.0)), (ACT.Ln, dict(bias=one)), (ACT.Exp, dict(scale=-1.0))):
                        step(act, act.activation(c, c, f, **kw), "gelu_act")

                def keep_output(w):
                    p, k = CU[w]
                    act.wait_ge(sem("c_out_done"), w + 1)
                    dst = (KCT, VCT)[k]
                    ins = act.activation(dst[:, p * P:(p + 1) * P], bank[6 + w % 2][:, 0:P], ACT.Copy)
                    if p == 0:
                        ins = act.activation(dst[:, NCC:NCALL], bank[6 + w % 2][:, P:P + NCP], ACT.Copy)
                    ins.then_inc(sem("c_out_kept"), 1)

                keep_prompt(nc.scalar, 0)

                for w in range(len(CU) + 2):
                    if w < len(CU):
                        keep_ct(nc.scalar, w, 0)
                    if 1 <= w <= len(CU):
                        gelu(w - 1)
                    if w >= 2:
                        keep_output(w - 2)
                    if w == len(CU):
                        act.wait_ge(sem("c_out_kept"), len(CU) - 1)
                        act.activation(ksq, KCT, ACT.Square).then_inc(sem("kc_squared"), 1)
                act.wait_ge(sem("c_out_kept"), len(CU))
                act.activation(cx[0][:, 0:P].rearrange("p (g n) -> p g n", g=NG),
                               VCT[:, NCC:NCALL].unsqueeze(1).to_broadcast([P, NG, NCP]), ACT.Copy
                               ).then_inc(sem("vct_kept"), 1)
                act.wait_ge(sem("kc_summed"), 1)
                act.activation(ksq[:, 0:NCC], bank[4][:, :], ACT.Ln, bias=eps, scale=1.0 / HD)
                act.activation(ksq[:, NCC:NCALL], bank[5][:, 0:NCP], ACT.Ln, bias=eps, scale=1.0 / HD
                               ).then_inc(sem("kc_ln"), 1)
                act.wait_ge(sem("kc_ln"), 1)
                act.activation(ksq, ksq, ACT.Exp, scale=-0.5).then_inc(sem("kc_rstd"), 1)

            @block.vector
            def _(dve):
                dve.memset(VB, 0.0)
                keep_prompt(nc.vector, 1)

                def gelu(w):
                    n, _ = chunks_of(w)
                    x, c, g = (t[w % 2][:, 0:4 * n] for t in (cx, cu, GH))
                    if w < 2:
                        dve.wait_ge(sem("h_done"), w + 1)
                        dve.tensor_tensor(par[:, P_HB + 2 * w:P_HB + 2 * w + 2], hidden_bank(w, 0)[:, :, P + NCP],
                                          par[:, P_B1 + 2 * w:P_B1 + 2 * w + 2], ALU.add).then_inc(sem("bias_kept"), 1)
                    dve.wait_ge(sem("x_kept"), w + 1)
                    if w >= 2:
                        dve.wait_ge(sem("gelu_done"), w - 1)
                    step(dve, dve.tensor_tensor(c, x, x, ALU.mult), "dve_done")
                    step(dve, dve.tensor_scalar(c, c, float(G_B), float(G_A), ALU.mult, ALU.add), "dve_done")
                    step(dve, dve.tensor_tensor(c, c, x, ALU.mult), "dve_done")
                    dve.tensor_scalar(c, c, -20.0, None, ALU.max).then_inc(sem("gelu_arg"), 1)
                    dve.wait_ge(sem("gelu_act"), 3 * (w + 1))
                    if w >= 2:
                        dve.wait_ge(sem("c_out_done"), w - 1)
                    dve.tensor_tensor(g, x, c, ALU.mult).then_inc(sem("gelu_done"), 1)

                for w in range(len(CU) + 1):
                    if w < len(CU):
                        keep_ct(nc.vector, w, 1)
                    if w >= 1:
                        gelu(w - 1)
                dve.wait_ge(sem("vc_turned"), 1)
                dve.tensor_copy(VC.rearrange("p a c -> p (a c)"), bank[6][:, :])
                for v in range(NKV):
                    for g in range(NG):
                        rr = slice(g * NCP, (g + 1) * NCP)
                        dve.tensor_copy(VB[rr, v, g * HD:(g + 1) * HD], bank[7][rr, v * HD:(v + 1) * HD])
                dve.wait_ge(sem("kc_rstd"), 1)
                dve.scalar_tensor_tensor(KCT, KCT, col(G_KC), ksq, ALU.mult, ALU.mult).then_inc(sem("kc_done"), 1)
                dve.wait_ge(sem("kc_done"), 1)



        NP_ = NB // 2
        cut = cutter(HT_)
        QD = cut(2 * NB * NS).rearrange("p (k b r) -> p k b r", k=2, b=NB)
        oA = cut(NP_ * HD).rearrange("p (a d) -> p a d", a=NP_)
        o2 = cut(NP_ * 2 * HD).rearrange("p (a i d) -> p a i d", a=NP_, i=2)
        DMk = cut(NP_ * 16).rearrange("p (a j) -> p a j", a=NP_)
        gateR = cut(NP_ * 3).rearrange("p (a b) -> p a b", a=NP_)
        gm = cut(NP_ * 24)[0:NS].rearrange("p (a c) -> p a c", a=NP_)
        gx = cut(NP_ * 24).rearrange("p (a h b) -> p a h b", a=NP_, h=NH)
        sp_ = cut(NP_ * NCS)
        sp3 = sp_.rearrange("p (a c) -> p a c", a=NP_)
        sm = cut(64)
        imp, val = (cut(NP_ * 16).rearrange("p (a j) -> p a j", a=NP_) for _ in range(2))
        srs = cut(64)
        cut = cutter(R1, R_ATT)
        cs = [cut(256) for _ in range(2)]
        csT = [cut(256) for _ in range(2)]
        cm = [cut(256) for _ in range(2)]
        otm = cut(512)
        sBD = cut(NP_ * P).rearrange("p (a c) -> p a c", a=NP_)
        ssT = cut(NP_ * P).rearrange("p (a r) -> p a r", a=NP_)
        NC = NCS - 1
        RING = 6
        slots = ([(R2, i * 3072, R2, i * 3072 + 2048) for i in range(3)] + [(W1[0], 0, W1[0], 2048)]
                 + [(R1, 0, R1, TT * 512), (R1, R_HG, R1, R_HG + 2048)])
        pastKV = [s[:, o:o + NPG * 256].rearrange("p (j c) -> p j c", j=NPG) for s, o, _, _ in slots]
        winKV = [s[:, o:o + 4 * 256].rearrange("p (j c) -> p j c", j=4) for _, _, s, o in slots]
        kTb = [W1[1][:, i * 1536:(i + 1) * 1536] for i in range(2)]

        def load_past(eng, b, pages_=range(NPG), window=True):
            for j in pages_:
                pg = eng.value_load(pages[0:1, NPG * b + j:NPG * b + j + 1], min_val=0, max_val=NPOOL - 1)
                eng.dma_start(pastKV[b % RING][:, j, :],
                              cache_nsa_kv[bass.ds(l, 1), bass.ds(pg, 1), :, 2:4].rearrange(
                                  "o q r k v d -> (o q r) (k v d)")).then_inc(sem(f"past_loaded{b % RING}"), 16)
            if window:
                eng.dma_start(winKV[b % RING], cache_win_kv[bass.ds(l, 1), b].rearrange(
                    "o (j p) k v d -> p (o j) (k v d)", p=P)).then_inc(sem(f"past_loaded{b % RING}"), 16)

        def past_count(b):
            return 16 * (NPG + 1) * (b // RING + 1)

        with nc.Block() as block:
            @block.sync
            def _(sp):
                for b in (0, 2, 3, 4):
                    load_past(sp, b)

            @block.tensor
            def _(pe):
                pe.wait_ge(sem("qd_made"), 2)
                for b in range(NB):
                    a, q = b // 2, b % 2
                    ins = pe.matmul(bank[4][q * NS:(q + 1) * NS, a * NCS:(a + 1) * NCS], QD[:, 0, b, :],
                                    KCT[:, b * NCS:(b + 1) * NCS], start=True, stop=True)
                ins.then_inc(sem("s_scored"), 1)
                pe.wait_ge(sem("gate_masked"), 1)
                pe.matmul(bank[7][:, 0:NP_ * 24], const("rowsel", NS), gm.rearrange("p a c -> p (a c)"), start=True, stop=True
                          ).then_inc(sem("gate_spread"), 1)

                def prompt_scores(t):
                    if t >= 2:
                        pe.wait_ge(sem("c_read"), 2 * (t - 1))
                    for v in range(NKV):
                        k = slice(v * HD, (v + 1) * HD)
                        for g in range(NG):
                            ins = pe.matmul(bank[2 * (t % 2) + v][:, g * NCP:(g + 1) * NCP],
                                            QN[k, g, t * P:(t + 1) * P], KCT[k, NCC:NCALL], start=True, stop=True)
                    ins.then_inc(sem("c_scored"), 1)

                prompt_scores(0)
                prompt_scores(1)
                pe.wait_ge(sem("s_probs"), 1)
                pe.matmul(bank[5][:, 0:NP_ * NCS], const("groupsum"), sp_, start=True, stop=True).then_inc(sem("s_imp"), 1)
                pe.wait_ge(sem("s_apart"), 1)
                for a in range(NP_):
                    ins = pe.transpose(bank[4][:, a * P:(a + 1) * P], sBD[:, a, :], ident)
                ins.then_inc(sem("s_turned"), 1)

                def prompt_turn(t):
                    pe.wait_ge(sem("c_probs"), t + 1)
                    if t == 0:
                        pe.wait_ge(sem("gate_read"), 1)
                    else:
                        pe.wait_ge(sem("c_turn_kept"), t)
                    for v in range(NKV):
                        ins = pe.transpose(bank[7][:, v * P:(v + 1) * P], cs[t % 2][:, v * P:(v + 1) * P], ident)
                    ins.then_inc(sem("c_turned"), 1)

                def prompt_values(t):
                    pe.wait_ge(sem("c_turn_kept"), t + 1)
                    if t == 0:
                        pe.wait_ge(sem("imp_made"), 1)
                    else:
                        pe.wait_ge(sem("c_kept"), t)
                    for v in range(NKV):
                        ins = pe.matmul(bank[5][:, v * 256:(v + 1) * 256], csT[t % 2][:, v * P:(v + 1) * P], VB[:, v, :],
                                        start=True, stop=True)
                    ins.then_inc(sem("c_valued"), 1)

                prompt_turn(0)
                pe.wait_ge(sem("s_turn_kept"), 1)
                for a in range(NP_):
                    ins = pe.matmul(bank[6][:, a * P:(a + 1) * P], ssT[:, a, :], VC[:, a, :], start=True, stop=True)
                ins.then_inc(sem("s_valued"), 1)
                prompt_values(0)
                for t in range(1, NT):
                    if t + 1 < NT:
                        prompt_scores(t + 1)
                    prompt_turn(t)
                    prompt_values(t)

            @block.scalar
            def _(act):
                load_past(act, 1, range(4))
                act.wait_ge(sem("s_shifted"), 1)
                act.activation(sp3[:, :, 0:NC], sp3[:, :, 0:NC], ACT.Exp).then_inc(sem("s_exp"), 1)

                def exponentials(t):
                    act.wait_ge(sem("c_shifted"), t + 1)
                    act.activation(cs[t % 2], cs[t % 2], ACT.Exp).then_inc(sem("c_exp"), 1)

                def keep_turn(t):
                    act.wait_ge(sem("c_turned"), t + 1)
                    act.activation(csT[t % 2], bank[7][:, 0:256], ACT.Copy).then_inc(sem("c_turn_kept"), 1)

                exponentials(0)
                load_past(act, 1, range(4, NPG), window=False)
                act.wait_ge(sem("s_turned"), 1)
                act.activation(ssT, bank[4][:, :].rearrange("p (a r) -> p a r", a=NP_), ACT.Copy
                               ).then_inc(sem("s_turn_kept"), 1)
                exponentials(1)
                for t in range(NT):
                    keep_turn(t)
                    if 2 <= t + 1 < NT:
                        exponentials(t + 1)

            @block.vector
            def _(dve):
                def shift(t):
                    p3 = cs[t % 2].rearrange("p (h c) -> p h c", h=NH)
                    m = cm[t % 2]
                    neg = const("cmpneg")[:, t * NCP:(t + 1) * NCP].unsqueeze(1)
                    dve.wait_ge(sem("c_scored"), t + 1)
                    if t >= 2:
                        dve.wait_ge(sem("c_turned"), t - 1)
                    for v in range(NKV):
                        dve.tensor_tensor(p3[:, v * NG:(v + 1) * NG, :],
                                          bank[2 * (t % 2) + v][:, 0:P].rearrange("p (g c) -> p g c", g=NG),
                                          neg.to_broadcast([P, NG, NCP]), ALU.add).then_inc(sem("c_read"), 1)
                    dve.wait_ge(sem("c_read"), 2 * t + 2)
                    step(dve, dve.tensor_reduce(m[:, 0:8], p3, AX, ALU.max, negate=True), "dve_done")
                    dve.tensor_tensor(p3, p3, bc(m[:, 0:8], NCP), ALU.add).then_inc(sem("c_shifted"), 1)

                def probabilities(t):
                    p3 = cs[t % 2].rearrange("p (h c) -> p h c", h=NH)
                    m = cm[t % 2]
                    vis = const("cmp01")[:, t * NCP:(t + 1) * NCP].unsqueeze(1)
                    dve.wait_ge(sem("c_exp"), t + 1)
                    dve.tensor_tensor(p3, p3, vis.to_broadcast([P, NH, NCP]), ALU.mult).then_inc(sem("c_probs"), 1)
                    dve.wait_ge(sem("c_probs"), t + 1)
                    step(dve, dve.tensor_reduce(m[:, 8:16], p3, AX, ALU.add), "dve_done")
                    step(dve, dve.tensor_scalar(m[:, 8:16], m[:, 8:16], 1e-30, None, ALU.max), "dve_done")
                    step(dve, dve.reciprocal(m[:, 16:24], m[:, 8:16]), "dve_done")
                    step(dve, dve.tensor_tensor(m[:, 16:24], m[:, 16:24],
                                                gate[:, t, :].rearrange("p (h b) -> p h b", b=3)[:, :, 0], ALU.mult), "dve_done")

                def add_branch(t):
                    dve.wait_ge(sem("c_valued"), t + 1)
                    dve.tensor_tensor(otm.rearrange("p (h d) -> p h d", d=HD),
                                      bank[5][:, :].rearrange("p (h d) -> p h d", d=HD), bc(cm[t % 2][:, 16:24], HD), ALU.mult
                                      ).then_inc(sem("c_kept"), 1)
                    dve.wait_ge(sem("c_kept"), t + 1)
                    step(dve, dve.tensor_tensor(o_tok[:, t, :], o_tok[:, t, :], otm, ALU.add), "dve_done")

                step(dve, dve.memset(QD, 0.0), "dve_done")
                step(dve, dve.memset(DMk, 0.0), "dve_done")
                dve.memset(sp3[:, :, NC:NCS], 0.0)
                step(dve, dve.memset(sBD, 0.0), "dve_done")
                for k, q in enumerate((QN, QT)):
                    for v in range(NKV):
                        rr = slice(v * HD, (v + 1) * HD)
                        ins = dve.tensor_copy(
                            QD[rr, k, :, v * NG * DT:(v + 1) * NG * DT].rearrange("p b (g t) -> p b g t", g=NG),
                            q[rr, :, SEQ:N].rearrange("p g (b t) -> p b g t", b=NB))
                    ins.then_inc(sem("qd_made"), 1)
                dve.tensor_tensor(gm, gate[0:NS, NT, :].unsqueeze(1).to_broadcast([NS, NP_, 24]),
                                  bc(const("pair", NS), 24), ALU.mult).then_inc(sem("gate_masked"), 1)
                dve.wait_ge(sem("s_scored"), 1)
                sc = bank[4][:, 0:NP_ * NCS].rearrange("p (a c) -> p a c", a=NP_)[:, :, 0:NC]
                pr = sp3[:, :, 0:NC]
                step(dve, dve.tensor_reduce(sm[:, 0:4], sc, AX, ALU.max, negate=True), "dve_done")
                dve.tensor_tensor(pr, sc, bc(sm[:, 0:4], NC), ALU.add).then_inc(sem("s_shifted"), 1)
                shift(0)
                dve.wait_ge(sem("gate_spread"), 1)
                step(dve, dve.tensor_tensor(gx, bank[7][:, 0:NP_ * 24].rearrange("p (a h b) -> p a h b", a=NP_, h=NH),
                                            const("head").unsqueeze(1).unsqueeze(3).to_broadcast([P, NP_, NH, 3]), ALU.mult),
                     "gate_read")
                step(dve, dve.tensor_reduce(gateR, gx.rearrange("p a h b -> p a b h"), AX, ALU.add), "dve_done")
                dve.wait_ge(sem("s_exp"), 1)
                step(dve, dve.tensor_reduce(sm[:, 4:8], pr, AX, ALU.add), "dve_done")
                step(dve, dve.reciprocal(sm[:, 8:12], sm[:, 4:8]), "dve_done")
                dve.tensor_tensor(pr, pr, bc(sm[:, 8:12], NC), ALU.mult).then_inc(sem("s_probs"), 1)
                dve.wait_ge(sem("s_probs"), 1)
                for q in range(2):
                    rr = slice(q * NS, (q + 1) * NS)
                    ins = dve.tensor_copy(sBD[rr, :, q * NCS:(q + 1) * NCS], sp3[rr])
                ins.then_inc(sem("s_apart"), 1)
                probabilities(0)
                shift(1)
                dve.wait_ge(sem("s_imp"), 1)
                step(dve, dve.tensor_reduce(imp, bank[5][:, 0:NP_ * NCS].rearrange("p (a j c) -> p a j c", a=NP_, c=4),
                                            AX, ALU.add), "imp_made")
                it, vt = imp[:, :, 1:15], val[:, :, 1:15]
                ix = const("blkidx")[:, 1:15].unsqueeze(1).to_broadcast([P, NP_, 14])
                step(dve, dve.tensor_reduce(sm[:, 12:16], it, AX, ALU.min), "dve_done")
                step(dve, dve.tensor_tensor(vt, it, bc(sm[:, 12:16], 14), ALU.is_le), "dve_done")
                step(dve, dve.tensor_tensor(vt, vt, ix, ALU.mult), "dve_done")
                step(dve, dve.tensor_reduce(sm[:, 16:20], vt, AX, ALU.max), "dve_done")
                step(dve, dve.tensor_tensor(vt, ix, bc(sm[:, 16:20], 14), ALU.is_equal), "dve_done")
                dve.tensor_scalar(DMk[:, :, 1:15], vt, NEG, None, ALU.mult)
                probabilities(1)
                add_branch(0)
                shift(2)
                dve.wait_ge(sem("s_turn_kept"), 1)
                dve.wait_ge(sem("s_valued"), 1)
                for q in range(2):
                    for v in range(NKV):
                        rr = slice(q * NS + 32 * v, q * NS + 32 * v + 32)
                        dve.tensor_tensor(oA[rr], bank[6][rr, :].rearrange("p (a c) -> p a c", a=NP_)[
                            :, :, v * HD:(v + 1) * HD], bc(gateR[rr, :, 0], HD), ALU.mult)
                probabilities(2)
                add_branch(1)
                shift(3)
                probabilities(3)
                add_branch(2)
                add_branch(3)

        cut = cutter(R1, R_ATT)
        Sb = [cut(1664) for _ in range(2)]
        cut = cutter(R1, R_HI + TT * 512)
        PT = cut(14 * P).rearrange("p (j r) -> p j r", j=14)
        NSLC = PAST + NS
        PARTS = [j * P for j in range(8)] + [NSLC + j * P for j in range(4)]

        with nc.Block() as block:
            @block.sync
            def _(sp):
                for b in range(5, NB):
                    if b >= RING:
                        sp.wait_ge(sem("b_valued"), (b - RING) // 2 + 1)
                    load_past(sp, b)
                sp.wait_ge(sem("b_valued"), 2)
                for g in range(2):
                    sp.dma_start(RAW[:, g * KC * GW:(g + 1) * KC * GW].rearrange("p (c n) -> p c n", c=KC),
                                 w_out[bass.ds(l, 1)].rearrange("o (c p) n -> p (o c) n", p=P)[:, :, g * GW:(g + 1) * GW]
                                 ).then_inc(sem(f"m_w_raw{g}"), 16)

            @block.tensor
            def _(pe):
                def turn_keys(a):
                    for n in range(6):
                        q, i = n // 3, n % 3
                        b = 2 * a + q
                        u = 6 * a + n
                        if i == 0:
                            pe.wait_ge(sem(f"past_loaded{b % RING}"), past_count(b))
                        if u >= 2:
                            pe.wait_ge(sem("k_kept"), u - 1)
                        if n == 1 and a >= 2:
                            pe.wait_ge(sem("o2_done"), a - 1)
                        for j in range(4):
                            src = pastKV[b % RING][:, 4 * i + j, 0:P] if i < 2 else winKV[b % RING][:, j, 0:P]
                            ins = pe.transpose(bank[1 - u % 2][:, j * P:(j + 1) * P], src, ident)
                        ins.then_inc(sem("k_turned"), 1)

                def scores(a):
                    pe.wait_ge(sem("k_kept"), 6 * a + 6)
                    for i in range(3):
                        if a >= 1 and i != 1:
                            pe.wait_ge(sem("b_read"), 2 * a - 1 if i == 0 else 2 * a)
                        for q in range(2):
                            pe.matmul(bank[2 + i][q * NS:(q + 1) * NS, :], QD[:, 1, 2 * a + q, :],
                                      kTb[q][:, i * 512:(i + 1) * 512], start=True, stop=True)
                    for q in range(2):
                        for i in range(2):
                            ins = pe.matmul(bank[5][q * NS:(q + 1) * NS, i * NS:(i + 1) * NS], QD[:, 1, 2 * a + q, :],
                                            KT[:, i, SEQ:N], start=True, stop=True)
                    ins.then_inc(sem("b_scored"), 1)

                def turn_probs(a):
                    s = Sb[a % 2]
                    for i in range(4):
                        u = 4 * a + i
                        pe.wait_ge(sem("b_probs"), 2 * a + (1 if i < 2 else 2))
                        pe.wait_ge(sem("o_turn_kept"), NT)
                        if u >= 2:
                            pe.wait_ge(sem("pT_kept"), u - 1)
                        if i < 3:
                            for j in range(4):
                                o = PARTS[4 * i + j]
                                ins = pe.transpose(bank[6 + i % 2][:, j * P:(j + 1) * P], s[:, o:o + P], ident)
                        else:
                            for j, o in enumerate((PAST, NSLC + WINB)):
                                ins = pe.transpose(bank[7][0:NS, j * P:(j + 1) * P], s[:, o:o + NS], ident)
                        ins.then_inc(sem("p_turned"), 1)

                def values(a):
                    if a >= 1:
                        pe.wait_ge(sem("o2_done"), a)
                    pe.wait_ge(sem("pT_kept"), 4 * a + 4)
                    for q in range(2):
                        rr = slice(q * NS, (q + 1) * NS)
                        b = (2 * a + q) % RING
                        for i, (js, V, new) in enumerate(((range(8), pastKV[b], 12), (range(8, 12), winKV[b], 13))):
                            o = bank[0][rr, i * P:(i + 1) * P]
                            for j in js:
                                pe.matmul(o, PT[:, j, rr], V[:, j - js[0], P:256], start=(j == js[0]), stop=False)
                            ins = pe.matmul(o, PT[0:NS, new, rr], vtok[i][0:NS, NT, :], start=False, stop=True)
                    ins.then_inc(sem("b_valued"), 1)

                turn_keys(0)
                for t in range(NT):
                    if t >= 2:
                        pe.wait_ge(sem("o_turn_kept"), t - 1)
                    for c in range(4):
                        ins = pe.transpose(bank[6 + t % 2][:, c * P:(c + 1) * P], o_tok[:, t, c * P:(c + 1) * P], ident)
                    ins.then_inc(sem("o_turned"), 1)
                scores(0)
                for a in range(NP_):
                    if a + 1 < NP_:
                        turn_keys(a + 1)
                        scores(a + 1)
                    turn_probs(a)
                    values(a)
                pe.wait_ge(sem("o_ready"), NP_)
                for a in range(NP_):
                    ins = pe.transpose(bank[0][0:HD, a * P:(a + 1) * P], oA[:, a, :], ident)
                ins.then_inc(sem("s_o_turned"), 1)

            @block.scalar
            def _(act):
                def keep_keys(a):
                    for n in range(6):
                        u = 6 * a + n
                        act.wait_ge(sem("k_turned"), u + 1)
                        if a >= 1:
                            act.wait_ge(sem("b_scored"), a)
                        act.activation(kTb[n // 3][:, n % 3 * 512:(n % 3 + 1) * 512], bank[1 - u % 2][:, :], ACT.Copy
                                       ).then_inc(sem("k_kept"), 1)

                keep_keys(0)
                for t in range(NT):
                    act.wait_ge(sem("o_turned"), t + 1)
                    act.activation(OT[:, 0:4, t * P:(t + 1) * P], bank[6 + t % 2][:, :].rearrange("p (c n) -> p c n", c=4),
                                   ACT.Copy).then_inc(sem("o_turn_kept"), 1)
                for a in range(NP_):
                    if a + 1 < NP_:
                        keep_keys(a + 1)
                    for i, (lo, hi) in enumerate(((0, NSLC), (NSLC, 1664))):
                        act.wait_ge(sem("b_maxed"), 2 * a + i + 1)
                        act.activation(Sb[a % 2][:, lo:hi], Sb[a % 2][:, lo:hi], ACT.Exp, bias=srs[:, 2 * a + i:2 * a + i + 1],
                                       accum_out=srs[:, 8 + 2 * a + i:9 + 2 * a + i]).then_inc(sem("b_probs"), 1)
                    if a >= 1:
                        act.wait_ge(sem("b_valued"), a)
                    for i in range(4):
                        act.wait_ge(sem("p_turned"), 4 * a + i + 1)
                        src = bank[6 + i % 2][:, :].rearrange("p (j r) -> p j r", j=4)
                        src, dst = (src, PT[:, 4 * i:4 * i + 4]) if i < 3 else (src[0:NS, 0:2], PT[0:NS, 12:14])
                        act.activation(dst, src, ACT.Copy).then_inc(sem("pT_kept"), 1)

            @block.vector
            def _(dve):
                def masked(a):
                    s = Sb[a % 2]
                    new = const("newneg")[:, a * NS:(a + 1) * NS]
                    dve.wait_ge(sem("b_scored"), a + 1)
                    if a >= 2:
                        dve.wait_ge(sem("p_turned"), 4 * (a - 1))
                    for i in range(2):
                        dve.tensor_tensor(s[:, i * 512:(i + 1) * 512].rearrange("p (j c) -> p j c", c=64),
                                          bank[2 + i][:, :].rearrange("p (j c) -> p j c", c=64),
                                          bc(DMk[:, a, 8 * i:8 * i + 8], 64), ALU.add)
                    dve.tensor_tensor(s[:, PAST:NSLC], bank[5][:, 0:NS], new, ALU.add).then_inc(sem("b_read"), 1)
                    dve.wait_ge(sem("b_read"), 2 * a + 1)
                    dve.tensor_reduce(srs[:, 2 * a:2 * a + 1], s[:, 0:NSLC], AX, ALU.max, negate=True
                                      ).then_inc(sem("b_maxed"), 1)
                    dve.tensor_tensor(s[:, NSLC:NSLC + DT], bank[4][:, 0:DT], const("winneg"), ALU.add)
                    dve.tensor_copy(s[:, NSLC + DT:NSLC + WINB], bank[4][:, DT:WINB])
                    dve.tensor_tensor(s[:, NSLC + WINB:1664], bank[5][:, NS:2 * NS], new, ALU.add).then_inc(sem("b_read"), 1)
                    dve.wait_ge(sem("b_read"), 2 * a + 2)
                    dve.tensor_reduce(srs[:, 2 * a + 1:2 * a + 2], s[:, NSLC:1664], AX, ALU.max, negate=True
                                      ).then_inc(sem("b_maxed"), 1)

                def finish(a):
                    dve.wait_ge(sem("b_probs"), 2 * a + 2)
                    c = srs[:, 16 + 2 * a:18 + 2 * a]
                    step(dve, dve.reciprocal(c, srs[:, 8 + 2 * a:10 + 2 * a]), "dve_done")
                    step(dve, dve.tensor_tensor(c, c, gateR[:, a, 1:3], ALU.mult), "dve_done")
                    dve.wait_ge(sem("b_valued"), a + 1)
                    for q in range(2):
                        for v in range(NKV):
                            rr = slice(q * NS + 32 * v, q * NS + 32 * v + 32)
                            ins = dve.tensor_tensor(o2[rr, a], bank[0][rr, 0:2 * P].rearrange("p (i c) -> p i c", i=2)[
                                :, :, v * HD:(v + 1) * HD], bc(c[rr], HD), ALU.mult)
                    ins.then_inc(sem("o2_done"), 1)
                    dve.wait_ge(sem("o2_done"), a + 1)
                    step(dve, dve.tensor_tensor(oA[:, a, :], oA[:, a, :], o2[:, a, 0, :], ALU.add), "dve_done")
                    dve.tensor_tensor(oA[:, a, :], oA[:, a, :], o2[:, a, 1, :], ALU.add).then_inc(sem("o_ready"), 1)

                for a in range(NP_ + 1):
                    if a < NP_:
                        masked(a)
                    if a >= 1:
                        finish(a - 1)
                dve.wait_ge(sem("s_o_turned"), 1)
                for p in range(2):
                    dve.tensor_copy(OT[p * HD:(p + 1) * HD, 0:4, SEQ:N].rearrange("p h (n t) -> p h n t", n=NB),
                                    bank[0][0:HD, :].rearrange("p (n h s t) -> p s h n t", n=NB, h=NH // 2, s=2)[:, p])

        mix_scope.close()

        mlp_scope = ExitStack()
        S7 = Split(mlp_scope, "m_")
        UH, UL = (mlp_scope.enter_context(nc.sbuf_tensor(n, [P, KC * N], F32R))[:, :].rearrange("p (c n) -> p c n", c=KC)
                  for n in ("UH", "UL"))
        sq2_ = mlp_scope.enter_context(nc.sbuf_tensor("sq2", [P, 4 * N], F32))
        sq2 = [sq2_[:, i * N:(i + 1) * N] for i in range(2)]
        relu = [sq2_[:, 2 * N + i * HALF:2 * N + (i + 1) * HALF] for i in range(4)]
        G7 = [("out", 0, g) for g in range(4)]
        for q in range(4):
            G7 += [(kind, q, g) for kind in ("up", "down") for g in range(4)]
        U7 = [(kind, q, 2 * g + m, s, i) for i, (kind, q, g) in enumerate(G7) for m in range(2) for s in range(2)]
        NOUT = 16
        FQ = DFF // 4
        RANK = [sum(U7[x][0] == U7[u][0] or (U7[u][0] != "up" and U7[x][0] != "up") for x in range(u + 1))
                for u in range(len(U7))]

        with nc.Block() as block:
            @block.sync
            def _(sp):
                for i, (kind, q, g) in enumerate(G7):
                    cols = slice(g * GW, (g + 1) * GW)
                    if kind == "out":
                        src = w_out[bass.ds(l, 1)].rearrange("o (c p) n -> p (o c) n", p=P)[:, :, cols]
                    elif kind == "up":
                        src = w_up[bass.ds(l, 1)].rearrange("o (c p) n -> p (o c) n", p=P)[
                            :, :, q * FQ + g * GW:q * FQ + (g + 1) * GW]
                    else:
                        src = w_down[bass.ds(l, 1)].rearrange("o (c p) n -> p (o c) n", p=P)[:, KC * q:KC * (q + 1), cols]
                    if i >= 2:
                        load_granule(sp, S7, i, src)

            @block.gpsimd
            def _(pool):
                for i in range(len(G7)):
                    split_lo(pool, S7, i, GW)

            @block.tensor
            def _(pe):
                pe.wait_ge(sem("m_w_lo"), 1)
                first_products(pe, bank[2:6], S7, 0, GW, "mix_lo", lambda c: c + 1)
                for u, (kind, q, m, s, i) in enumerate(U7):
                    if u < 4:
                        continue
                    if u == NOUT:
                        norm_products(pe, "n2")
                        pe.wait_ge(sem("m_w_lo"), i + 1)
                        pe.wait_ge(sem("m_added"), RANK[NOUT - 1])
                        first_products(pe, [bank[2 + x % 6] for x in range(NOUT, NOUT + 4)], S7, i, GW, "n2_out",
                                       lambda c: c + 1)
                    if NOUT <= u < NOUT + 4:
                        continue
                    first = kind == "down" and m == 0 and s == 0
                    pe.wait_ge(sem("m_w_lo"), i + 1)
                    if u >= 6:
                        pe.wait_ge(sem("m_relued" if U7[u - 6][0] == "up" else "m_added"), RANK[u - 6])
                    ah, al = (UH, UL) if kind == "down" else (S7.ah, S7.al)
                    feature_product(pe, bank[2 + u % 6][:, 0:HALF], S7, i, GW, slice(m % 2 * P, (m % 2 + 1) * P), ah, al,
                                    halves(s), ("relu_lo", 16 * q + 2) if first else None).then_inc(sem("m_done"), 1)

            def relu_hi(act, n):
                act.wait_ge(sem("relu_squared"), n + 1)
                q = n // 16
                if q >= 1 and n % 16 == 0:
                    act.wait_ge(sem("m_done"), NOUT + 32 * q)
                act.activation(UH[:, n % 16 // 2, halves(n % 2)], relu[n % 4], ACT.Copy).then_inc(sem("relu_hi"), 1)

            @block.scalar
            def _(act):
                split_hi(act, S7, 0, GW, 0)
                for c in range(KC):
                    act.activation(S7.ah[:, c, :], OT[:, c, :], ACT.Copy).then_inc(sem("mix_hi"), 1)
                split_hi(act, S7, 1, GW, 0)
                for u, (kind, q, m, s, i) in enumerate(U7):
                    if (kind == "out" and s == 1 and m >= 1) or u == NOUT:
                        c = m - 1 if kind == "out" else KC - 1
                        act.wait_ge(sem("m_added"), 2 * c + 2)
                        square(act, "n2", sq2, c)
                    if u == NOUT:
                        norm_scalar(act, "n2", sq2, S7)
                    if kind == "up":
                        act.wait_ge(sem("m_done"), u + 1)
                        n = RANK[u] - 1
                        if n >= 4:
                            act.wait_ge(sem("relu_lo"), n - 3)
                        act.activation(relu[n % 4], bank[2 + u % 6][:, 0:HALF], ACT.Relu).then_inc(sem("m_relued"), 1)
                        if n % 16 >= 1:
                            relu_hi(act, n - 1)
                        if n % 16 == 15:
                            relu_hi(act, n)
                    if u % 4 == 3 and i + 2 < len(G7):
                        split_hi(act, S7, i + 2, GW, u + 1)

            @block.vector
            def _(dve):
                for c in range(KC):
                    dve.wait_ge(sem("mix_hi"), c + 1)
                    dve.tensor_tensor(S7.al[:, c, :], OT[:, c, :], S7.ah[:, c, :].bitcast(F32), ALU.subtract
                                      ).then_inc(sem("mix_lo"), 1)

                def relu_lo(n):
                    dve.wait_ge(sem("relu_hi"), n + 1)
                    x = (slice(None), n % 16 // 2, halves(n % 2))
                    dve.tensor_tensor(UL[x], relu[n % 4], UH[x].bitcast(F32), ALU.subtract).then_inc(sem("relu_lo"), 1)

                for u, (kind, q, m, s, i) in enumerate(U7):
                    if u == NOUT:
                        add_square(dve, "n2", sq2, KC - 1)
                        norm_vector(dve, "n2", sq2, S7, G_MLP)
                    if kind == "up":
                        n = RANK[u] - 1
                        dve.wait_ge(sem("m_relued"), n + 1)
                        dve.tensor_tensor(relu[n % 4], relu[n % 4], relu[n % 4], ALU.mult).then_inc(sem("relu_squared"), 1)
                        if n % 16 >= 1:
                            relu_lo(n - 1)
                        if n % 16 == 15:
                            relu_lo(n)
                    else:
                        dve.wait_ge(sem("m_done"), u + 1)
                        if kind == "down" and q >= 1:
                            dve.wait_ge(sem("m_added"), RANK[u] - 16)
                        x = XT[:, m, halves(s)]
                        dve.tensor_tensor(x, x, bank[2 + u % 6][:, 0:HALF], ALU.add).then_inc(sem("m_added"), 1)
                        if kind == "out" and s == 1 and m >= 2:
                            add_square(dve, "n2", sq2, m - 1)

        mlp_scope.close()
        clear_semaphores()
        layers.close()

        YU = [(t, q) for t in range(TT) for q in range(2)]
        xout = [ctx.enter_context(nc.sbuf_tensor(f"xout{i}", [P, SLOT], F32)) for i in range(2)]
        Y = [xout[0][:, :].rearrange("p (t c) -> p t c", t=NT), xout[1][:, 0:DM].rearrange("p (t c) -> p t c", t=1)]
        with nc.Block() as block:
            @block.tensor
            def _(pe):
                for u, (t, q) in enumerate(YU):
                    r = rows_of(t)
                    if u >= 8:
                        pe.wait_ge(sem("y_kept"), u - 7)
                    for c in range(4):
                        ins = pe.transpose(bank[u % 8][0:r, c * P:(c + 1) * P], XT[:, 4 * q + c, t * P:t * P + r], ident)
                    ins.then_inc(sem("y_turned"), 1)

            @block.vector
            def _(dve):
                for u, (t, q) in enumerate(YU):
                    r = rows_of(t)
                    dve.wait_ge(sem("y_turned"), u + 1)
                    dst = (Y[0][:, t] if t < NT else Y[1][0:NS, 0])[:, q * 512:(q + 1) * 512]
                    dve.tensor_copy(dst, bank[u % 8][0:r, :]).then_inc(sem("y_kept"), 1)

            @block.sync
            def _(sp):
                for t in range(NT):
                    sp.wait_ge(sem("y_kept"), 2 * t + 2)
                    sp.dma_start(y_prompt[0, t * P:(t + 1) * P, :], Y[0][:, t]).then_inc(sem("y_stored"), 16)
                sp.wait_ge(sem("y_kept"), 2 * TT)
                sp.dma_start(y_sample.rearrange("b t c -> (b t) c"), Y[1][0:NS, 0]).then_inc(sem("y_stored"), 16)
                sp.wait_ge(sem("y_stored"), 16 * TT)


_INS = ['x_prompt', 'x_sample', 'cache_nsa_kv', 'cache_win_kv', 'state_hgrn', 'page_table', 'attn_norm_g', 'w_in',
        'q_norm_g', 'k_norm_g', 'cmp_pos', 'cmp_w1', 'cmp_b1', 'cmp_w2', 'hg_lb_param', 'hg_norm_g', 'w_out',
        'mlp_norm_g', 'w_up', 'w_down']
_OUTS = [(1, SEQ, DM), (NB, DT, DM), (DEPTH, 1, SEQ, 4, NKV, HD), (DEPTH, 1, SEQ, 2, NKV, HD),
         (DEPTH, 1, HH, P, P), (DEPTH, NB, DT, 4, NKV, HD), (DEPTH, NB, DT, 2, NKV, HD), (DEPTH, NB, HH, P, P)]


def kernel(**inputs):
    import concourse.bacc as bacc
    from concourse.bass_utils import run_bass_kernel_spmd

    nc = bacc.Bacc("TRN2", target_bir_lowering=False, num_devices=1)
    arrays, args = {}, []
    for name in _INS + ['constants']:
        a = CONSTANTS if name == 'constants' else np.ascontiguousarray(inputs[name])
        arrays[f"in_{name}"] = a
        args.append(nc.dram_tensor(f"in_{name}", a.shape, mybir.dt.from_np(a.dtype), kind="ExternalInput").ap())
    for i, shape in enumerate(_OUTS):
        args.append(nc.dram_tensor(f"out_{i}", shape, F32, kind="ExternalOutput").ap())
    build(nc, *args)
    r = run_bass_kernel_spmd(nc, [arrays], core_ids=[0])
    return tuple(r.results[0][f"out_{i}"] for i in range(len(_OUTS)))
```
